# Optimizing a Trainium2 kernel written in Bass

```python
import math
import jax, jax.numpy as jnp
from jax import lax
import numpy as np

D_MODEL = 1024
BATCH = 1
SEQ = 512
DEPTH = 1
DEC_BATCH = 8
DEC_SEQ = 1
PAST_LEN = 4096
PAGE_SIZE = 128

DN_HEADS = 8
DN_DK = 128
DN_DV = 128
DN_CONV = 4
DN_CHUNK = 64
RET_HEADS = 4
RET_DK = 256
RET_DV = 512
RET_CHUNK = 128
ROPE_BASE = 10000.0
N_EXPERTS = 64
TOP_K = 8
N_GROUPS = 8
TOPK_GROUPS = 4
D_EXPERT = 256
D_SHARED = 256
ROUTED_SCALE = 2.5
MOE_BLOCK = 128
MOD_CHUNKS = 6
EPS = 1e-6

DN_QK = DN_HEADS * DN_DK
DN_VW = DN_HEADS * DN_DV
DN_CONV_W = 2 * DN_QK + DN_VW
RET_QK = RET_HEADS * RET_DK
RET_VW = RET_HEADS * RET_DV
IN_SPLITS = (DN_CONV_W, DN_HEADS, DN_HEADS, DN_VW, RET_QK, RET_QK, RET_VW, RET_VW, D_MODEL, D_MODEL)
D_IN_PROJ = sum(IN_SPLITS)

kernel_name = "hybrid_deltanet_retention_moe_adaln_step"

def _rms_norm(x, w):
    xf = x.astype(jnp.float32)
    y = xf * lax.rsqrt(jnp.mean(xf * xf, axis=-1, keepdims=True) + EPS)
    return (y * w.astype(jnp.float32)).astype(x.dtype)

def _l2norm(x):
    xf = x.astype(jnp.float32)
    return xf * lax.rsqrt(jnp.sum(xf * xf, axis=-1, keepdims=True) + EPS)

def _heads(t, n_heads):
    b, l, w = t.shape
    return t.reshape(b, l, n_heads, w // n_heads).transpose(0, 2, 1, 3)

def _to_chunks(t, c):
    b, h, l = t.shape[:3]
    t = t.reshape(b, h, l // c, c, *t.shape[3:])
    return jnp.moveaxis(t, 2, 0)

def _causal_conv(u, buf, w):
    l = u.shape[1]
    ext = jnp.concatenate([buf.astype(u.dtype), u], axis=1)
    out = ext[:, 0:l] * w[0]
    for i in range(1, DN_CONV):
        out = out + ext[:, i:i + l] * w[i]
    return jax.nn.silu(out), ext[:, l:]

def _rotary(x, pos):
    half = x.shape[-1] // 2
    inv = ROPE_BASE ** (-jnp.arange(half, dtype=jnp.float32) / half)
    ang = pos.astype(jnp.float32)[:, None] * inv[None, :]
    cos, sin = jnp.cos(ang), jnp.sin(ang)
    xf = x.astype(jnp.float32)
    x1, x2 = xf[..., :half], xf[..., half:]
    return jnp.concatenate([x1 * cos - x2 * sin, x1 * sin + x2 * cos], axis=-1)

def _gated_delta_rule(q, k, v, g, beta, s0):
    b, h, l, dk = q.shape
    dv = v.shape[-1]
    c = DN_CHUNK if l % DN_CHUNK == 0 else l
    q, k, v, g, beta = (_to_chunks(t.astype(jnp.float32), c) for t in (q, k, v, g, beta))
    gc = jnp.cumsum(g, axis=-1)
    idx = jnp.arange(c)
    causal = idx[:, None] >= idx[None, :]
    strict = idx[:, None] > idx[None, :]
    diff = gc[..., :, None] - gc[..., None, :]
    decay = jnp.where(causal, jnp.exp(jnp.where(causal, diff, 0.0)), 0.0)
    kb = k * beta[..., None]
    a_mat = jnp.where(strict, jnp.einsum('nbhik,nbhjk->nbhij', kb, k) * decay, 0.0)
    lhs = a_mat + jnp.eye(c, dtype=jnp.float32)
    rhs = jnp.concatenate([v * beta[..., None], kb * jnp.exp(gc)[..., None]], axis=-1)
    sol = lax.linalg.triangular_solve(lhs, rhs, left_side=True, lower=True, transpose_a=False, unit_diagonal=True)
    u, w = sol[..., :dv], sol[..., dv:]
    qk = jnp.where(causal, jnp.einsum('nbhik,nbhjk->nbhij', q, k) * decay, 0.0)
    q_dec = q * jnp.exp(gc)[..., None]
    g_last = gc[..., -1]
    k_end = k * jnp.exp(g_last[..., None] - gc)[..., None]

    def step(s, xs):
        q_n, w_n, u_n, qk_n, k_n, gl_n = xs
        v_new = u_n - jnp.einsum('bhck,bhkv->bhcv', w_n, s)
        o = jnp.einsum('bhck,bhkv->bhcv', q_n, s) + jnp.einsum('bhij,bhjv->bhiv', qk_n, v_new)
        s = s * jnp.exp(gl_n)[..., None, None] + jnp.einsum('bhck,bhcv->bhkv', k_n, v_new)
        return s, o

    s_fin, o = lax.scan(step, s0.astype(jnp.float32), (q_dec, w, u, qk, k_end, g_last))
    o = jnp.moveaxis(o, 0, 2).reshape(b, h, l, dv)
    return o, s_fin

def _retention(q, k, v, s0):
    b, h, l, dk = q.shape
    dv = v.shape[-1]
    c = RET_CHUNK if l % RET_CHUNK == 0 else l
    log_gamma = jnp.log(1.0 - 2.0 ** (-5.0 - jnp.arange(h, dtype=jnp.float32)))
    q, k, v = (_to_chunks(t.astype(jnp.float32), c) for t in (q, k, v))
    idx = jnp.arange(c, dtype=jnp.float32)
    rel = idx[:, None] - idx[None, :]
    d_mat = jnp.where(rel >= 0, jnp.exp(jnp.maximum(rel, 0.0) * log_gamma[:, None, None]), 0.0)
    intra = jnp.einsum('nbhij,nbhjv->nbhiv', jnp.einsum('nbhik,nbhjk->nbhij', q, k) * d_mat, v)
    q_dec = q * jnp.exp((idx[None, :] + 1.0) * log_gamma[:, None])[:, :, None]
    k_dec = k * jnp.exp((c - 1.0 - idx[None, :]) * log_gamma[:, None])[:, :, None]
    chunk_decay = jnp.exp(c * log_gamma)[:, None, None]

    def step(s, xs):
        q_n, k_n, v_n = xs
        o = jnp.einsum('bhck,bhkv->bhcv', q_n, s)
        s = s * chunk_decay + jnp.einsum('bhck,bhcv->bhkv', k_n, v_n)
        return s, o

    s_fin, cross = lax.scan(step, s0.astype(jnp.float32), (q_dec, k_dec, v))
    o = jnp.moveaxis(intra + cross, 0, 2).reshape(b, h, l, dv)
    return o, s_fin

def _token_mixers(h, pos, conv_buf, s_delta, s_ret, w_in, conv_w, a_log, dt_bias, dn_norm_w,
                  ret_gn_w, ret_gn_b, w_down_a, w_down_b, w_out):
    b, l, _ = h.shape
    points = np.cumsum(IN_SPLITS)[:-1].tolist()
    qkv_a, b_a, a_a, z_a, q_b, k_b, v_b, g_b, gate_a, gate_b = jnp.split(h @ w_in, points, axis=-1)
    qkv_a, conv_new = _causal_conv(qkv_a, conv_buf, conv_w)
    q_a, k_a, v_a = jnp.split(qkv_a, [DN_QK, 2 * DN_QK], axis=-1)
    q_a = _l2norm(_heads(q_a, DN_HEADS)) * (DN_DK ** -0.5)
    k_a = _l2norm(_heads(k_a, DN_HEADS))
    v_a = _heads(v_a, DN_HEADS)
    beta = jax.nn.sigmoid(b_a.astype(jnp.float32)).transpose(0, 2, 1)
    g = (-jnp.exp(a_log.astype(jnp.float32))
         * jax.nn.softplus(a_a.astype(jnp.float32) + dt_bias.astype(jnp.float32))).transpose(0, 2, 1)
    o_a, s_delta_new = _gated_delta_rule(q_a, k_a, v_a, g, beta, s_delta)
    o_a = o_a.transpose(0, 2, 1, 3).astype(h.dtype)
    z = z_a.reshape(b, l, DN_HEADS, DN_DV)
    o_a = (_rms_norm(o_a, dn_norm_w) * jax.nn.silu(z)).reshape(b, l, DN_VW)
    y_a = o_a @ w_down_a
    q_b = _rotary(_heads(q_b, RET_HEADS), pos)
    k_b = _rotary(_heads(k_b, RET_HEADS), pos) * (RET_DK ** -0.5)
    v_b = _heads(v_b, RET_HEADS)
    o_b, s_ret_new = _retention(q_b, k_b, v_b, s_ret)
    o_b = o_b.transpose(0, 2, 1, 3)
    mu = jnp.mean(o_b, axis=-1, keepdims=True)
    var = jnp.mean(jnp.square(o_b - mu), axis=-1, keepdims=True)
    o_b = (((o_b - mu) * lax.rsqrt(var + EPS)).reshape(b, l, RET_VW) * ret_gn_w.astype(jnp.float32)
           + ret_gn_b.astype(jnp.float32))
    o_b = o_b.astype(h.dtype) * jax.nn.silu(g_b)
    y_b = o_b @ w_down_b
    merged = jax.nn.sigmoid(gate_a) * y_a + jax.nn.sigmoid(gate_b) * y_b
    return (merged @ w_out, conv_new, s_delta_new.astype(s_delta.dtype), s_ret_new.astype(s_ret.dtype))

def _moe(h, router_w, router_bias, w_gate, w_up, w_down, ws_gate, ws_up, ws_down):
    b, l, d = h.shape
    x = h.reshape(b * l, d)
    t = x.shape[0]
    scores = jax.nn.sigmoid(x.astype(jnp.float32) @ router_w.astype(jnp.float32).T)
    biased = scores + router_bias.astype(jnp.float32)
    grp_score = lax.top_k(biased.reshape(t, N_GROUPS, N_EXPERTS // N_GROUPS), 2)[0].sum(-1)
    _, top_g = lax.top_k(grp_score, TOPK_GROUPS)
    gmask = jnp.any(top_g[:, :, None] == jnp.arange(N_GROUPS)[None, None, :], axis=1)
    emask = jnp.repeat(gmask, N_EXPERTS // N_GROUPS, axis=-1)
    _, top_e = lax.top_k(jnp.where(emask, biased, -jnp.inf), TOP_K)
    wts = jnp.take_along_axis(scores, top_e, axis=-1)
    wts = wts / jnp.sum(wts, axis=-1, keepdims=True) * ROUTED_SCALE
    n = t * TOP_K
    flat_e = top_e.reshape(n)
    flat_t = jnp.arange(n, dtype=jnp.int32) // TOP_K
    flat_w = wts.reshape(n)
    order = jnp.argsort(flat_e)
    se, st, sw = flat_e[order], flat_t[order], flat_w[order]
    counts = jnp.bincount(flat_e, length=N_EXPERTS)
    padded = ((counts + MOE_BLOCK - 1) // MOE_BLOCK) * MOE_BLOCK
    pad_end = jnp.cumsum(padded)
    pad_start = pad_end - padded
    start = jnp.cumsum(counts) - counts
    dest = pad_start[se] + (jnp.arange(n) - start[se])
    n_blocks = -(-n // MOE_BLOCK) + N_EXPERTS
    p = n_blocks * MOE_BLOCK
    row_tok = jnp.full((p,), t, dtype=jnp.int32).at[dest].set(st)
    row_w = jnp.zeros((p,), jnp.float32).at[dest].set(sw)
    block_e = jnp.minimum(jnp.searchsorted(pad_end, jnp.arange(n_blocks) * MOE_BLOCK, side='right'),
                          N_EXPERTS - 1)
    x_pad = jnp.concatenate([x, jnp.zeros((1, d), x.dtype)], axis=0)
    xb = x_pad[row_tok].reshape(n_blocks, MOE_BLOCK, d)

    def expert_block(args):
        xi, e = args
        hid = jax.nn.silu(xi @ w_gate[e]) * (xi @ w_up[e])
        return hid @ w_down[e]

    yb = lax.map(expert_block, (xb, block_e)).reshape(p, d)
    routed = jax.ops.segment_sum(yb * row_w[:, None].astype(yb.dtype), row_tok, num_segments=t + 1)[:t]
    shared = (jax.nn.silu(x @ ws_gate) * (x @ ws_up)) @ ws_down
    return (routed + shared).reshape(b, l, d)

def _trunk(x, c, pos, conv_bufs, s_deltas, s_rets, params):
    (w_mod, b_mod, norm_mix_w, w_in, conv_w, a_log, dt_bias, dn_norm_w, ret_gn_w, ret_gn_b,
     w_down_a, w_down_b, w_out, norm_ffn_w, router_w, router_bias, w_gate, w_up, w_down,
     ws_gate, ws_up, ws_down, final_norm_w) = params
    new_conv, new_delta, new_ret = [], [], []
    for layer in range(DEPTH):
        mod = jax.nn.silu(c) @ w_mod[layer] + b_mod[layer]
        sh1, sc1, g1, sh2, sc2, g2 = jnp.split(mod[:, None, :], MOD_CHUNKS, axis=-1)
        hmix = _rms_norm(x, norm_mix_w[layer]) * (1.0 + sc1) + sh1
        mix, cb, sd, sr = _token_mixers(hmix, pos, conv_bufs[layer], s_deltas[layer], s_rets[layer],
                                        w_in[layer], conv_w[layer], a_log[layer], dt_bias[layer],
                                        dn_norm_w[layer], ret_gn_w[layer], ret_gn_b[layer],
                                        w_down_a[layer], w_down_b[layer], w_out[layer])
        x = x + g1 * mix
        hffn = _rms_norm(x, norm_ffn_w[layer]) * (1.0 + sc2) + sh2
        x = x + g2 * _moe(hffn, router_w[layer], router_bias[layer], w_gate[layer], w_up[layer],
                          w_down[layer], ws_gate[layer], ws_up[layer], ws_down[layer])
        new_conv.append(cb)
        new_delta.append(sd)
        new_ret.append(sr)
    return (_rms_norm(x, final_norm_w), jnp.stack(new_conv), jnp.stack(new_delta), jnp.stack(new_ret))

def setup_inputs(seed: int = 0) -> dict:
    key = jax.random.key(seed)
    ks = jax.random.split(key, 32)
    f32 = jnp.float32

    def nrm(k, shape, scale):
        return jax.random.normal(k, shape, f32) * scale

    dt = jnp.exp(jax.random.uniform(ks[12], (DEPTH, DN_HEADS), f32, math.log(1e-3), math.log(1e-1)))
    return {
        "x_prompt": nrm(ks[0], (BATCH, SEQ, D_MODEL), 1.0),
        "x_sample": nrm(ks[1], (DEC_BATCH, DEC_SEQ, D_MODEL), 1.0),
        "state_conv": nrm(ks[2], (DEPTH, DEC_BATCH, DN_CONV - 1, DN_CONV_W), 1.0),
        "state_delta": nrm(ks[3], (DEPTH, DEC_BATCH, DN_HEADS, DN_DK, DN_DV), 0.1),
        "state_ret": nrm(ks[4], (DEPTH, DEC_BATCH, RET_HEADS, RET_DK, RET_DV), 0.1),
        "c_prompt": nrm(ks[5], (BATCH, D_MODEL), 1.0),
        "c_sample": nrm(ks[6], (DEC_BATCH, D_MODEL), 1.0),
        "w_mod": nrm(ks[7], (DEPTH, D_MODEL, MOD_CHUNKS * D_MODEL), 0.2 * D_MODEL ** -0.5),
        "b_mod": nrm(ks[8], (DEPTH, MOD_CHUNKS * D_MODEL), 0.02),
        "norm_mix_w": 1.0 + nrm(ks[9], (DEPTH, D_MODEL), 0.02),
        "w_in": nrm(ks[10], (DEPTH, D_MODEL, D_IN_PROJ), D_MODEL ** -0.5),
        "conv_w": nrm(ks[11], (DEPTH, DN_CONV, DN_CONV_W), DN_CONV ** -0.5),
        "a_log": jnp.log(jax.random.uniform(ks[13], (DEPTH, DN_HEADS), f32, 1.0, 16.0)),
        "dt_bias": dt + jnp.log(-jnp.expm1(-dt)),
        "dn_norm_w": 1.0 + nrm(ks[14], (DEPTH, DN_DV), 0.02),
        "ret_gn_w": 1.0 + nrm(ks[15], (DEPTH, RET_VW), 0.02),
        "ret_gn_b": nrm(ks[16], (DEPTH, RET_VW), 0.02),
        "w_down_a": nrm(ks[17], (DEPTH, DN_VW, D_MODEL), DN_VW ** -0.5),
        "w_down_b": nrm(ks[18], (DEPTH, RET_VW, D_MODEL), RET_VW ** -0.5),
        "w_out": nrm(ks[19], (DEPTH, D_MODEL, D_MODEL), D_MODEL ** -0.5),
        "norm_ffn_w": 1.0 + nrm(ks[20], (DEPTH, D_MODEL), 0.02),
        "router_w": nrm(ks[21], (DEPTH, N_EXPERTS, D_MODEL), D_MODEL ** -0.5),
        "router_bias": nrm(ks[22], (DEPTH, N_EXPERTS), 0.01),
        "w_gate": nrm(ks[23], (DEPTH, N_EXPERTS, D_MODEL, D_EXPERT), D_MODEL ** -0.5),
        "w_up": nrm(ks[24], (DEPTH, N_EXPERTS, D_MODEL, D_EXPERT), D_MODEL ** -0.5),
        "w_down": nrm(ks[25], (DEPTH, N_EXPERTS, D_EXPERT, D_MODEL), D_EXPERT ** -0.5),
        "ws_gate": nrm(ks[26], (DEPTH, D_MODEL, D_SHARED), D_MODEL ** -0.5),
        "ws_up": nrm(ks[27], (DEPTH, D_MODEL, D_SHARED), D_MODEL ** -0.5),
        "ws_down": nrm(ks[28], (DEPTH, D_SHARED, D_MODEL), D_SHARED ** -0.5),
        "final_norm_w": 1.0 + nrm(ks[29], (D_MODEL,), 0.02),
    }

def reference(x_prompt, x_sample, state_conv, state_delta, state_ret, c_prompt, c_sample,
              w_mod, b_mod, norm_mix_w, w_in, conv_w, a_log, dt_bias, dn_norm_w, ret_gn_w, ret_gn_b,
              w_down_a, w_down_b, w_out, norm_ffn_w, router_w, router_bias, w_gate, w_up, w_down,
              ws_gate, ws_up, ws_down, final_norm_w):
    params = (w_mod, b_mod, norm_mix_w, w_in, conv_w, a_log, dt_bias, dn_norm_w, ret_gn_w, ret_gn_b,
              w_down_a, w_down_b, w_out, norm_ffn_w, router_w, router_bias, w_gate, w_up, w_down,
              ws_gate, ws_up, ws_down, final_norm_w)
    bp, lp = x_prompt.shape[0], x_prompt.shape[1]
    zero_conv = jnp.zeros((DEPTH, bp, DN_CONV - 1, DN_CONV_W), x_prompt.dtype)
    zero_delta = jnp.zeros((DEPTH, bp, DN_HEADS, DN_DK, DN_DV), state_delta.dtype)
    zero_ret = jnp.zeros((DEPTH, bp, RET_HEADS, RET_DK, RET_DV), state_ret.dtype)
    pos_prompt = jnp.arange(lp, dtype=jnp.int32)
    pos_sample = PAST_LEN + jnp.arange(x_sample.shape[1], dtype=jnp.int32)
    y_prompt, conv_p, delta_p, ret_p = _trunk(x_prompt, c_prompt, pos_prompt, zero_conv, zero_delta,
                                              zero_ret, params)
    y_sample, conv_s, delta_s, ret_s = _trunk(x_sample, c_sample, pos_sample, state_conv, state_delta,
                                              state_ret, params)
    return (y_prompt, y_sample, conv_p, delta_p, ret_p, conv_s, delta_s, ret_s)


_drawn_inputs = setup_inputs


def setup_inputs(seed=0):
    import zlib

    import numpy as np

    out = dict(_drawn_inputs(seed))
    spreads = {}
    factors = {'dn_norm_w': 8.0,
     'ret_gn_w': 8.0,
     'ret_gn_b': 8.0,
     'norm_ffn_w': 5.365,
     'router_bias': 3.659,
     'final_norm_w': 2.894}
    for name, (base, spread) in spreads.items():
        noise = np.random.default_rng([zlib.crc32(name.encode()), seed]).standard_normal(out[name].shape)
        drawn = base * np.exp(spread * noise) if base else spread * noise
        out[name] = __import__('jax').numpy.asarray(drawn.astype(out[name].dtype))
    for name, factor in factors.items():
        out[name] = (out[name] * factor).astype(out[name].dtype)
    return out
```

```python
from contextlib import ExitStack

import numpy as np

import concourse.bass as bass
from concourse import mybir

F32 = mybir.dt.float32
ALU = mybir.AluOpType
ACT = mybir.ActivationFunctionType
AX = mybir.AxisListType

D = 1024
DT = D // 128
P = 512
NS = 8
T = P + NS
TH = T // 2
C = 128
NC = P // C
H = 8
DK = 128
CONV = 4
CW = 3 * H * DK
CT = CW // 128
RH = 4
RK = 256
RV = 512
E = 64
TOPK = 8
NG = 8
TOPG = 4
DE = 256
RSCALE = 2.5
EPS = 1e-6
LEVELS = 7
PAST = 4096
Q_A, K_A, V_A, B_A, Z_A, Q_B, K_B, V_B, G_B, GATE_A, GATE_B = (
    0, 1024, 2048, 3072, 3088, 4112, 5136, 6160, 8208, 10256, 11280)
MOD_TURNS = 4
SLOTS = 6
R_BMOD, R_NMIX, R_NFFN, R_NFIN, R_GNW, R_GNB, R_DN, R_END = 0, 48, 56, 64, 72, 88, 104, 105
H_CONV, H_GC, H_BETA, H_BEXP, H_KEND, H_COLS = 0, 12, 16, 20, 24, 28


def constants():
    f = np.float32
    i = np.arange(C)
    ident = np.eye(128, dtype=f)
    incl = (i[None, :] >= i[:, None]).astype(f)
    level = np.zeros((LEVELS, C, C), f)
    for l in range(LEVELS):
        b = 1 << l
        same = (i[None, :] // (2 * b)) == (i[:, None] // (2 * b))
        level[l] = same & ((i[None, :] // b) % 2 == 1) & ((i[:, None] // b) % 2 == 0)
    half = RK // 2
    inv = f(10000.0) ** (-np.arange(half, dtype=f) / f(half))
    pos = np.concatenate([np.arange(P), np.full(NS, PAST)]).astype(f)
    ang = (inv[:, None] * pos[None, :]).astype(f)
    rot = np.stack([np.cos(ang), np.sin(ang)], axis=1).astype(f)
    lg = np.log(1.0 - 2.0 ** (-5.0 - np.arange(RH)))
    rel = np.arange(P)[None, :] - np.arange(128)[:, None]
    dmat = np.where(rel >= 0, np.exp(np.maximum(rel, 0) * lg[:, None, None]), 0.0) / 16.0
    left = (P - 1 - (np.arange(NC)[None, :] * 128 + np.arange(128)[:, None]))
    rcol = np.zeros((RH, 128, 8))
    rcol[:, :, 0:NC] = np.exp(left * lg[:, None, None]) / 16.0
    rcol[:, :, NC] = np.exp(lg)[:, None]
    mask8 = np.broadcast_to(np.eye(NS, dtype=f), (128, NS, NS))
    misc = np.concatenate([ident, incl, level.transpose(1, 0, 2).reshape(128, -1), mask8.reshape(128, -1)], axis=1)
    return {"misc": np.ascontiguousarray(misc, dtype=f), "rot": np.ascontiguousarray(rot),
            "dmat": dmat.astype(f), "rcol": rcol.astype(f)}


def build(nc, A):
    ctx = ExitStack()
    with ctx:
        sems = {}

        def S(name):
            if name not in sems:
                sems[name] = ctx.enter_context(nc.semaphore(name))
            return sems[name]

        def sb(name, shape, stack=ctx, dt=F32):
            return stack.enter_context(nc.sbuf_tensor(name, shape, dt))

        XT = sb("XT", [128, DT, T])
        HT = sb("HT", [128, DT, T])
        OA = sb("OA", [128, H, T])
        W = sb("W", [128, SLOTS, 8, 256])
        misc = sb("misc", [128, 128 * (2 + LEVELS) + NS * NS])
        ident = misc[:, 0:128]
        incl = misc[:, 128:256]
        lmask = misc[:, 256:256 + LEVELS * 128].rearrange("p (l i) -> p l i", l=LEVELS)
        mask8 = misc[:, 256 + LEVELS * 128:].rearrange("p (a b) -> p a b", a=NS)
        ones = sb("ones", [128, 128])
        eps = sb("eps", [128, 1])
        colsT = sb("colsT", [128, R_END])
        modT = sb("modT", [128, 48, 1 + NS])
        amod = sb("amod", [128, DT, 1 + NS])
        rsn = sb("rsn", [128, 2, TH])
        sqn = sb("sqn", [128, 2, T])
        hcols = sb("hcols", [128, H, H_COLS])
        cst = sb("cst", [128, CT, NS, CONV - 1])
        ps = ctx.enter_context(nc.psum_tensor("ps", [128, 8, 512], F32))

        chain = [0]

        def link(dve, ins):
            chain[0] += 1
            ins.then_inc(S("vector_chain"), 1)
            dve.wait_ge(S("vector_chain"), chain[0])

        def pair(b):
            return ps[:, b:b + 2, 0:TH]

        def halves(ap):
            return ap.rearrange("p (a n) -> p a n", a=2)

        w_in = A["w_in"][0].rearrange("(k p) n -> p k n", p=128)
        w_mod = A["w_mod"][0].rearrange("(k p) n -> p k n", p=128)
        rows_d = nc.dram_tensor("decay_rows", [H, 2, T], F32, kind="Internal").ap()

        loads = [0] * SLOTS
        fulls = [0] * SLOTS

        def load_slot(sp, s, src, turn=0, shape=None):
            sp.wait_ge(S(f"slot{s}_free"), loads[s] + turn + 1)
            sp.sem_inc(S("pad"), 1)
            dst = W[:, s] if shape is None else shape(W[:, s])
            return sp.dma_start(dst, src).then_inc(S(f"slot{s}_full"), 16)

        def slot_ready(pe, s, turn=0):
            pe.wait_ge(S(f"slot{s}_full"), (fulls[s] + turn + 1) * 16)

        st0 = ExitStack()
        xin = sb("xin", [128, NC + 1, D], st0)
        cin = sb("cin", [1 + NS, D], st0)
        csT = sb("csT", [128, DT, 1 + NS], st0)
        prow = sb("prow", [R_END, 128], st0)
        crow = sb("crow", [96, 128], st0)
        srow = sb("srow", [120, 5, 128], st0)
        convT = sb("convT", [128, CONV, CT], st0)
        hd_bc = sb("hd_bc", [128, 2, H], st0)
        wba = sb("wba", [128, DT, 16], st0)
        tok = sb("tok", [128, 12, NC + 1, H], st0)
        rows = sb("rows", [H, 2, T], st0)
        st0.close()
        SROWS = NS * 3 * CT
        SGRP = [(g * 120, min(120, SROWS - g * 120)) for g in range(5)]

        PARAMS = 14

        def sync_start(sp):
            sp.dma_start(misc[:, :], A["misc"]).then_inc(S("params_in"), 16)
            sp.dma_start(cin[0:1, :], A["c_prompt"]).then_inc(S("params_in"), 16)
            sp.dma_start(cin[1:1 + NS, :], A["c_sample"]).then_inc(S("params_in"), 16)
            for r, name, n in ((R_BMOD, "b_mod", 48), (R_NMIX, "norm_mix_w", 8), (R_NFFN, "norm_ffn_w", 8),
                               (R_GNW, "ret_gn_w", 16), (R_GNB, "ret_gn_b", 16), (R_DN, "dn_norm_w", 1)):
                sp.dma_start(prow[r:r + n, :], A[name][0].rearrange("(r p) -> r p", p=128)).then_inc(S("params_in"), 16)
            sp.dma_start(prow[R_NFIN:R_NFIN + 8, :], A["final_norm_w"].rearrange("(r p) -> r p", p=128)).then_inc(S("params_in"), 16)
            sp.dma_start(crow[:, :], A["conv_w"][0].rearrange("i (t p) -> (i t) p", p=128)).then_inc(S("params_in"), 16)
            for t in range(NC):
                sp.dma_start(xin[:, t, :], A["x_prompt"][0, t * 128:(t + 1) * 128, :]).then_inc(S("x_in"), 16)
            sp.dma_start(xin[0:NS, NC, :], A["x_sample"][:, 0, :]).then_inc(S("x_in"), 16)
            flat = A["state_conv"][0].rearrange("b i (t p) -> (b i t) p", p=128)
            for g, (r, n) in enumerate(SGRP):
                sp.dma_start(srow[0:n, g, :], flat[r:r + n, :]).then_inc(S("srow_in"), 16)
            for n, name in enumerate(("a_log", "dt_bias")):
                sp.dma_start(hd_bc[:, n, :], A[name].partition_broadcast(128).rearrange("p a h -> p (a h)")).then_inc(S("params_in"), 16)
            sp.dma_start(wba[:, :, :], w_in[:, :, B_A:B_A + 16]).then_inc(S("params_in"), 16)
            with sp.Fori(0, MOD_TURNS) as i:
                for s in range(SLOTS):
                    load_slot(sp, s, w_mod[:, :, bass.ds(i * 1536 + s * 256, 256)], i)
            for s in range(SLOTS):
                loads[s] += MOD_TURNS

        def tensor_start(pe):
            for s in range(SLOTS):
                pe.sem_inc(S(f"slot{s}_free"), 1)
            pe.wait_ge(S("params_in"), PARAMS * 16)
            pe.wait_ge(S("consts_set"), 2)
            for t in range(DT):
                mm = pe.transpose(ps[:, 0, t * 9:t * 9 + 9], cin[:, t * 128:(t + 1) * 128], ident[0:9, 0:9])
            mm.then_inc(S("start_ps"), 1)
            pe.transpose(ps[:, 1, 0:R_END], prow[:, :], ident[0:R_END, 0:R_END])
            pe.transpose(ps[:, 1, 128:128 + 96], crow[:, :], ident[0:96, 0:96]).then_inc(S("start_ps"), 1)
            pe.wait_ge(S("srow_in"), 5 * 16)
            for g, (r, n) in enumerate(SGRP):
                mm = pe.transpose(ps[:, 2 + g // 4, (g % 4) * 120:(g % 4) * 120 + n], srow[0:n, g, :], ident[0:n, 0:n])
            mm.then_inc(S("start_ps"), 1)
            pe.wait_ge(S("x_in"), 5 * 16)
            for d in range(DT):
                if d >= 4:
                    pe.wait_ge(S("xT_copied"), d - 3)
                for t in range(NC):
                    mm = pe.transpose(ps[:, 4 + d % 4, t * 128:(t + 1) * 128], xin[:, t, d * 128:(d + 1) * 128], ident)
                mm.then_inc(S("xT"), 1)
            pe.wait_ge(S("cs_silu"), 1)
            for d in range(DT):
                mm = pe.transpose(ps[:, 0, 128 + d * NS:128 + (d + 1) * NS], xin[0:NS, NC, d * 128:(d + 1) * 128], ident[0:NS, 0:NS])
            mm.then_inc(S("xsT"), 1)
            pe.wait_ge(S("rows_copied"), 2)
            with pe.Fori(0, MOD_TURNS) as i:
                pe.wait_ge(S("mod_copied"), i + 1)
                for s in range(SLOTS):
                    slot_ready(pe, s, i)
                    for m in range(2):
                        for k in range(DT):
                            mm = pe.matmul(ps[:, 1, (2 * s + m) * 9:(2 * s + m) * 9 + 9], W[:, s, k, m * 128:(m + 1) * 128],
                                           csT[:, k, :], start=(k == 0), stop=(k == DT - 1))
                    mm.then_inc(S(f"slot{s}_free"), 1)
            for s in range(SLOTS):
                fulls[s] += MOD_TURNS

        def scalar_start(act):
            act.wait_ge(S("start_ps"), 1)
            act.activation(csT[:, :, :], ps[:, 0, 0:72].rearrange("p (t b) -> p t b", t=DT), ACT.Silu).then_inc(S("cs_silu"), 1)
            for d in range(DT):
                act.wait_ge(S("xT"), d + 1)
                act.copy(XT[:, d, 0:P], ps[:, 4 + d % 4, :]).then_inc(S("xT_copied"), 1)
            act.wait_ge(S("xsT"), 1)
            act.copy(XT[:, :, P:T], ps[:, 0, 128:128 + DT * NS].rearrange("p (d b) -> p d b", d=DT)).then_inc(S("xsT_copied"), 1)

        def vector_start(dve):
            dve.memset(ones[:, :], 1.0).then_inc(S("consts_set"), 1)
            dve.memset(eps[:, :], EPS).then_inc(S("consts_set"), 1)
            dve.wait_ge(S("start_ps"), 2)
            dve.tensor_copy(colsT[:, :], ps[:, 1, 0:R_END]).then_inc(S("rows_copied"), 1)
            dve.tensor_copy(convT[:, :, :], ps[:, 1, 128:224].rearrange("p (i t) -> p i t", i=CONV)).then_inc(S("rows_copied"), 1)
            dve.wait_ge(S("rows_copied"), 2)
            for s in range(3):
                dve.tensor_copy(hcols[:, :, s * 4:s * 4 + 4], convT[:, :, s * H:(s + 1) * H].rearrange("p i h -> p h i"))
            dve.wait_ge(S("start_ps"), 3)
            for g, (r, n) in enumerate(SGRP):
                for q in range(n // CT):
                    b, i = divmod((r + q * CT) // CT, 3)
                    o = (g % 4) * 120 + q * CT
                    dve.tensor_copy(cst[:, :, b, i], ps[:, 2 + g // 4, o:o + CT])
            dve.sem_inc(S("mod_copied"), 1)
            with dve.Fori(0, MOD_TURNS) as i:
                dve.wait_ge(S("slot5_free"), i + 2)
                dve.tensor_tensor(modT[:, bass.ds(i * 12, 12), :], ps[:, 1, 0:108].rearrange("p (t b) -> p t b", t=12),
                                  colsT[:, bass.ds(i * 12, 12)].unsqueeze(2).to_broadcast([128, 12, 9]), ALU.add)\
                   .then_inc(S("mod_copied"), 1)

        def tensor_norm(pe, z, free):
            for sem, value in free:
                pe.wait_ge(S(sem), value)
            for d in range(DT):
                pe.wait_ge(S("norm_sq"), z * DT + d + 1)
                for a in range(2):
                    mm = pe.matmul(ps[:, a, 0:TH], ones[:, :], sqn[:, d % 2, a * TH:(a + 1) * TH],
                                   start=(d == 0), stop=(d == DT - 1))
                mm.then_inc(S("norm_sum"), 1)

        def scalar_norm(act, z, ready):
            for sem, value in ready:
                act.wait_ge(S(sem), value)
            for d in range(DT):
                if d >= 2:
                    act.wait_ge(S("norm_sum"), z * DT + d - 1)
                act.activation(sqn[:, d % 2, :], XT[:, d, :], ACT.Square).then_inc(S("norm_sq"), 1)
            act.wait_ge(S("norm_sum"), (z + 1) * DT)
            act.activation(rsn[:, :, :], pair(0), ACT.Sqrt, bias=eps[:, :], scale=1.0 / D).then_inc(S("norm_rms"), 1)

        def vector_norm(dve, z, r_w, part):
            if part is not None:
                for d in range(DT):
                    ins = dve.tensor_scalar(amod[:, d, :], modT[:, part * 8 + 8 + d, :], 1.0, colsT[:, r_w + d:r_w + d + 1],
                                            ALU.add, ALU.mult)
                link(dve, ins)
            dve.wait_ge(S("norm_rms"), z + 1)
            link(dve, dve.reciprocal(rsn[:, :, :], rsn[:, :, :]))
            flat = rsn[:, :, :].rearrange("p a n -> p (a n)")
            if part is None:
                for d in range(DT):
                    ins = dve.scalar_tensor_tensor(HT[:, d, :], XT[:, d, :], colsT[:, r_w + d:r_w + d + 1], flat, ALU.mult, ALU.mult)
                ins.then_inc(S("norm_done"), 1)
                return
            for d in range(DT):
                ins = dve.tensor_tensor(HT[:, d, :], XT[:, d, :], flat, ALU.mult)
            link(dve, ins)
            for d in range(DT):
                dve.tensor_scalar(HT[:, d, 0:P], HT[:, d, 0:P], amod[:, d, 0:1], modT[:, part * 8 + d, 0:1], ALU.mult, ALU.add)\
                   .then_inc(S("norm_done"), 1)
            link(dve, dve.tensor_tensor(HT[:, :, P:T], HT[:, :, P:T], amod[:, :, 1:9], ALU.mult))
            dve.tensor_tensor(HT[:, :, P:T], HT[:, :, P:T], modT[:, part * 8:part * 8 + 8, 1:9], ALU.add).then_inc(S("norm_done"), 1)

        NORMED = DT + 1

        X_B, X_A, X_T, X_G, X_BETA, X_GC, X_EGC, X_KE = range(8)

        def tensor_gates(pe):
            pe.wait_ge(S("norm_done"), NORMED)
            for t in range(NC + 1):
                n = 128 if t < NC else NS
                for k in range(DT):
                    mm = pe.matmul(ps[0:n, 2, t * 16:t * 16 + 16], HT[:, k, t * 128:t * 128 + n], wba[:, k, :],
                                   start=(k == 0), stop=(k == DT - 1))
            mm.then_inc(S("gate_ps"), 1)
            pe.wait_ge(S("g_ready"), 2)
            g = tok[:, X_G, 0:NC, :].rearrange("p t h -> p (t h)")
            pe.matmul(ps[:, 3, 0:32], incl, g, start=True, stop=True)
            pe.matmul(ps[:, 3, 64:96], ones[:, :], g, start=True, stop=True).then_inc(S("gate_ps"), 1)
            for t in range(NC):
                pe.matmul(ps[0:H, 4, t * 128:(t + 1) * 128], tok[:, X_G, t, :], incl, start=True, stop=True)
                pe.matmul(ps[0:H, 6, t * 128:(t + 1) * 128], tok[:, X_BETA, t, :], ident, start=True, stop=True)
            pe.matmul(ps[0:H, 5, 0:NS], tok[0:NS, X_G, NC, :], ident[0:NS, 0:NS], start=True, stop=True)
            pe.matmul(ps[0:H, 5, 8:8 + NS], tok[0:NS, X_BETA, NC, :], ident[0:NS, 0:NS], start=True, stop=True).then_inc(S("gate_ps"), 1)

        def scalar_gates(act):
            act.wait_ge(S("ba_copied"), 4)
            act.activation(tok[:, X_T, :, :], tok[:, X_B, :, :], ACT.Exp, scale=-1.0).then_inc(S("gate_fn"), 1)
            act.activation(tok[:, 9, :, :], tok[:, 8, :, :], ACT.Exp, scale=-1.0).then_inc(S("gate_fn"), 1)
            act.wait_ge(S("params_in"), PARAMS * 16)
            act.activation(hd_bc[:, 0, :], hd_bc[:, 0, :], ACT.Exp).then_inc(S("gate_fn"), 1)
            act.wait_ge(S("gate_fn"), 2)
            act.activation(tok[:, 10, :, :], tok[:, 9, :, :], ACT.Ln, bias=1.0).then_inc(S("gate_fn"), 1)
            act.wait_ge(S("gc_copied"), 2)
            act.activation(tok[:, X_EGC, 0:NC, :], tok[:, X_GC, 0:NC, :], ACT.Exp).then_inc(S("gate_fn"), 1)
            act.activation(tok[:, X_KE, 0:NC, :], tok[:, X_KE, 0:NC, :], ACT.Exp).then_inc(S("gate_fn"), 1)
            act.wait_ge(S("gate_ps"), 3)
            act.copy(rows[:, 0, 0:P], ps[0:H, 4, :]).then_inc(S("rows_done"), 1)
            act.copy(rows[:, 1, 0:P], ps[0:H, 6, :]).then_inc(S("rows_done"), 1)
            act.copy(rows[:, :, P:T], ps[0:H, 5, 0:16].rearrange("p (a b) -> p a b", a=2)).then_inc(S("rows_done"), 1)

        def vector_gates(dve):
            link(dve, dve.memset(tok[:, :, NC, :], 0.0))
            dve.wait_ge(S("gate_ps"), 1)
            dve.wait_ge(S("params_in"), PARAMS * 16)
            v = ps[:, 2, 0:64].rearrange("p (t c) -> p t c", t=NC)
            dt = hd_bc[:, 1, :]
            dve.tensor_copy(tok[:, X_B, 0:NC, :], v[:, :, 0:8]).then_inc(S("ba_copied"), 1)
            dve.tensor_copy(tok[0:NS, X_B, NC, :], ps[0:NS, 2, 64:72]).then_inc(S("ba_copied"), 1)
            dve.tensor_tensor(tok[:, X_A, 0:NC, :], v[:, :, 8:16], dt.unsqueeze(1).to_broadcast([128, NC, H]), ALU.add)
            link(dve, dve.tensor_tensor(tok[0:NS, X_A, NC, :], ps[0:NS, 2, 72:80], dt[0:NS, :], ALU.add))
            dve.scalar_tensor_tensor(tok[:, 8, :, :], tok[:, X_A, :, :], -1.0, tok[:, X_A, :, :], ALU.mult, ALU.max).then_inc(S("ba_copied"), 1)
            dve.tensor_scalar(tok[:, 11, :, :], tok[:, X_A, :, :], 0.0, None, ALU.max).then_inc(S("ba_copied"), 1)
            dve.wait_ge(S("gate_fn"), 1)
            link(dve, dve.tensor_scalar(tok[:, X_T, :, :], tok[:, X_T, :, :], 1.0, None, ALU.add))
            dve.reciprocal(tok[:, X_BETA, :, :], tok[:, X_T, :, :]).then_inc(S("g_ready"), 1)
            dve.wait_ge(S("gate_fn"), 4)
            link(dve, dve.tensor_tensor(tok[:, 10, :, :], tok[:, 10, :, :], tok[:, 11, :, :], ALU.add))
            dve.wait_ge(S("gate_fn"), 3)
            dve.scalar_tensor_tensor(tok[:, X_G, :, :], tok[:, 10, :, :], -1.0,
                                     hd_bc[:, 0, :].unsqueeze(1).to_broadcast([128, NC + 1, H]), ALU.mult, ALU.mult).then_inc(S("g_ready"), 1)
            dve.wait_ge(S("gate_ps"), 2)
            dve.tensor_copy(tok[:, X_GC, 0:NC, :], ps[:, 3, 0:32].rearrange("p (t h) -> p t h", t=NC)).then_inc(S("gc_copied"), 1)
            dve.wait_ge(S("gc_copied"), 1)
            dve.tensor_tensor(tok[:, X_KE, 0:NC, :], ps[:, 3, 64:96].rearrange("p (t h) -> p t h", t=NC), tok[:, X_GC, 0:NC, :],
                              ALU.subtract).then_inc(S("gc_copied"), 1)
            dve.wait_ge(S("gate_fn"), 6)
            v = lambda x: tok[:, x, 0:NC, :].rearrange("p t h -> p h t")
            dve.tensor_copy(hcols[:, :, H_GC:H_GC + NC], v(X_GC))
            dve.tensor_copy(hcols[:, :, H_BETA:H_BETA + NC], v(X_BETA))
            dve.tensor_copy(hcols[:, :, H_KEND:H_KEND + NC], v(X_KE))
            link(dve, dve.tensor_tensor(hcols[:, :, H_BEXP:H_BEXP + NC], v(X_BETA), v(X_EGC), ALU.mult))

        st3 = ExitStack()
        raw = sb("raw", [128, 3, CONV - 1 + T], st3)
        cacc = sb("cacc", [128, 3, T], st3)
        sacc = sb("sacc", [128, 3, NS, CONV], st3)
        sqk = sb("sqk", [128, 4, TH], st3)
        qk = sb("qk", [128, 2, T], st3)
        zs = sb("zs", [128, T], st3)
        rb = sb("rb", [128, 2, T], st3)
        eg = sb("eg", [128, T], st3)
        qd = sb("qd", [128, T], st3)
        dec = sb("dec", [128, NC, C], st3)
        bdec = sb("bdec", [128, NC, C], st3)
        qkd = sb("qkd", [128, NC, C], st3)
        at = sb("at", [128, NC, C], st3)
        atl = sb("atl", [128, LEVELS, NC, C], st3)
        Tm = sb("Tm", [128, NC, C], st3)
        Um = sb("Um", [128, NC, C], st3)
        Pm = sb("Pm", [128, NC, C], st3)
        kend = sb("kend", [128, NC, DK], st3)
        kbg = sb("kbg", [128, NC, DK], st3)
        vb = sb("vb", [128, NC, DK], st3)
        nwT = sb("nwT", [128, NC, C], st3)
        vnew = sb("vnew", [128, NC, DK], st3)
        Sc = sb("Sc", [128, NC, DK], st3)
        hc = sb("hc", [128, H_COLS], st3)
        sst = sb("sst", [128, NS, DK], st3)
        stmp = sb("stmp", [128, NS, DK], st3)
        svd = sb("svd", [128, NS, DK], st3)
        snew = sb("snew", [128, NS, DK], st3)
        nka = sb("nka", [128, 2, NS], st3)
        oT = sb("oT", [128, T], st3)
        osq = sb("osq", [128, 2, TH], st3)
        tail = sb("tail", [11, 3, DK], st3)
        zero28 = sb("zero28", [128, H_COLS], st3)
        st3.close()
        conv_p_d = A["out_conv_p"][0, 0].rearrange("i (s h p) -> i h s p", s=3, h=H)
        conv_s_d = A["out_conv_s"][0, :, 2].rearrange("b (s h p) -> b h s p", s=3, h=H)
        st_d = A["state_delta"][0]

        def slot_cols(s):
            return W[:, s].rearrange("p k n -> p (k n)").rearrange("p (m k n) -> p m k n", m=2, k=8)

        def sync_delta(sp):
            sp.wait_ge(S("rows_done"), 3)
            sp.dma_start(rows_d, rows[:, :, :]).then_inc(S("rows_out"), 16)
            sp.wait_ge(S("rows_out"), 16)
            with sp.Fori(0, H) as h:
                for s, cols in ((0, (Q_A, K_A)), (1, (V_A, Z_A))):
                    sp.wait_ge(S(f"slot{s}_free"), loads[s] + h + 1)
                    for m in range(2):
                        sp.dma_start(slot_cols(s)[:, m], w_in[:, :, bass.ds(h * 128 + cols[m], 128)]).then_inc(S(f"dslot{s}_full"), 16)
                sp.wait_ge(S("d_go"), h + 1)
                sp.dma_start(rb[:, :, :], rows_d[bass.ds(h, 1)].rearrange("h a t -> (h a t)").partition_broadcast(128)
                             .rearrange("p (a t) -> p a t", a=2)).then_inc(S("rb_in"), 16)
                sp.dma_start(sst[:, :, :], st_d[:, bass.ds(h, 1)].rearrange("b h k v -> k (b h) v")).then_inc(S("sst_in"), 16)
                sp.wait_ge(S("tail_done"), h + 1)
                sp.dma_start(conv_p_d[:, bass.ds(h, 1)].rearrange("i h s p -> (i h) s p"), tail[0:3, :, :]).then_inc(S("d_stored"), 16)
                sp.dma_start(conv_s_d[:, bass.ds(h, 1)].rearrange("b h s p -> (b h) s p"), tail[3:11, :, :]).then_inc(S("d_stored"), 16)
                sp.wait_ge(S("snew"), h + 1)
                sp.dma_start(A["out_delta_s"][0, :, bass.ds(h, 1)].rearrange("b h k v -> k (b h) v"), snew[:, :, :]).then_inc(S("d_stored"), 16)
                sp.wait_ge(S("d_state"), (h + 1) * NC)
                sp.dma_start(A["out_delta_p"][0, 0, bass.ds(h, 1)].rearrange("h k v -> k (h v)"), Sc[:, NC - 1, :]).then_inc(S("d_stored"), 16)
                sp.wait_ge(S("d_stored"), (h + 1) * 64)
                sp.sem_inc(S("pad"), 1)
            for s in (0, 1):
                loads[s] += H
            sp.dma_start(A["out_conv_s"][0, :, 0:2], A["state_conv"][0, :, 1:3]).then_inc(S("conv_out"), 16)

        def project(pe, bank, w):
            for k in range(DT):
                for a in range(2):
                    mm = pe.matmul(ps[:, bank + a, 0:TH], w[:, k, :], HT[:, k, a * TH:(a + 1) * TH], start=(k == 0), stop=(k == DT - 1))
            return mm

        def tensor_delta(pe):
            pe.wait_ge(S("rows_done"), 3)
            with pe.Fori(0, H) as h:
                n = h + 1
                pe.wait_ge(S("d_go"), h + 1)
                for s in (0, 1):
                    pe.wait_ge(S(f"dslot{s}_full"), n * 32)
                    w = slot_cols(s)
                    project(pe, 4 * s, w[:, 0]).then_inc(S("d_proj"), 1)
                    project(pe, 4 * s + 2, w[:, 1]).then_inc(S(f"slot{s}_free"), 1)
                pe.wait_ge(S("d_sqk"), n)
                for c in range(4):
                    mm = pe.matmul(ps[:, c, 0:TH], ones[:, :], sqk[:, c, :], start=True, stop=True)
                mm.then_inc(S("d_ssum"), 1)
                pe.wait_ge(S("d_zs"), n)
                for s in range(3):
                    mm = pe.transpose(ps[0:11, 6, s * 128:(s + 1) * 128], raw[:, s, 3 + P - 3:3 + T], ident)
                mm.then_inc(S("d_tail"), 1)
                pe.wait_ge(S("d_qk"), n)
                for c in range(NC):
                    kc = qk[:, 1, c * C:(c + 1) * C]
                    pe.matmul(ps[:, 4, c * C:(c + 1) * C], kc, kc, start=True, stop=True)
                    mm = pe.matmul(ps[:, 5, c * C:(c + 1) * C], kc, qk[:, 0, c * C:(c + 1) * C], start=True, stop=True)
                mm.then_inc(S("d_kk"), 1)
                pe.wait_ge(S("tail_done"), n)
                for c in range(NC):
                    pe.transpose(ps[:, 6, c * C:(c + 1) * C], qk[:, 1, c * C:(c + 1) * C], ident)
                    mm = pe.transpose(ps[:, 7, c * C:(c + 1) * C], cacc[:, 2, c * C:(c + 1) * C], ident)
                mm.then_inc(S("d_kvT"), 1)
                pe.wait_ge(S("d_atl"), h * LEVELS + 1)
                for c in range(NC):
                    mm = pe.transpose(ps[:, 0, c * C:(c + 1) * C], atl[:, 0, c, :], ident)
                mm.then_inc(S("d_A0"), 1)
                for l in range(1, LEVELS):
                    pe.wait_ge(S("d_atl"), h * LEVELS + l + 1)
                    pe.wait_ge(S("d_T"), h * (LEVELS - 1) + l)
                    for c in range(NC):
                        mm = pe.matmul(ps[:, 1, c * C:(c + 1) * C], atl[:, l, c, :], Tm[:, c, :], start=True, stop=True)
                    mm.then_inc(S("d_P"), 1)
                    pe.wait_ge(S("d_Pcopy"), h * (LEVELS - 1) + l)
                    pe.wait_ge(S("d_U"), h * LEVELS + l)
                    for c in range(NC):
                        mm = pe.matmul(ps[:, 2, c * C:(c + 1) * C], Pm[:, c, :], Um[:, c, :], start=True, stop=True)
                    mm.then_inc(S("d_dU"), 1)
                    if l < LEVELS - 1:
                        for c in range(NC):
                            mm = pe.matmul(ps[:, 3, c * C:(c + 1) * C], Um[:, c, :], Pm[:, c, :], start=True, stop=True)
                        mm.then_inc(S("d_dT"), 1)
                pe.wait_ge(S("d_U"), (h + 1) * LEVELS)
                pe.wait_ge(S("d_kv"), n * 3)
                for c in range(NC):
                    mm = pe.matmul(ps[:, 0, c * C:(c + 1) * C], kbg[:, c, :], Um[:, c, :], start=True, stop=True)
                mm.then_inc(S("d_wT"), 1)
                pe.wait_ge(S("s_vd"), n)
                pe.wait_ge(S("s_ks"), n)
                for a in range(2):
                    pe.matmul(ps[:, 1 + a, :], ones[:, :], svd[:, 4 * a:4 * a + 4, :].rearrange("p b v -> p (b v)"), start=True, stop=False)
                    mm = pe.matmul(ps[:, 1 + a, :], ones[:, :], stmp[:, 4 * a:4 * a + 4, :].rearrange("p b v -> p (b v)"), start=False, stop=True)
                mm.then_inc(S("s_u"), 1)
                pe.wait_ge(S("d_nwT"), n)
                pe.wait_ge(S("d_at"), n * 2)
                for c in range(NC):
                    cc = slice(c * C, (c + 1) * C)
                    mm = pe.matmul(ps[:, 4, cc], Um[:, c, :], vb[:, c, :], start=True, stop=(c == 0))
                    if c:
                        pe.wait_ge(S("d_state"), h * NC + c)
                        mm = pe.matmul(ps[:, 4, cc], nwT[:, c, :], Sc[:, c - 1, :], start=False, stop=True)
                    mm.then_inc(S("d_vn"), 1)
                    pe.wait_ge(S("d_vnew"), h * NC + c + 1)
                    pe.matmul(ps[:, 5, 0:DK], kend[:, c, :], vnew[:, c, :], start=True, stop=True).then_inc(S("d_ds"), 1)
                    if c:
                        pe.matmul(ps[:, 6, cc], Sc[:, c - 1, :], qd[:, cc], start=True, stop=False)
                    mm = pe.matmul(ps[:, 6, cc], vnew[:, c, :], qkd[:, c, :], start=(c == 0), stop=True)
                pe.wait_ge(S("snew"), n)
                for b in range(NS):
                    mm = pe.matmul(ps[:, 7, b:b + 1], snew[:, b, :], qd[:, P + b:P + b + 1], start=True, stop=True)
                mm.then_inc(S("d_o"), 1)
                pe.wait_ge(S("d_osq"), n)
                pe.wait_ge(S("d_state"), (h + 1) * NC)
                for a in range(2):
                    mm = pe.matmul(ps[:, 4 + a, 0:TH], ones[:, :], osq[:, a, :], start=True, stop=True)
                mm.then_inc(S("d_osum"), 1)

        def scalar_delta(act):
            with act.Fori(0, H) as h:
                n = h + 1
                act.wait_ge(S("d_go"), h + 1)
                act.wait_ge(S("d_proj"), h * 2 + 1)
                act.copy(raw[:, 0, 3:].rearrange("p (a n) -> p a n", a=2), pair(0)).then_inc(S("d_raw"), 1)
                act.wait_ge(S("slot0_free"), MOD_TURNS + 1 + n)
                act.copy(raw[:, 1, 3:].rearrange("p (a n) -> p a n", a=2), pair(2)).then_inc(S("d_raw"), 1)
                act.wait_ge(S("d_proj"), h * 2 + 2)
                act.copy(raw[:, 2, 3:].rearrange("p (a n) -> p a n", a=2), pair(4)).then_inc(S("d_raw"), 1)
                act.wait_ge(S("slot1_free"), MOD_TURNS + 1 + n)
                act.activation(halves(zs[:, :]), pair(6), ACT.Silu).then_inc(S("d_zs"), 1)
                act.wait_ge(S("d_conv"), n * 13)
                act.activation(cacc[:, :, :], cacc[:, :, :], ACT.Silu).then_inc(S("d_silu"), 1)
                act.wait_ge(S("d_silu"), n)
                act.activation(sqk[:, :, :].rearrange("p a n -> p (a n)"), cacc[:, 0:2, :].rearrange("p a n -> p (a n)"), ACT.Square)\
                   .then_inc(S("d_sqk"), 1)
                act.wait_ge(S("d_tail"), n)
                act.wait_ge(S("rb_in"), n * 16)
                act.copy(tail[:, :, :], ps[0:11, 6, 0:384].rearrange("p (s f) -> p s f", s=3)).then_inc(S("tail_done"), 1)
                act.wait_ge(S("d_ssum"), n)
                act.activation(sqk[:, :, :], ps[:, 0:4, 0:TH], ACT.Sqrt, bias=eps[:, :]).then_inc(S("d_rqk"), 1)
                act.wait_ge(S("rb_in"), n * 16)
                act.activation(eg[:, :], rb[:, 0, :], ACT.Exp).then_inc(S("d_eg"), 1)
                act.wait_ge(S("d_diff"), n * NC)
                act.activation(dec[:, :, :], dec[:, :, :], ACT.Exp).then_inc(S("d_dec"), 1)
                for l in range(1, LEVELS):
                    act.wait_ge(S("d_P"), h * (LEVELS - 1) + l)
                    act.copy(Pm[:, :, :].rearrange("p c i -> p (c i)"), ps[:, 1, :]).then_inc(S("d_Pcopy"), 1)
                act.wait_ge(S("d_wT"), n)
                act.mul(nwT[:, :, :].rearrange("p c i -> p (c i)"), ps[:, 0, :], -1.0).then_inc(S("d_nwT"), 1)
                for c in range(NC):
                    act.wait_ge(S("d_vn"), h * NC + c + 1)
                    act.copy(vnew[:, c, :], ps[:, 4, c * C:(c + 1) * C]).then_inc(S("d_vnew"), 1)
                act.wait_ge(S("d_o"), n)
                act.copy(oT[:, 0:P], ps[:, 6, :]).then_inc(S("d_oT"), 1)
                act.copy(oT[:, P:T], ps[:, 7, 0:NS]).then_inc(S("d_oT"), 1)
                act.wait_ge(S("d_oT"), n * 2)
                act.activation(osq[:, :, :], halves(oT[:, :]), ACT.Square).then_inc(S("d_osq"), 1)
                act.wait_ge(S("d_osum"), n)
                act.activation(osq[:, :, :], pair(4), ACT.Sqrt, bias=eps[:, :], scale=1.0 / DK).then_inc(S("d_orms"), 1)

        D_STEPS = 9

        def vector_delta(dve):
            dve.memset(raw[:, :, 0:3], 0.0)
            link(dve, dve.memset(zero28[:, :], 0.0))
            dve.sem_inc(S("d_go"), 1)
            with dve.Fori(0, H) as h:
                n = h + 1
                dve.tensor_tensor(hc[:, :], hcols[:, bass.ds(h, 1), :].rearrange("p h c -> p (h c)"), zero28[:, :], ALU.add).then_inc(S("d_step"), 1)
                dve.wait_ge(S("d_step"), h * D_STEPS + 1)
                for s in range(3):
                    dve.wait_ge(S("d_raw"), h * 3 + s + 1)
                    dve.tensor_scalar(cacc[:, s, 0:P], raw[:, s, 0:P], hc[:, s * 4:s * 4 + 1], None, ALU.mult).then_inc(S("d_conv"), 1)
                for i in range(1, CONV):
                    for s in range(3):
                        dve.wait_ge(S("d_conv"), h * 13 + (i - 1) * 3 + s + 1)
                        dve.scalar_tensor_tensor(cacc[:, s, 0:P], raw[:, s, i:i + P], hc[:, s * 4 + i:s * 4 + i + 1], cacc[:, s, 0:P],
                                                 ALU.mult, ALU.add).then_inc(S("d_conv"), 1)
                for s in range(3):
                    dve.tensor_tensor(sacc[:, s, :, 0:3], cst[:, bass.ds(h + s * H, 1), :, :].rearrange("p h b i -> p (h b) i"),
                                      hc[:, s * 4:s * 4 + 3].unsqueeze(1).to_broadcast([128, NS, 3]), ALU.mult).then_inc(S("d_sacc"), 1)
                    dve.tensor_scalar(sacc[:, s, :, 3], raw[:, s, 3 + P:3 + T], hc[:, s * 4 + 3:s * 4 + 4], None, ALU.mult).then_inc(S("d_sacc"), 1)
                dve.wait_ge(S("d_sacc"), n * 6)
                dve.tensor_reduce(cacc[:, :, P:T], sacc[:, :, :, :], AX.X, ALU.add).then_inc(S("d_conv"), 1)
                dve.wait_ge(S("rb_in"), n * 16)
                for c in range(NC):
                    dve.tensor_scalar(dec[:, c, :], rb[:, 0, c * C:(c + 1) * C], hc[:, H_GC + c:H_GC + c + 1], 0.0, ALU.subtract, ALU.min)\
                       .then_inc(S("d_diff"), 1)
                dve.wait_ge(S("d_rqk"), n)
                dve.reciprocal(sqk[:, :, :], sqk[:, :, :]).then_inc(S("d_step"), 1)
                dve.wait_ge(S("d_step"), h * D_STEPS + 2)
                dve.tensor_tensor(qk[:, :, :].rearrange("p a n -> p (a n)"), cacc[:, 0:2, :].rearrange("p a n -> p (a n)"),
                                  sqk[:, :, :].rearrange("p a n -> p (a n)"), ALU.mult).then_inc(S("d_qk"), 1)
                dve.wait_ge(S("d_dec"), n)
                dve.tensor_tensor(dec[:, :, :], dec[:, :, :], incl.unsqueeze(1).to_broadcast([128, NC, C]), ALU.mult).then_inc(S("d_step"), 1)
                dve.wait_ge(S("d_step"), h * D_STEPS + 3)
                dve.tensor_tensor(bdec[:, :, :], dec[:, :, :], rb[:, 1, 0:P].rearrange("p (c i) -> p c i", c=NC), ALU.mult).then_inc(S("d_step"), 1)
                dve.wait_ge(S("d_kk"), n)
                dve.wait_ge(S("d_step"), h * D_STEPS + 4)
                dve.tensor_tensor(at[:, :, :], ps[:, 4, :].rearrange("p (c i) -> p c i", c=NC), bdec[:, :, :], ALU.mult).then_inc(S("d_at"), 1)
                dve.scalar_tensor_tensor(qkd[:, :, :], ps[:, 5, :].rearrange("p (c i) -> p c i", c=NC), DK ** -0.5, dec[:, :, :],
                                         ALU.mult, ALU.mult).then_inc(S("d_at"), 1)
                dve.wait_ge(S("d_at"), n * 2)
                for l in range(LEVELS):
                    dve.tensor_tensor(atl[:, l], at[:, :, :], lmask[:, l].unsqueeze(1).to_broadcast([128, NC, C]), ALU.mult).then_inc(S("d_atl"), 1)
                eye = ident.unsqueeze(1).to_broadcast([128, NC, C])
                dve.wait_ge(S("d_atl"), h * LEVELS + 1)
                dve.tensor_tensor(Um[:, :, :], eye, atl[:, 0], ALU.subtract).then_inc(S("d_U"), 1)
                dve.wait_ge(S("d_A0"), n)
                dve.tensor_tensor(Tm[:, :, :], eye, ps[:, 0, :].rearrange("p (c i) -> p c i", c=NC), ALU.subtract).then_inc(S("d_T"), 1)
                dve.wait_ge(S("d_eg"), n)
                dve.scalar_tensor_tensor(qd[:, 0:P], qk[:, 0, 0:P], DK ** -0.5, eg[:, 0:P], ALU.mult, ALU.mult)
                dve.tensor_scalar(qd[:, P:T], qk[:, 0, P:T], DK ** -0.5, None, ALU.mult)
                dve.wait_ge(S("d_kvT"), n)
                for dst, bank, col in ((kend, 6, H_KEND), (kbg, 6, H_BEXP), (vb, 7, H_BETA)):
                    dve.tensor_tensor(dst[:, :, :], ps[:, bank, :].rearrange("p (c k) -> p c k", c=NC),
                                      hc[:, col:col + NC].unsqueeze(2).to_broadcast([128, NC, DK]), ALU.mult).then_inc(S("d_kv"), 1)
                dve.scalar_tensor_tensor(nka[:, 0, :], qk[:, 1, P:T], -1.0, eg[:, P:T], ALU.mult, ALU.mult).then_inc(S("d_step"), 1)
                dve.tensor_tensor(nka[:, 1, :], qk[:, 1, P:T], rb[:, 1, P:T], ALU.mult).then_inc(S("d_step"), 1)
                dve.wait_ge(S("d_step"), h * D_STEPS + 6)
                dve.wait_ge(S("sst_in"), n * 16)
                dve.tensor_tensor(stmp[:, :, :], sst[:, :, :], nka[:, 0, :].unsqueeze(2).to_broadcast([128, NS, DK]), ALU.mult).then_inc(S("s_ks"), 1)
                for l in range(1, LEVELS):
                    dve.wait_ge(S("d_dU"), h * (LEVELS - 1) + l)
                    if l < LEVELS - 1:
                        dve.wait_ge(S("d_dT"), h * (LEVELS - 2) + l)
                    dve.tensor_tensor(Um[:, :, :], Um[:, :, :], ps[:, 2, :].rearrange("p (c i) -> p c i", c=NC), ALU.subtract).then_inc(S("d_U"), 1)
                    if l < LEVELS - 1:
                        dve.tensor_tensor(Tm[:, :, :], Tm[:, :, :], ps[:, 3, :].rearrange("p (c i) -> p c i", c=NC), ALU.subtract).then_inc(S("d_T"), 1)
                dve.wait_ge(S("s_u"), n)
                dve.wait_ge(S("s_decayed"), n)
                dve.tensor_tensor(stmp[:, :, :], ps[:, 1:3, :].rearrange("p a (b v) -> p (a b) v", b=4),
                                  nka[:, 1, :].unsqueeze(2).to_broadcast([128, NS, DK]), ALU.mult).then_inc(S("d_step"), 1)
                dve.wait_ge(S("d_step"), h * D_STEPS + 7)
                dve.tensor_tensor(snew[:, :, :], sst[:, :, :], stmp[:, :, :], ALU.add).then_inc(S("snew"), 1)
                for c in range(NC):
                    dve.wait_ge(S("d_ds"), h * NC + c + 1)
                    if c == 0:
                        dve.tensor_copy(Sc[:, 0, :], ps[:, 5, 0:DK]).then_inc(S("d_state"), 1)
                    else:
                        dve.wait_ge(S("d_state"), h * NC + c)
                        dve.scalar_tensor_tensor(Sc[:, c, :], Sc[:, c - 1, :], eg[:, c * C + C - 1:c * C + C], ps[:, 5, 0:DK],
                                                 ALU.mult, ALU.add).then_inc(S("d_state"), 1)
                dve.wait_ge(S("d_orms"), n)
                dve.reciprocal(osq[:, :, :], osq[:, :, :]).then_inc(S("d_step"), 1)
                dve.wait_ge(S("d_step"), h * D_STEPS + 8)
                dve.tensor_tensor(halves(oT[:, :]), halves(oT[:, :]), osq[:, :, :], ALU.mult).then_inc(S("d_step"), 1)
                dve.wait_ge(S("d_step"), h * D_STEPS + 9)
                dve.scalar_tensor_tensor(OA[:, bass.ds(h, 1), :].rearrange("p h t -> p (h t)"), oT[:, :], colsT[:, R_DN:R_DN + 1], zs[:, :],
                                         ALU.mult, ALU.mult).then_inc(S("d_go"), 1)

        def pool_delta(pool):
            with pool.Fori(0, H) as h:
                n = h + 1
                pool.wait_ge(S("d_silu"), n)
                pool.tensor_tensor(svd[:, :, :], ident.unsqueeze(1).to_broadcast([128, NS, DK]),
                                   cacc[:, 2, P:T].unsqueeze(2).to_broadcast([128, NS, DK]), ALU.mult).then_inc(S("s_vd"), 1)
                pool.wait_ge(S("s_ks"), n)
                pool.wait_ge(S("d_eg"), n)
                pool.tensor_tensor(sst[:, :, :], sst[:, :, :], eg[:, P:T].unsqueeze(2).to_broadcast([128, NS, DK]), ALU.mult).then_inc(S("s_decayed"), 1)

        OB = sb("OB", [128, RH * 4, T])
        st4 = ExitStack()
        rot = sqn
        rt = sb("rt", [128, 4, T], st4)
        ON = sb("ON", [128, NC + 1, RV], st4)
        flat_on = ON[:, :, :].rearrange("p t v -> p (t v)")
        qr = flat_on[:, 0:2 * T].rearrange("p (a t) -> p a t", a=2)
        kr = flat_on[:, 2 * T:4 * T].rearrange("p (a t) -> p a t", a=2)
        V = sb("V", [128, NC + 1, RV], st4)
        SG = sb("SG", [128, 4, T], st4)
        dm = sb("dm", [128, P], st4)
        PT = sb("PT", [128, 1280], st4)
        PO = (0, 512, 896, 1152)
        kd = PT[:, 0:NC * RK].rearrange("p (t k) -> p t k", t=NC)
        rst = sb("rst", [128, 2, 2, RV], st4)
        rnew = sb("rnew", [128, 2, 2, RV], st4)
        rc = sb("rc", [128, 8], st4)
        bn6 = sb("bn6", [128, NC + 1, 6], st4)
        mv = sb("mv", [128, NC + 1, 2], st4)
        sd = sb("sd", [128, NC + 1], st4)
        qdg = sb("qdg", [128, 2, NS, NS], st4)
        gnc = sb("gnc", [128, 2, 4], st4)
        zero4 = sb("zero4", [128, 4], st4)
        st4.close()
        kdg = rt[0:NS, :, :].rearrange("p a t -> p (a t)")[:, 0:NS * RK].rearrange("p (b k) -> p b k", b=NS)
        ret_p_d = A["out_ret_p"][0, 0].rearrange("h (a p) v -> p h a v", p=128)
        ret_s_d = A["out_ret_s"][0].rearrange("b h (a p) v -> p b h a v", p=128)
        ret_i_d = A["state_ret"][0].rearrange("b h (a p) v -> p b h a v", p=128)

        def delta_over(eng):
            eng.wait_ge(S("d_go"), H + 1)
            eng.wait_ge(S("d_stored"), H * 64)

        def sync_ret(sp):
            delta_over(sp)
            sp.wait_ge(S("norm_done"), NORMED)
            sp.dma_start(rot[:, :, :], A["rot"]).then_inc(S("rot_in"), 16)
            with sp.Fori(0, RH) as h:
                for s, col, w in ((0, Q_B, RK), (1, K_B, RK), (2, V_B, RV), (3, V_B + 256, RV), (4, G_B, RV), (5, G_B + 256, RV)):
                    load_slot(sp, s, w_in[:, :, bass.ds(h * w + col, 256)], h)
                sp.wait_ge(S("r_go"), h + 1)
                sp.dma_start(dm[:, :], A["dmat"][bass.ds(h, 1)].rearrange("h p i -> p (h i)")).then_inc(S("r_tab"), 16)
                sp.dma_start(rc[:, :], A["rcol"][bass.ds(h, 1)].rearrange("h p i -> p (h i)")).then_inc(S("r_tab"), 16)
            for s in range(SLOTS):
                loads[s] += RH

        def tensor_ret(pe):
            with pe.Fori(0, RH) as h:
                n = h + 1
                pe.wait_ge(S("r_go"), n)
                for s in (0, 1):
                    slot_ready(pe, s, h)
                    project(pe, 4 * s, W[:, s, :, 0:128])
                    project(pe, 4 * s + 2, W[:, s, :, 128:256]).then_inc(S(f"slot{s}_free"), 1)
                for s in (2, 3):
                    slot_ready(pe, s, h)
                    for t in range(NC + 1):
                        if s == 2 and t == 0:
                            pe.wait_ge(S("r_rt"), h * 8 + 4)
                        if s == 2 and t == NC:
                            pe.wait_ge(S("r_rt"), h * 8 + 8)
                        m = 128 if t < NC else NS
                        for k in range(DT):
                            mm = pe.matmul(ps[0:m, t, (s - 2) * 256:(s - 1) * 256], HT[:, k, t * 128:t * 128 + m], W[:, s, k, :],
                                           start=(k == 0), stop=(k == DT - 1))
                    mm.then_inc(S(f"slot{s}_free"), 1)
                for f in range(4):
                    s = 4 + f // 2
                    if f % 2 == 0:
                        slot_ready(pe, s, h)
                    if f in (1, 2):
                        pe.wait_ge(S("r_V"), h * 5 + 2 * f)
                    if f == 3:
                        pe.wait_ge(S("r_sg"), h * 4 + 1)
                    mm = project(pe, (6, 0, 2, 6)[f], W[:, s, :, (f % 2) * 128:(f % 2) * 128 + 128])
                    if f % 2 == 0:
                        mm.then_inc(S("r_g"), 1)
                    else:
                        mm.then_inc(S(f"slot{s}_free"), 1)
                pe.wait_ge(S("r_qkr"), n * 4)
                pe.wait_ge(S("r_V"), n * 5)
                for t in range(NC):
                    if t == 2:
                        pe.wait_ge(S("r_sg"), h * 4 + 2)
                    for a in range(2):
                        mm = pe.matmul(ps[:, (4, 5, 0, 1)[t], 0:P - t * 128], kr[:, a, t * 128:(t + 1) * 128], qr[:, a, t * 128:P],
                                       start=(a == 0), stop=(a == 1))
                    mm.then_inc(S("r_s"), 1)
                for i in range(NC):
                    pe.wait_ge(S("r_pt"), h * 4 + i + 1)
                    pe.wait_ge(S("r_sg"), h * 4 + (3 if i < 2 else 4))
                    for j in range(i + 1):
                        o = PO[j] + (i - j) * 128
                        mm = pe.matmul(ps[:, (2, 3, 6, 7)[i], :], PT[:, o:o + 128], V[:, j, :], start=(j == 0), stop=(j == i))
                    mm.then_inc(S("r_o"), 1)
                for t in range(NC):
                    for a in range(2):
                        pe.transpose(ps[:, t // 2, (t % 2) * 256 + a * 128:(t % 2) * 256 + (a + 1) * 128], kr[:, a, t * 128:(t + 1) * 128], ident)
                for a in range(2):
                    mm = pe.transpose(ps[0:NS, 4, a * 128:(a + 1) * 128], kr[:, a, P:T], ident)
                mm.then_inc(S("r_kT"), 1)
                pe.wait_ge(S("r_kd"), n * 2)
                for a in range(2):
                    for t in range(NC):
                        mm = pe.matmul(ps[:, 4 + a, :], kd[:, t, a * 128:(a + 1) * 128], V[:, t, :], start=(t == 0), stop=(t == NC - 1))
                mm.then_inc(S("r_sf"), 1)
                pe.wait_ge(S("r_on"), h * 5 + 4)
                for b in range(NS):
                    if b == 1:
                        pe.wait_ge(S("r_sfc"), n)
                    if b >= 2:
                        pe.wait_ge(S("r_new"), h * NS + b - 1)
                    for a in range(2):
                        mm = pe.matmul(ps[:, (b % 2) * 4 + a, :], kdg[:, b, a * 128:(a + 1) * 128], V[0:NS, NC, :], start=True, stop=True)
                    mm.then_inc(S("r_kv"), 1)
                    if b >= 1:
                        tensor_ret_o(pe, h, b - 1)
                tensor_ret_o(pe, h, NS - 1)
                for f in range(4):
                    if f == 3:
                        pe.wait_ge(S("r_on"), n * 5)
                    for i in range(NC):
                        mm = pe.transpose(ps[:, (2, 3, 7, 0)[f], i * 128:(i + 1) * 128], ON[:, i, f * 128:(f + 1) * 128], ident)
                    mm.then_inc(S("r_onT"), 1)
                for f in range(4):
                    mm = pe.transpose(ps[:, 1, f * NS:(f + 1) * NS], ON[0:NS, NC, f * 128:(f + 1) * 128], ident[0:NS, 0:NS])
                mm.then_inc(S("r_onT"), 1)
            for s in range(SLOTS):
                fulls[s] += RH

        def tensor_ret_o(pe, h, b):
            pe.wait_ge(S("r_new"), h * NS + b + 1)
            for a in range(2):
                mm = pe.matmul(ps[0:NS, 6, :], qdg[:, a, b, :], rnew[:, b % 2, a, :], start=(b == 0 and a == 0), stop=(b == NS - 1 and a == 1))
            mm.then_inc(S("r_os"), 1)

        def scalar_ret(act):
            delta_over(act)
            with act.Fori(0, RH) as h:
                n = h + 1
                hs = bass.ds(h, 1)
                act.wait_ge(S("r_go"), n)
                for b in range(2):
                    act.dma_start(rst[:, b], ret_i_d[:, b, hs].rearrange("p h a v -> p (h a) v")).then_inc(S(f"r_st{b}"), 16)
                act.wait_ge(S("slot3_free"), MOD_TURNS + 1 + n)
                for t in range(NC):
                    act.copy(V[:, t, :], ps[:, t, :]).then_inc(S("r_V"), 1)
                act.copy(V[0:NS, NC, :], ps[0:NS, 4, :]).then_inc(S("r_V"), 1)
                for f in range(4):
                    if f % 2 == 0:
                        act.wait_ge(S("r_g"), h * 2 + f // 2 + 1)
                    else:
                        act.wait_ge(S(f"slot{4 + f // 2}_free"), MOD_TURNS + 1 + n)
                    act.activation(halves(SG[:, f, :]), pair((6, 0, 2, 6)[f]), ACT.Silu).then_inc(S("r_sg"), 1)
                act.wait_ge(S("r_mv"), h * 5 + 4)
                act.activation(sd[:, 0:NC], mv[:, 0:NC, 1], ACT.Sqrt, bias=eps[:, :]).then_inc(S("r_sd"), 1)
                act.wait_ge(S("r_sf"), n)
                act.copy(rnew[:, 1], ps[:, 4:6, :]).then_inc(S("r_sfc"), 1)
                act.wait_ge(S("r_sfc"), n)
                act.dma_start(ret_p_d[:, hs].rearrange("p h a v -> p (h a) v"), rnew[:, 1]).then_inc(S("r_out1"), 16)
                for b in range(NS):
                    act.wait_ge(S("r_new"), h * NS + b + 1)
                    act.dma_start(ret_s_d[:, b, hs].rearrange("p h a v -> p (h a) v"), rnew[:, b % 2]).then_inc(S(f"r_out{b % 2}"), 16)
                    if b + 2 < NS:
                        act.dma_start(rst[:, b % 2], ret_i_d[:, b + 2, hs].rearrange("p h a v -> p (h a) v")).then_inc(S(f"r_st{b % 2}"), 16)
                act.wait_ge(S("r_mv"), n * 5)
                act.activation(sd[0:NS, NC:NC + 1], mv[0:NS, NC, 1:2], ACT.Sqrt, bias=eps[0:NS, :]).then_inc(S("r_sd"), 1)
                for f in range(4):
                    act.wait_ge(S("r_onT"), h * 5 + f + 1)
                    act.activation(rt[:, f, 0:P], ps[:, (2, 3, 7, 0)[f], :], ACT.Identity, scale=gnc[:, 0, f:f + 1], bias=gnc[:, 1, f:f + 1])\
                       .then_inc(S("r_aff"), 1)
                act.wait_ge(S("r_onT"), n * 5)
                for f in range(4):
                    act.activation(rt[:, f, P:T], ps[:, 1, f * NS:(f + 1) * NS], ACT.Identity, scale=gnc[:, 0, f:f + 1], bias=gnc[:, 1, f:f + 1])\
                       .then_inc(S("r_aff"), 1)

        R_STEPS = 7

        def vector_ret(dve):
            delta_over(dve)
            link(dve, dve.memset(zero4[:, :], 0.0))
            dve.wait_ge(S("rot_in"), 16)
            dve.sem_inc(S("r_go"), 1)
            with dve.Fori(0, RH) as h:
                n = h + 1
                for i, r in enumerate((R_GNW, R_GNB)):
                    dve.tensor_tensor(gnc[:, i, :], colsT[:, bass.ds(h * 4 + r, 4)], zero4[:, :], ALU.add)
                for s, dst in ((0, qr), (1, kr)):
                    dve.wait_ge(S(f"slot{s}_free"), MOD_TURNS + H + 1 + n)
                    if s == 1:
                        dve.wait_ge(S("r_qkr"), h * 4 + 2)
                    for j, (x, c) in enumerate(((0, 0), (2, 1), (0, 1), (2, 0))):
                        dve.tensor_tensor(halves(rt[:, j, :]), pair(4 * s + x), halves(rot[:, c, :]), ALU.mult).then_inc(S("r_rt"), 1)
                dve.wait_ge(S("r_qkr"), n * 4)
                for a in range(2):
                    dve.tensor_tensor(qdg[:, a], qr[:, a, P:T].unsqueeze(1).to_broadcast([128, NS, NS]), mask8, ALU.mult)
                dve.wait_ge(S("r_tab"), n * 32)
                for t in range(NC):
                    w = P - t * 128
                    dve.wait_ge(S("r_s"), h * 4 + t + 1)
                    dve.tensor_tensor(PT[:, PO[t]:PO[t] + w], ps[:, (4, 5, 0, 1)[t], 0:w], dm[:, 0:w], ALU.mult).then_inc(S("r_pt"), 1)
                for i in range(NC):
                    dve.wait_ge(S("r_o"), h * 4 + i + 1)
                    dve.bn_stats(bn6[:, i, :], ps[:, (2, 3, 6, 7)[i], :]).then_inc(S("r_step"), 1)
                    dve.wait_ge(S("r_step"), h * R_STEPS + i + 1)
                    dve.sem_inc(S("pad"), 1)
                    dve.bn_aggr(mv[:, i, :], bn6[:, i, :]).then_inc(S("r_mv"), 1)
                dve.wait_ge(S("r_kT"), n)
                dve.tensor_tensor(kd[:, :, :], ps[:, 0:2, :].rearrange("p a (t k) -> p (a t) k", t=2),
                                  rc[:, 0:NC].unsqueeze(2).to_broadcast([128, NC, RK]), ALU.mult).then_inc(S("r_kd"), 1)
                dve.scalar_tensor_tensor(kdg, ps[0:NS, 4, 0:RK].unsqueeze(1).to_broadcast([NS, NS, RK]), RK ** -0.5,
                                         ident[0:NS, 0:NS].unsqueeze(2).to_broadcast([NS, NS, RK]), ALU.mult, ALU.mult).then_inc(S("r_kd"), 1)
                dve.wait_ge(S("r_sd"), h * 2 + 1)
                dve.reciprocal(sd[:, 0:NC], sd[:, 0:NC]).then_inc(S("r_step"), 1)
                dve.wait_ge(S("r_step"), h * R_STEPS + 5)
                for i in range(NC):
                    dve.tensor_scalar(ON[:, i, :], ps[:, (2, 3, 6, 7)[i], :], mv[:, i, 0:1], sd[:, i:i + 1], ALU.subtract, ALU.mult).then_inc(S("r_on"), 1)
                for b in range(NS):
                    dve.wait_ge(S("r_kv"), h * NS + b + 1)
                    dve.wait_ge(S(f"r_st{b % 2}"), (h * 4 + b // 2 + 1) * 16)
                    if b % 2 == 1:
                        dve.wait_ge(S("r_out1"), (h * 5 + b // 2 + 1) * 16)
                    elif b >= 2:
                        dve.wait_ge(S("r_out0"), (h * 4 + b // 2) * 16)
                    if b >= 2:
                        dve.wait_ge(S("r_os"), h * NS + b - 1)
                    dve.scalar_tensor_tensor(rnew[:, b % 2], rst[:, b % 2], rc[:, NC:NC + 1], ps[:, (b % 2) * 4:(b % 2) * 4 + 2, :],
                                             ALU.mult, ALU.add).then_inc(S("r_new"), 1)
                dve.wait_ge(S("r_os"), n * NS)
                dve.bn_stats(bn6[0:NS, NC, :], ps[0:NS, 6, :]).then_inc(S("r_step"), 1)
                dve.wait_ge(S("r_step"), h * R_STEPS + 6)
                dve.sem_inc(S("pad"), 1)
                dve.bn_aggr(mv[0:NS, NC, :], bn6[0:NS, NC, :]).then_inc(S("r_mv"), 1)
                dve.wait_ge(S("r_sd"), n * 2)
                dve.reciprocal(sd[0:NS, NC:NC + 1], sd[0:NS, NC:NC + 1]).then_inc(S("r_step"), 1)
                dve.wait_ge(S("r_step"), h * R_STEPS + 7)
                dve.tensor_scalar(ON[0:NS, NC, :], ps[0:NS, 6, :], mv[0:NS, NC, 0:1], sd[0:NS, NC:NC + 1], ALU.subtract, ALU.mult)\
                   .then_inc(S("r_on"), 1)
                dve.wait_ge(S("r_aff"), n * 8)
                dve.wait_ge(S("r_out0"), n * 64)
                dve.wait_ge(S("r_out1"), n * 80)
                dve.tensor_tensor(OB[:, bass.ds(h * 4, 4), :], rt[:, :, :], SG[:, :, :], ALU.mult).then_inc(S("r_go"), 1)

        def pool_ret(pool):
            with pool.Fori(0, RH) as h:
                for s, dst in ((0, qr), (1, kr)):
                    pool.wait_ge(S("r_rt"), h * 8 + 4 * s + 4)
                    pool.tensor_tensor(dst[:, 0, :], rt[:, 0, :], rt[:, 1, :], ALU.subtract).then_inc(S("r_qkr"), 1)
                    pool.tensor_tensor(dst[:, 1, :], rt[:, 2, :], rt[:, 3, :], ALU.add).then_inc(S("r_qkr"), 1)

        Y = sb("Y", [128, DT, T])
        st5 = ExitStack()
        sg = sb("sg", [128, 2, T], st5)
        mt = sb("mt", [128, 2, T], st5)
        smx = sb("smx", [128, DT, NS], st5)
        st5.close()
        GATE_TURNS = 4
        USED_MIX = [MOD_TURNS + H + RH if s < 2 else MOD_TURNS + RH for s in range(SLOTS)]
        wda = A["w_down_a"][0].rearrange("(k p) n -> p k n", p=128)
        wdb = A["w_down_b"][0].rearrange("(k p) n -> p k n", p=128)
        wo = A["w_out"][0].rearrange("(k p) n -> p k n", p=128)

        def sync_merge(sp):
            with sp.Fori(0, GATE_TURNS) as i:
                for s, src in enumerate((w_in[:, :, bass.ds(i * 256 + GATE_A, 256)], w_in[:, :, bass.ds(i * 256 + GATE_B, 256)],
                                         wda[:, :, bass.ds(i * 256, 256)], wdb[:, 0:8, bass.ds(i * 256, 256)],
                                         wdb[:, 8:16, bass.ds(i * 256, 256)])):
                    load_slot(sp, s, src, i)
            for s in range(5):
                loads[s] += GATE_TURNS
            for s in range(4):
                load_slot(sp, s, wo[:, :, s * 256:(s + 1) * 256])
                loads[s] += 1

        def product(pe, bank, parts):
            for k, (w, x) in enumerate(parts):
                for a in range(2):
                    mm = pe.matmul(ps[:, bank + a, 0:TH], w, x[:, a * TH:(a + 1) * TH], start=(k == 0), stop=(k == len(parts) - 1))
            return mm

        def tensor_merge(pe):
            pe.wait_ge(S("r_go"), RH + 1)
            with pe.Fori(0, GATE_TURNS) as i:
                for m in range(2):
                    f = slice(m * 128, (m + 1) * 128)
                    plans = ((0, [(W[:, 0, k, f], HT[:, k, :]) for k in range(DT)], (0,)),
                             (2, [(W[:, 1, k, f], HT[:, k, :]) for k in range(DT)], (1,)),
                             (4, [(W[:, 2, k, f], OA[:, k, :]) for k in range(DT)], (2,)),
                             (6, [(W[:, 3 + k // 8, k % 8, f], OB[:, k, :]) for k in range(16)], (3, 4)))
                    for q, (bank, parts, slots) in enumerate(plans):
                        if m == 0:
                            for s in slots:
                                slot_ready(pe, s, i)
                        if q < 2:
                            pe.wait_ge(S("m_sig"), i * 4 + m * 2 + q + 1)
                        else:
                            pe.wait_ge(S("m_mul"), i * 4 + m * 2 + q - 1)
                        mm = product(pe, bank, parts)
                        mm.then_inc(S("m_tile"), 1)
                    if m == 1:
                        for s in range(5):
                            pe.wait_ge(S("m_tile"), i * 8 + 8)
                            pe.sem_inc(S(f"slot{s}_free"), 1)
            for s in range(5):
                fulls[s] += GATE_TURNS
            pe.wait_ge(S("m_merged"), 9)
            for d in range(DT):
                if d % 2 == 0:
                    slot_ready(pe, d // 2)
                if d >= 4:
                    pe.wait_ge(S("m_res"), d - 3)
                mm = product(pe, 2 * (d % 4), [(W[:, d // 2, k, (d % 2) * 128:(d % 2) * 128 + 128], Y[:, k, :]) for k in range(DT)])
                mm.then_inc(S("m_out"), 1)
            pe.wait_ge(S("m_out"), DT)
            for s in range(4):
                pe.sem_inc(S(f"slot{s}_free"), 1)
                fulls[s] += 1

        def scalar_merge(act):
            act.wait_ge(S("r_go"), RH + 1)
            act.sem_inc(S("m_sig"), 2)
            with act.Fori(0, GATE_TURNS) as i:
                for m in range(2):
                    act.wait_ge(S("m_mul"), i * 4 + m * 2 + 2)
                    for q in range(2):
                        act.wait_ge(S("m_tile"), i * 8 + m * 4 + q + 1)
                        act.activation(halves(sg[:, q, :]), pair(2 * q), ACT.Sigmoid).then_inc(S("m_sig"), 1)

        def vector_merge(dve):
            dve.sem_inc(S("m_mul"), 2)
            dve.sem_inc(S("m_merged"), 1)
            with dve.Fori(0, GATE_TURNS) as i:
                for m in range(2):
                    dve.wait_ge(S("m_merged"), i * 2 + m + 1)
                    for q in range(2):
                        dve.wait_ge(S("m_tile"), i * 8 + m * 4 + q + 3)
                        dve.wait_ge(S("m_sig"), i * 4 + m * 2 + q + 3)
                        dve.tensor_tensor(halves(mt[:, q, :]), pair(4 + 2 * q), halves(sg[:, q, :]), ALU.mult).then_inc(S("m_mul"), 1)
                    dve.wait_ge(S("m_mul"), i * 4 + m * 2 + 4)
                    dve.tensor_tensor(Y[:, bass.ds(i * 2 + m, 1), :].rearrange("p d t -> p (d t)"), mt[:, 0, :], mt[:, 1, :], ALU.add)\
                       .then_inc(S("m_merged"), 1)
            residual(dve, "m_out", "m_res", 2)

        def residual(dve, ready, done, part):
            for d in range(DT):
                g = modT[:, part * 8 + d, :]
                dve.wait_ge(S(ready), d + 1)
                b = 2 * (d % 4)
                dve.scalar_tensor_tensor(XT[:, d, 0:TH], ps[:, b, 0:TH], g[:, 0:1], XT[:, d, 0:TH], ALU.mult, ALU.add)
                dve.scalar_tensor_tensor(XT[:, d, TH:P], ps[:, b + 1, 0:P - TH], g[:, 0:1], XT[:, d, TH:P], ALU.mult, ALU.add)
                dve.tensor_tensor(smx[:, d, :], ps[:, b + 1, P - TH:TH], g[:, 1:9], ALU.mult).then_inc(S(done), 1)
            dve.wait_ge(S(done), DT)
            dve.tensor_tensor(XT[:, :, P:T], XT[:, :, P:T], smx[:, :, :], ALU.add).then_inc(S(done), 1)

        st6 = ExitStack()
        rwrow = sb("rwrow", [E, DT, 128], st6)
        rwT = sb("rwT", [128, DT, E], st6)
        rbias = sb("rbias", [128, E], st6)
        NT = NC + 1
        sc = sb("sc", [128, NT, E], st6)
        bs = sb("bs", [128, NT, E], st6)
        rep = sb("rep", [128, NT, E], st6)
        sel = sb("sel", [128, NT, E], st6)
        g8 = sb("g8", [128, NT, NG, 8], st6)
        gs = sb("gs", [128, NT, 16], st6)
        gv = sb("gv", [128, NT, 8], st6)
        gr = sb("gr", [128, NT, 16], st6)
        gm = sb("gm", [128, NT, NG], st6)
        v8 = sb("v8", [128, NT, 8], st6)
        wsum = sb("wsum", [128, NT], st6)
        cwT = sb("cwT", [E, T], st6)
        st6.close()
        LOW, LOWER = -1e30, -2e30
        cw_d = nc.dram_tensor("combine_weights", [E, T], F32, kind="Internal").ap()

        def sync_route(sp):
            sp.wait_ge(S("m_res"), DT + 1)
            sp.dma_start(rwrow[:, :, :], A["router_w"][0].rearrange("e (k p) -> e k p", p=128)).then_inc(S("router_in"), 16)
            sp.dma_start(rbias[:, :], A["router_bias"].partition_broadcast(128).rearrange("p a e -> p (a e)")).then_inc(S("router_in"), 16)

        def tensor_route(pe):
            pe.wait_ge(S("router_in"), 32)
            for k in range(DT):
                mm = pe.transpose(ps[:, 2, k * E:(k + 1) * E], rwrow[:, k, :], ident[0:E, 0:E])
            mm.then_inc(S("route_ps"), 1)
            pe.wait_ge(S("rwT"), 1)
            pe.wait_ge(S("norm_done"), 2 * NORMED)
            for t in range(NT):
                n = 128 if t < NC else NS
                for k in range(DT):
                    mm = pe.matmul(ps[0:n, 3, t * E:(t + 1) * E], HT[:, k, t * 128:t * 128 + n], rwT[:, k, :], start=(k == 0), stop=(k == DT - 1))
            mm.then_inc(S("route_ps"), 1)

        def scalar_route(act):
            act.wait_ge(S("route_ps"), 1)
            act.wait_ge(S("m_res"), DT + 1)
            act.copy(rwT[:, :, :], ps[:, 2, :].rearrange("p (k e) -> p k e", k=DT)).then_inc(S("rwT"), 1)
            act.wait_ge(S("sc_clear"), 1)
            act.wait_ge(S("route_ps"), 2)
            act.activation(sc[:, 0:NC, :], ps[:, 3, 0:NC * E].rearrange("p (t e) -> p t e", t=NC), ACT.Exp, scale=-1.0).then_inc(S("sc_exp"), 1)
            act.activation(sc[0:NS, NC, :], ps[0:NS, 3, NC * E:NT * E], ACT.Exp, scale=-1.0).then_inc(S("sc_exp"), 1)

        def vector_route(dve):
            dve.wait_ge(S("m_res"), DT + 1)
            dve.memset(sc[:, NC, :], 0.0).then_inc(S("sc_clear"), 1)
            dve.memset(gs[:, :, 8:16], LOW)
            link(dve, dve.memset(gv[:, :, 4:8], LOW))
            dve.wait_ge(S("sc_exp"), 2)
            flat = lambda x: x[:, :, :].rearrange("p t e -> p (t e)")
            link(dve, dve.tensor_scalar(flat(sc), flat(sc), 1.0, None, ALU.add))
            link(dve, dve.reciprocal(flat(sc), flat(sc)))
            dve.wait_ge(S("router_in"), 32)
            link(dve, dve.tensor_tensor(bs[:, :, :], sc[:, :, :], rbias[:, :].unsqueeze(1).to_broadcast([128, NT, E]), ALU.add))
            for t in range(NT):
                for g in range(NG):
                    ins = dve.max(g8[:, t, g, :], bs[:, t, g * 8:(g + 1) * 8])
            link(dve, ins)
            link(dve, dve.tensor_tensor(gs[:, :, 0:NG], g8[:, :, :, 0], g8[:, :, :, 1], ALU.add))
            for t in range(NT):
                ins = dve.max(v8[:, t, :], gs[:, t, 0:NG])
            link(dve, ins)
            link(dve, dve.tensor_copy(gv[:, :, 0:TOPG], v8[:, :, 0:TOPG]))
            for t in range(NT):
                ins = dve.match_replace(gr[:, t, :], gv[:, t, :], gs[:, t, :], LOWER)
            link(dve, ins)
            link(dve, dve.tensor_tensor(gm[:, :, :], gr[:, :, 0:NG], gs[:, :, 0:NG], ALU.not_equal))
            link(dve, dve.tensor_copy(rep[:, :, :].rearrange("p t (g e) -> p t g e", g=NG), gm[:, :, :].unsqueeze(3).to_broadcast([128, NT, NG, 8])))
            dve.tensor_tensor(flat(bs), flat(bs), flat(rep), ALU.mult)
            link(dve, dve.tensor_scalar(flat(rep), flat(rep), 1.0, -LOW, ALU.subtract, ALU.mult))
            link(dve, dve.tensor_tensor(flat(bs), flat(bs), flat(rep), ALU.add))
            for t in range(NT):
                ins = dve.max(v8[:, t, :], bs[:, t, :])
            link(dve, ins)
            for t in range(NT):
                ins = dve.match_replace(rep[:, t, :], v8[:, t, :], bs[:, t, :], LOWER)
            link(dve, ins)
            link(dve, dve.tensor_tensor(flat(sel), flat(rep), flat(bs), ALU.not_equal))
            link(dve, dve.tensor_tensor(flat(sc), flat(sc), flat(sel), ALU.mult))
            link(dve, dve.tensor_reduce(wsum[:, :], sc[:, :, :], AX.X, ALU.add))
            link(dve, dve.reciprocal(wsum[:, :], wsum[:, :]))
            dve.scalar_tensor_tensor(sc[:, :, :], sc[:, :, :], RSCALE, wsum[:, :].unsqueeze(2).to_broadcast([128, NT, E]), ALU.mult, ALU.mult)\
               .then_inc(S("cw"), 1)

        st7 = ExitStack()
        cwb = sb("cwb", [128, 2, T], st7)
        gsl = sb("gsl", [128, 2, T], st7)
        hid = sb("hid", [128, 2, T], st7)
        st7.close()
        wg = A["w_gate"][0].rearrange("e (k p) n -> p e k n", p=128)
        wu = A["w_up"][0].rearrange("e (k p) n -> p e k n", p=128)
        wd = A["w_down"][0].rearrange("e (k p) n -> p e k n", p=128)

        def down(s):
            return W[:, s].rearrange("p k n -> p (k n)").rearrange("p (k n) -> p k n", k=2)

        def sync_experts(sp):
            load_slot(sp, 0, A["ws_gate"][0].rearrange("(k p) n -> p k n", p=128))
            load_slot(sp, 1, A["ws_up"][0].rearrange("(k p) n -> p k n", p=128))
            load_slot(sp, 2, A["ws_down"][0].rearrange("(k p) n -> p k n", p=128), shape=lambda w: w.rearrange("p k n -> p (k n)").rearrange("p (k n) -> p k n", k=2))
            for s in range(3):
                loads[s] += 1
            sp.wait_ge(S("cwT"), 2)
            sp.dma_start(cw_d, cwT[:, :]).then_inc(S("cw_out"), 16)
            sp.wait_ge(S("cw_out"), 16)
            with sp.Fori(0, E // 2) as i:
                for j in range(2):
                    e = i * 2 + j
                    es = bass.ds(e, 1)
                    load_slot(sp, 3 * j, wg[:, es].rearrange("p e k n -> p (e k) n"), i)
                    load_slot(sp, 3 * j + 1, wu[:, es].rearrange("p e k n -> p (e k) n"), i)
                    load_slot(sp, 3 * j + 2, wd[:, es].rearrange("p e k n -> p (e k) n"), i, shape=lambda w: w.rearrange("p k n -> p (k n)").rearrange("p (k n) -> p k n", k=2))
                    sp.wait_ge(S("e_hid"), e * 2 + 1)
                    sp.sem_inc(S("pad"), 1)
                    sp.dma_start(cwb[:, j, :], cw_d[es].rearrange("e t -> (e t)").partition_broadcast(128)).then_inc(S(f"cwb{j}_in"), 16)
            for s in range(SLOTS):
                loads[s] += E // 2

        def tensor_expert(pe, j, m, turn):
            for f in range(2):
                for q in range(2):
                    if f == 0:
                        slot_ready(pe, 3 * j + q, turn)
                    pe.wait_ge(S("e_y"), m * 8 + 5 + 2 * f + q)
                    mm = product(pe, 4 * f + 2 * q, [(W[:, 3 * j + q, k, f * 128:(f + 1) * 128], HT[:, k, :]) for k in range(DT)])
                    if f == 0:
                        mm.then_inc(S("e_gu"), 1)
                    else:
                        mm.then_inc(S(f"slot{3 * j + q}_free"), 1)
            slot_ready(pe, 3 * j + 2, turn)
            for d in range(DT):
                if d == 0:
                    pe.wait_ge(S("e_hid"), m * 2 + 2)
                elif d >= 4:
                    pe.wait_ge(S("e_y"), m * 8 + 5 + d)
                mm = product(pe, 2 * (d % 4), [(down(3 * j + 2)[:, k, d * 128:(d + 1) * 128], hid[:, k, :]) for k in range(2)])
                if d < DT - 1:
                    mm.then_inc(S("e_down"), 1)
                else:
                    mm.then_inc(S(f"slot{3 * j + 2}_free"), 1)

        def tensor_experts(pe):
            pe.wait_ge(S("cw"), 1)
            for t in range(NC):
                pe.transpose(ps[0:E, 4, t * 128:(t + 1) * 128], sc[:, t, :], ident)
            pe.transpose(ps[0:E, 5, 0:NS], sc[0:NS, NC, :], ident[0:NS, 0:NS]).then_inc(S("route_ps"), 1)
            pe.wait_ge(S("cwT"), 2)
            tensor_expert(pe, 0, 0, 0)
            for s in range(3):
                fulls[s] += 1
            with pe.Fori(0, E // 2) as i:
                for j in range(2):
                    tensor_expert(pe, j, i * 2 + j + 1, i)
            for s in range(SLOTS):
                fulls[s] += E // 2

        USED_MOE = [u + g for u, g in zip(USED_MIX, (5, 5, 5, 5, 4, 0))]

        def scalar_expert(act, j, m, uses, shared=False):
            for f in range(2):
                if not shared:
                    act.wait_ge(S("e_hid"), m * 2 + f - 1)
                if f == 0:
                    act.wait_ge(S("e_gu"), m * 2 + 1)
                else:
                    act.wait_ge(S(f"slot{3 * j}_free"), uses(3 * j) + 2)
                act.activation(halves(gsl[:, f, :]), pair(4 * f), ACT.Silu).then_inc(S("e_silu"), 1)

        def scalar_experts(act):
            act.wait_ge(S("route_ps"), 3)
            act.copy(cwT[:, 0:P], ps[0:E, 4, :]).then_inc(S("cwT"), 1)
            act.copy(cwT[:, P:T], ps[0:E, 5, 0:NS]).then_inc(S("cwT"), 1)
            act.wait_ge(S("cw_out"), 16)
            scalar_expert(act, 0, 0, lambda s: USED_MOE[s], shared=True)
            with act.Fori(0, E // 2) as i:
                for j in range(2):
                    scalar_expert(act, j, i * 2 + j + 1, lambda s: i + USED_MOE[s] + (1 if s < 3 else 0))

        def vector_expert(dve, j, m, uses, shared=False, turn=0):
            for f in range(2):
                if f == 0:
                    dve.wait_ge(S("e_gu"), m * 2 + 2)
                else:
                    dve.wait_ge(S(f"slot{3 * j + 1}_free"), uses(3 * j + 1) + 2)
                dve.wait_ge(S("e_silu"), m * 2 + f + 1)
                if shared:
                    dve.tensor_tensor(halves(hid[:, f, :]), pair(4 * f + 2), halves(gsl[:, f, :]), ALU.mult).then_inc(S("e_hid"), 1)
                else:
                    if f == 0:
                        dve.wait_ge(S(f"cwb{j}_in"), (turn + 1) * 16)
                    dve.tensor_tensor(halves(gsl[:, f, :]), pair(4 * f + 2), halves(gsl[:, f, :]), ALU.mult).then_inc(S("e_gu2"), 1)
                    dve.wait_ge(S("e_gu2"), (m - 1) * 2 + f + 1)
                    dve.tensor_tensor(hid[:, f, :], gsl[:, f, :], cwb[:, j, :], ALU.mult).then_inc(S("e_hid"), 1)
            for d in range(DT):
                if d < DT - 1:
                    dve.wait_ge(S("e_down"), m * 7 + d + 1)
                else:
                    dve.wait_ge(S(f"slot{3 * j + 2}_free"), uses(3 * j + 2) + 2)
                if shared:
                    dve.tensor_copy(halves(Y[:, d, :]), pair(2 * (d % 4))).then_inc(S("e_y"), 1)
                else:
                    dve.tensor_tensor(halves(Y[:, d, :]), pair(2 * (d % 4)), halves(Y[:, d, :]), ALU.add).then_inc(S("e_y"), 1)

        def vector_experts(dve):
            dve.sem_inc(S("e_y"), 8)
            dve.wait_ge(S("cw_out"), 16)
            vector_expert(dve, 0, 0, lambda s: USED_MOE[s], shared=True)
            with dve.Fori(0, E // 2) as i:
                for j in range(2):
                    vector_expert(dve, j, i * 2 + j + 1, lambda s: i + USED_MOE[s] + (1 if s < 3 else 0), turn=i)

        yout = sb("yout", [128, 2, D])

        def vector_final(dve):
            for d in range(DT):
                g = modT[:, 40 + d, :]
                if d == 0:
                    dve.wait_ge(S("e_y"), 8 * (E + 2))
                dve.scalar_tensor_tensor(XT[:, d, 0:P], Y[:, d, 0:P], g[:, 0:1], XT[:, d, 0:P], ALU.mult, ALU.add).then_inc(S("f_res"), 1)
            link(dve, dve.tensor_tensor(Y[:, :, P:T], Y[:, :, P:T], modT[:, 40:48, 1:9], ALU.mult))
            dve.tensor_tensor(XT[:, :, P:T], XT[:, :, P:T], Y[:, :, P:T], ALU.add).then_inc(S("f_res"), 1)

        def tensor_final(pe):
            pe.wait_ge(S("norm_done"), 2 * NORMED + 1)
            for t in range(NC + 1):
                n = 128 if t < NC else NS
                if t >= 2:
                    pe.wait_ge(S("f_copied"), (t - 1) * 2)
                for d in range(DT):
                    mm = pe.transpose(ps[0:n, 4 + 2 * (t % 2) + d // 4, (d % 4) * 128:(d % 4) * 128 + 128], HT[:, d, t * 128:t * 128 + n], ident)
                mm.then_inc(S("f_T"), 1)

        def scalar_final(act):
            for t in range(NC + 1):
                n = 128 if t < NC else NS
                act.wait_ge(S("f_T"), t + 1)
                if t >= 2:
                    act.wait_ge(S(f"y_out{t % 2}"), (t // 2) * 16)
                for a in range(2):
                    act.copy(yout[0:n, t % 2, a * 512:(a + 1) * 512], ps[0:n, 4 + 2 * (t % 2) + a, :]).then_inc(S("f_copied"), 1)

        def sync_final(sp):
            for t in range(NC + 1):
                sp.wait_ge(S("f_copied"), (t + 1) * 2)
                if t < NC:
                    sp.dma_start(A["out_y_p"][0, t * 128:(t + 1) * 128, :], yout[:, t % 2, :]).then_inc(S(f"y_out{t % 2}"), 16)
                else:
                    sp.dma_start(A["out_y_s"][:, 0, :], yout[0:NS, t % 2, :]).then_inc(S(f"y_out{t % 2}"), 16)
            sp.wait_ge(S("y_out0"), 48)
            sp.wait_ge(S("y_out1"), 32)
            sp.wait_ge(S("conv_out"), 16)
            sp.wait_ge(S("d_stored"), H * 64)
            sp.wait_ge(S("r_out0"), RH * 64)
            sp.wait_ge(S("r_out1"), RH * 80)

        block = ctx.enter_context(nc.Block())

        @block.sync
        def _(sp):
            sync_start(sp)
            sync_delta(sp)
            sync_ret(sp)
            sync_merge(sp)
            sync_route(sp)
            sync_experts(sp)
            sync_final(sp)

        @block.tensor
        def _(pe):
            tensor_start(pe)
            tensor_norm(pe, 0, [("mod_copied", MOD_TURNS + 1), ("xsT_copied", 1)])
            tensor_gates(pe)
            tensor_delta(pe)
            tensor_ret(pe)
            tensor_merge(pe)
            tensor_norm(pe, 1, [("m_res", DT + 1)])
            tensor_route(pe)
            tensor_experts(pe)
            tensor_norm(pe, 2, [("e_y", 8 * (E + 2))])
            tensor_final(pe)

        @block.scalar
        def _(act):
            scalar_start(act)
            scalar_norm(act, 0, [("xT_copied", DT), ("xsT_copied", 1)])
            scalar_gates(act)
            scalar_delta(act)
            scalar_ret(act)
            scalar_merge(act)
            scalar_norm(act, 1, [("m_res", DT + 1)])
            scalar_route(act)
            scalar_experts(act)
            scalar_norm(act, 2, [("f_res", DT + 1)])
            scalar_final(act)

        @block.vector
        def _(dve):
            vector_start(dve)
            vector_norm(dve, 0, R_NMIX, 0)
            vector_gates(dve)
            vector_delta(dve)
            vector_ret(dve)
            vector_merge(dve)
            vector_norm(dve, 1, R_NFFN, 3)
            vector_route(dve)
            vector_experts(dve)
            vector_final(dve)
            vector_norm(dve, 2, R_NFIN, None)

        @block.gpsimd
        def _(pool):
            pool_delta(pool)
            pool_ret(pool)


_INS = ['x_prompt', 'x_sample', 'state_conv', 'state_delta', 'state_ret', 'c_prompt', 'c_sample',
        'w_mod', 'b_mod', 'norm_mix_w', 'w_in', 'conv_w', 'a_log', 'dt_bias', 'dn_norm_w', 'ret_gn_w', 'ret_gn_b',
        'w_down_a', 'w_down_b', 'w_out', 'norm_ffn_w', 'router_w', 'router_bias', 'w_gate', 'w_up', 'w_down',
        'ws_gate', 'ws_up', 'ws_down', 'final_norm_w']
_OUTS = [('y_p', (1, P, D)), ('y_s', (NS, 1, D)), ('conv_p', (1, 1, 3, CW)), ('delta_p', (1, 1, H, DK, DK)),
         ('ret_p', (1, 1, RH, RK, RV)), ('conv_s', (1, NS, 3, CW)), ('delta_s', (1, NS, H, DK, DK)),
         ('ret_s', (1, NS, RH, RK, RV))]


def kernel(**inputs):
    import concourse.bacc as _bacc
    from concourse.bass_utils import run_bass_kernel_spmd as _run

    nc = _bacc.Bacc("TRN2", target_bir_lowering=False, num_devices=1)
    arrays, aps = {}, {}
    given = {name: np.ascontiguousarray(inputs[name]) for name in _INS}
    for name, a in list(given.items()) + list(constants().items()):
        arrays[f"in_{name}_dram"] = a
        aps[name] = nc.dram_tensor(f"in_{name}_dram", a.shape, mybir.dt.from_np(a.dtype), kind="ExternalInput").ap()
    for name, shape in _OUTS:
        aps[f"out_{name}"] = nc.dram_tensor(f"out_{name}_dram", shape, F32, kind="ExternalOutput").ap()
    build(nc, aps)
    r = _run(nc, [arrays], core_ids=[0])
    return tuple(r.results[0][f"out_{name}_dram"] for name, _ in _OUTS)
```

```python
from contextlib import ExitStack

import numpy as np

import concourse.bass as bass
from concourse import mybir

F32 = mybir.dt.float32
ALU = mybir.AluOpType
ACT = mybir.ActivationFunctionType
AX = mybir.AxisListType

D = 1024
DT = D // 128
P = 512
NS = 8
T = P + NS
TH = T // 2
C = 128
NC = P // C
H = 8
DK = 128
CONV = 4
CW = 3 * H * DK
CT = CW // 128
RH = 4
RK = 256
RV = 512
E = 64
TOPK = 8
NG = 8
TOPG = 4
DE = 256
RSCALE = 2.5
EPS = 1e-6
NB = 102
BIG = 8192
M_PLACE, M_BLOCK, M_THR, M_EXP, M_CAP, M_POS, M_END = 0, 128, 128 + NB, 133 + NB, 134 + NB, 136 + NB, 136 + NB + T
LEVELS = 7
PAST = 4096
Q_A, K_A, V_A, B_A, Z_A, Q_B, K_B, V_B, G_B, GATE_A, GATE_B = (
    0, 1024, 2048, 3072, 3088, 4112, 5136, 6160, 8208, 10256, 11280)
MOD_TURNS = 4
SLOTS = 6
R_BMOD, R_NMIX, R_NFFN, R_NFIN, R_GNW, R_GNB, R_DN, R_END = 0, 48, 56, 64, 72, 88, 104, 105
H_CONV, H_GC, H_BETA, H_BEXP, H_KEND, H_COLS = 0, 12, 16, 20, 24, 28


def constants():
    f = np.float32
    i = np.arange(C)
    ident = np.eye(128, dtype=f)
    incl = (i[None, :] >= i[:, None]).astype(f)
    level = np.zeros((LEVELS, C, C), f)
    for l in range(LEVELS):
        b = 1 << l
        same = (i[None, :] // (2 * b)) == (i[:, None] // (2 * b))
        level[l] = same & ((i[None, :] // b) % 2 == 1) & ((i[:, None] // b) % 2 == 0)
    half = RK // 2
    inv = f(10000.0) ** (-np.arange(half, dtype=f) / f(half))
    pos = np.concatenate([np.arange(P), np.full(NS, PAST)]).astype(f)
    ang = (inv[:, None] * pos[None, :]).astype(f)
    rot = np.stack([np.cos(ang), np.sin(ang)], axis=1).astype(f)
    lg = np.log(1.0 - 2.0 ** (-5.0 - np.arange(RH)))
    rel = np.arange(P)[None, :] - np.arange(128)[:, None]
    dmat = np.where(rel >= 0, np.exp(np.maximum(rel, 0) * lg[:, None, None]), 0.0) / 16.0
    left = (P - 1 - (np.arange(NC)[None, :] * 128 + np.arange(128)[:, None]))
    rcol = np.zeros((RH, 128, 8))
    rcol[:, :, 0:NC] = np.exp(left * lg[:, None, None]) / 16.0
    rcol[:, :, NC] = np.exp(lg)[:, None]
    mask8 = np.broadcast_to(np.eye(NS, dtype=f), (128, NS, NS))
    misc = np.concatenate([ident, incl, level.transpose(1, 0, 2).reshape(128, -1), mask8.reshape(128, -1)], axis=1)
    moe = np.zeros((128, M_END))
    moe[:, M_PLACE:M_BLOCK] = np.arange(1, 129)
    moe[:, M_BLOCK:M_THR] = np.arange(NB)
    moe[:, M_THR:M_EXP] = np.arange(5) * 128
    moe[:, M_EXP] = np.arange(128)
    for j in range(2):
        moe[:, M_CAP + j] = np.where(np.arange(128) < 127, BIG, (T + j) * TOPK)
    moe[:, M_POS:M_END] = np.arange(T) * TOPK - 1 - BIG
    return {"moe": moe.astype(f), "misc": np.ascontiguousarray(misc, dtype=f), "rot": np.ascontiguousarray(rot),
            "dmat": dmat.astype(f), "rcol": rcol.astype(f)}


def build(nc, A):
    ctx = ExitStack()
    with ctx:
        sems = {}

        def S(name):
            if name not in sems:
                sems[name] = ctx.enter_context(nc.semaphore(name))
            return sems[name]

        def sb(name, shape, stack=ctx, dt=F32):
            return stack.enter_context(nc.sbuf_tensor(name, shape, dt))

        XT = sb("XT", [128, DT, T])
        HT = sb("HT", [128, DT, T])
        OA = sb("OA", [128, H, T])
        W = sb("W", [128, SLOTS, 8, 256])
        misc = sb("misc", [128, 128 * (2 + LEVELS) + NS * NS])
        ident = misc[:, 0:128]
        incl = misc[:, 128:256]
        lmask = misc[:, 256:256 + LEVELS * 128].rearrange("p (l i) -> p l i", l=LEVELS)
        mask8 = misc[:, 256 + LEVELS * 128:].rearrange("p (a b) -> p a b", a=NS)
        ones = sb("ones", [128, 128])
        eps = sb("eps", [128, 1])
        colsT = sb("colsT", [128, R_END])
        modT = sb("modT", [128, 48, 1 + NS])
        amod = sb("amod", [128, DT, 1 + NS])
        rsn = sb("rsn", [128, 2, TH])
        sqn = sb("sqn", [128, 2, T])
        hcols = sb("hcols", [128, H, H_COLS])
        cst = sb("cst", [128, CT, NS, CONV - 1])
        ps = ctx.enter_context(nc.psum_tensor("ps", [128, 8, 512], F32))

        chain = [0]

        def link(dve, ins):
            chain[0] += 1
            ins.then_inc(S("vector_chain"), 1)
            dve.wait_ge(S("vector_chain"), chain[0])

        def pair(b):
            return ps[:, b:b + 2, 0:TH]

        def halves(ap):
            return ap.rearrange("p (a n) -> p a n", a=2)

        w_in = A["w_in"][0].rearrange("(k p) n -> p k n", p=128)
        w_mod = A["w_mod"][0].rearrange("(k p) n -> p k n", p=128)
        rows_d = nc.dram_tensor("decay_rows", [H, 2, T], F32, kind="Internal").ap()

        loads = [0] * SLOTS
        fulls = [0] * SLOTS

        def load_slot(sp, s, src, turn=0, shape=None):
            sp.wait_ge(S(f"slot{s}_free"), loads[s] + turn + 1)
            sp.sem_inc(S("pad"), 1)
            dst = W[:, s] if shape is None else shape(W[:, s])
            return sp.dma_start(dst, src).then_inc(S(f"slot{s}_full"), 16)

        def slot_ready(pe, s, turn=0):
            pe.wait_ge(S(f"slot{s}_full"), (fulls[s] + turn + 1) * 16)

        mrow = OA[0:1 + NS, 0:3, :].rearrange("p a t -> p (a t)")[:, 0:1536]
        st0 = ExitStack()
        xin = sb("xin", [128, NC + 1, D], st0)
        cin = sb("cin", [1 + NS, D], st0)
        csT = sb("csT", [128, DT, 1 + NS], st0)
        prow = sb("prow", [R_END, 128], st0)
        crow = sb("crow", [96, 128], st0)
        srow = sb("srow", [120, 5, 128], st0)
        convT = sb("convT", [128, CONV, CT], st0)
        hd_bc = sb("hd_bc", [128, 2, H], st0)
        wba = sb("wba", [128, DT, 16], st0)
        tok = sb("tok", [128, 12, NC + 1, H], st0)
        rows = sb("rows", [H, 2, T], st0)
        st0.close()
        SROWS = NS * 3 * CT
        SGRP = [(g * 120, min(120, SROWS - g * 120)) for g in range(5)]

        PARAMS = 14

        def sync_start(sp):
            sp.dma_start(misc[:, :], A["misc"]).then_inc(S("params_in"), 16)
            sp.dma_start(cin[0:1, :], A["c_prompt"]).then_inc(S("params_in"), 16)
            sp.dma_start(cin[1:1 + NS, :], A["c_sample"]).then_inc(S("params_in"), 16)
            for r, name, n in ((R_BMOD, "b_mod", 48), (R_NMIX, "norm_mix_w", 8), (R_NFFN, "norm_ffn_w", 8),
                               (R_GNW, "ret_gn_w", 16), (R_GNB, "ret_gn_b", 16), (R_DN, "dn_norm_w", 1)):
                sp.dma_start(prow[r:r + n, :], A[name][0].rearrange("(r p) -> r p", p=128)).then_inc(S("params_in"), 16)
            sp.dma_start(prow[R_NFIN:R_NFIN + 8, :], A["final_norm_w"].rearrange("(r p) -> r p", p=128)).then_inc(S("params_in"), 16)
            sp.dma_start(crow[:, :], A["conv_w"][0].rearrange("i (t p) -> (i t) p", p=128)).then_inc(S("params_in"), 16)
            for t in range(NC):
                sp.dma_start(xin[:, t, :], A["x_prompt"][0, t * 128:(t + 1) * 128, :]).then_inc(S("x_in"), 16)
            sp.dma_start(xin[0:NS, NC, :], A["x_sample"][:, 0, :]).then_inc(S("x_in"), 16)
            flat = A["state_conv"][0].rearrange("b i (t p) -> (b i t) p", p=128)
            for g, (r, n) in enumerate(SGRP):
                sp.dma_start(srow[0:n, g, :], flat[r:r + n, :]).then_inc(S("srow_in"), 16)
            for n, name in enumerate(("a_log", "dt_bias")):
                sp.dma_start(hd_bc[:, n, :], A[name].partition_broadcast(128).rearrange("p a h -> p (a h)")).then_inc(S("params_in"), 16)
            sp.dma_start(wba[:, :, :], w_in[:, :, B_A:B_A + 16]).then_inc(S("params_in"), 16)
            with sp.Fori(0, MOD_TURNS) as i:
                for s in range(SLOTS):
                    load_slot(sp, s, w_mod[:, :, bass.ds(i * 1536 + s * 256, 256)], i)
            for s in range(SLOTS):
                loads[s] += MOD_TURNS

        def tensor_start(pe):
            for s in range(SLOTS):
                pe.sem_inc(S(f"slot{s}_free"), 1)
            pe.wait_ge(S("params_in"), PARAMS * 16)
            pe.wait_ge(S("consts_set"), 2)
            for t in range(DT):
                mm = pe.transpose(ps[:, 0, t * 9:t * 9 + 9], cin[:, t * 128:(t + 1) * 128], ident[0:9, 0:9])
            mm.then_inc(S("start_ps"), 1)
            pe.transpose(ps[:, 1, 0:R_END], prow[:, :], ident[0:R_END, 0:R_END])
            pe.transpose(ps[:, 1, 128:128 + 96], crow[:, :], ident[0:96, 0:96]).then_inc(S("start_ps"), 1)
            pe.wait_ge(S("srow_in"), 5 * 16)
            for g, (r, n) in enumerate(SGRP):
                mm = pe.transpose(ps[:, 2 + g // 4, (g % 4) * 120:(g % 4) * 120 + n], srow[0:n, g, :], ident[0:n, 0:n])
            mm.then_inc(S("start_ps"), 1)
            pe.wait_ge(S("x_in"), 5 * 16)
            for d in range(DT):
                if d >= 4:
                    pe.wait_ge(S("xT_copied"), d - 3)
                for t in range(NC):
                    mm = pe.transpose(ps[:, 4 + d % 4, t * 128:(t + 1) * 128], xin[:, t, d * 128:(d + 1) * 128], ident)
                mm.then_inc(S("xT"), 1)
            pe.wait_ge(S("cs_silu"), 1)
            for d in range(DT):
                mm = pe.transpose(ps[:, 0, 128 + d * NS:128 + (d + 1) * NS], xin[0:NS, NC, d * 128:(d + 1) * 128], ident[0:NS, 0:NS])
            mm.then_inc(S("xT"), 1)
            pe.wait_ge(S("rows_copied"), 2)
            pe.wait_ge(S("xT_copied"), DT)
            with pe.Fori(0, MOD_TURNS) as i:
                pe.wait_ge(S("mod_copied"), i + 1)
                for s in range(SLOTS):
                    slot_ready(pe, s, i)
                    for k in range(DT):
                        mm = pe.matmul(ps[0:1 + NS, 4 + s // 2, (s % 2) * 256:(s % 2) * 256 + 256], csT[:, k, :], W[:, s, k, :],
                                       start=(k == 0), stop=(k == DT - 1))
                    mm.then_inc(S(f"slot{s}_free"), 1)
                pe.wait_ge(S("mod_rows"), i + 1)
                pe.sem_inc(S("pad"), 1)
                for t in range(12):
                    mm = pe.transpose(ps[:, 1, t * 9:t * 9 + 9], mrow[:, t * 128:(t + 1) * 128], ident[0:1 + NS, 0:1 + NS])
                mm.then_inc(S("mod_T"), 1)
            for s in range(SLOTS):
                fulls[s] += MOD_TURNS

        def scalar_start(act):
            act.wait_ge(S("start_ps"), 1)
            act.activation(csT[:, :, :], ps[:, 0, 0:72].rearrange("p (t b) -> p t b", t=DT), ACT.Silu).then_inc(S("cs_silu"), 1)
            for d in range(DT):
                act.wait_ge(S("xT"), d + 1)
                act.copy(XT[:, d, 0:P], ps[:, 4 + d % 4, :]).then_inc(S("xT_copied"), 1)
            act.wait_ge(S("xT"), DT + 1)
            act.copy(XT[:, :, P:T], ps[:, 0, 128:128 + DT * NS].rearrange("p (d b) -> p d b", d=DT)).then_inc(S("xT_copied"), 1)
            with act.Fori(0, MOD_TURNS) as i:
                act.wait_ge(S("slot5_free"), i + 2)
                act.copy(mrow, ps[0:1 + NS, 4:7, :].rearrange("p a n -> p (a n)")).then_inc(S("mod_rows"), 1)

        def vector_start(dve):
            dve.memset(ones[:, :], 1.0).then_inc(S("consts_set"), 1)
            dve.memset(eps[:, :], EPS).then_inc(S("consts_set"), 1)
            dve.wait_ge(S("start_ps"), 2)
            dve.tensor_copy(colsT[:, :], ps[:, 1, 0:R_END]).then_inc(S("rows_copied"), 1)
            dve.tensor_copy(convT[:, :, :], ps[:, 1, 128:224].rearrange("p (i t) -> p i t", i=CONV)).then_inc(S("rows_copied"), 1)
            dve.wait_ge(S("rows_copied"), 2)
            for s in range(3):
                dve.tensor_copy(hcols[:, :, s * 4:s * 4 + 4], convT[:, :, s * H:(s + 1) * H].rearrange("p i h -> p h i"))
            dve.wait_ge(S("start_ps"), 3)
            for g, (r, n) in enumerate(SGRP):
                for q in range(n // CT):
                    b, i = divmod((r + q * CT) // CT, 3)
                    o = (g % 4) * 120 + q * CT
                    dve.tensor_copy(cst[:, :, b, i], ps[:, 2 + g // 4, o:o + CT])
            dve.sem_inc(S("mod_copied"), 1)
            with dve.Fori(0, MOD_TURNS) as i:
                dve.wait_ge(S("mod_T"), i + 1)
                dve.tensor_tensor(modT[:, bass.ds(i * 12, 12), :], ps[:, 1, 0:108].rearrange("p (t b) -> p t b", t=12),
                                  colsT[:, bass.ds(i * 12, 12)].unsqueeze(2).to_broadcast([128, 12, 9]), ALU.add)\
                   .then_inc(S("mod_copied"), 1)

        def tensor_norm(pe, z, free):
            for sem, value in free:
                pe.wait_ge(S(sem), value)
            for d in range(DT):
                pe.wait_ge(S("norm_sq"), z * DT + d + 1)
                for a in range(2):
                    mm = pe.matmul(ps[:, a, 0:TH], ones[:, :], sqn[:, d % 2, a * TH:(a + 1) * TH],
                                   start=(d == 0), stop=(d == DT - 1))
                mm.then_inc(S("norm_sum"), 1)

        def scalar_norm(act, z, ready):
            for sem, value in ready:
                act.wait_ge(S(sem), value)
            for d in range(DT):
                if d >= 2:
                    act.wait_ge(S("norm_sum"), z * DT + d - 1)
                act.activation(sqn[:, d % 2, :], XT[:, d, :], ACT.Square).then_inc(S("norm_sq"), 1)
            act.wait_ge(S("norm_sum"), (z + 1) * DT)
            act.activation(rsn[:, :, :], pair(0), ACT.Ln, bias=eps[:, :], scale=1.0 / D).then_inc(S("norm_rms"), 1)
            act.wait_ge(S("norm_rms"), 2 * z + 1)
            act.activation(rsn[:, :, :], rsn[:, :, :], ACT.Exp, scale=-0.5).then_inc(S("norm_rms"), 1)

        def vector_norm(dve, z, r_w, part):
            if part is not None:
                for d in range(DT):
                    ins = dve.tensor_scalar(amod[:, d, :], modT[:, part * 8 + 8 + d, :], 1.0, colsT[:, r_w + d:r_w + d + 1],
                                            ALU.add, ALU.mult)
                link(dve, ins)
            dve.wait_ge(S("norm_rms"), 2 * z + 2)
            flat = rsn[:, :, :].rearrange("p a n -> p (a n)")
            if part is None:
                for d in range(DT):
                    ins = dve.scalar_tensor_tensor(HT[:, d, :], XT[:, d, :], colsT[:, r_w + d:r_w + d + 1], flat, ALU.mult, ALU.mult)
                ins.then_inc(S("norm_done"), 1)
                return
            for d in range(DT):
                ins = dve.tensor_tensor(HT[:, d, :], XT[:, d, :], flat, ALU.mult)
            link(dve, ins)
            for d in range(DT):
                dve.tensor_scalar(HT[:, d, 0:P], HT[:, d, 0:P], amod[:, d, 0:1], modT[:, part * 8 + d, 0:1], ALU.mult, ALU.add)\
                   .then_inc(S("norm_done"), 1)
            link(dve, dve.tensor_tensor(HT[:, :, P:T], HT[:, :, P:T], amod[:, :, 1:9], ALU.mult))
            dve.tensor_tensor(HT[:, :, P:T], HT[:, :, P:T], modT[:, part * 8:part * 8 + 8, 1:9], ALU.add).then_inc(S("norm_done"), 1)

        NORMED = DT + 1

        X_B, X_A, X_T, X_G, X_BETA, X_GC, X_EGC, X_KE = range(8)

        def tensor_gates(pe):
            pe.wait_ge(S("norm_done"), NORMED)
            for t in range(NC + 1):
                n = 128 if t < NC else NS
                for k in range(DT):
                    mm = pe.matmul(ps[0:n, 2, t * 16:t * 16 + 16], HT[:, k, t * 128:t * 128 + n], wba[:, k, :],
                                   start=(k == 0), stop=(k == DT - 1))
            mm.then_inc(S("gate_ps"), 1)
            pe.wait_ge(S("g_ready"), 2)
            g = tok[:, X_G, 0:NC, :].rearrange("p t h -> p (t h)")
            pe.matmul(ps[:, 3, 0:32], incl, g, start=True, stop=True)
            pe.matmul(ps[:, 3, 64:96], ones[:, :], g, start=True, stop=True).then_inc(S("gate_ps"), 1)
            for t in range(NC):
                pe.matmul(ps[0:H, 4, t * 128:(t + 1) * 128], tok[:, X_G, t, :], incl, start=True, stop=True)
                pe.matmul(ps[0:H, 6, t * 128:(t + 1) * 128], tok[:, X_BETA, t, :], ident, start=True, stop=True)
            pe.matmul(ps[0:H, 5, 0:NS], tok[0:NS, X_G, NC, :], ident[0:NS, 0:NS], start=True, stop=True)
            pe.matmul(ps[0:H, 5, 8:8 + NS], tok[0:NS, X_BETA, NC, :], ident[0:NS, 0:NS], start=True, stop=True).then_inc(S("gate_ps"), 1)

        def scalar_gates(act):
            act.wait_ge(S("ba_copied"), 4)
            act.activation(tok[:, X_T, :, :], tok[:, X_B, :, :], ACT.Exp, scale=-1.0).then_inc(S("gate_fn"), 1)
            act.activation(tok[:, 9, :, :], tok[:, 8, :, :], ACT.Exp, scale=-1.0).then_inc(S("gate_fn"), 1)
            act.wait_ge(S("params_in"), PARAMS * 16)
            act.activation(hd_bc[:, 0, :], hd_bc[:, 0, :], ACT.Exp).then_inc(S("gate_fn"), 1)
            act.wait_ge(S("gate_fn"), 2)
            act.activation(tok[:, 10, :, :], tok[:, 9, :, :], ACT.Ln, bias=1.0).then_inc(S("gate_fn"), 1)
            act.wait_ge(S("gc_copied"), 2)
            act.activation(tok[:, X_EGC, 0:NC, :], tok[:, X_GC, 0:NC, :], ACT.Exp).then_inc(S("gate_fn"), 1)
            act.activation(tok[:, X_KE, 0:NC, :], tok[:, X_KE, 0:NC, :], ACT.Exp).then_inc(S("gate_fn"), 1)
            act.wait_ge(S("gate_ps"), 3)
            act.copy(rows[:, 0, 0:P], ps[0:H, 4, :]).then_inc(S("rows_done"), 1)
            act.copy(rows[:, 1, 0:P], ps[0:H, 6, :]).then_inc(S("rows_done"), 1)
            act.copy(rows[:, :, P:T], ps[0:H, 5, 0:16].rearrange("p (a b) -> p a b", a=2)).then_inc(S("rows_done"), 1)

        def vector_gates(dve):
            link(dve, dve.memset(tok[:, :, NC, :], 0.0))
            dve.wait_ge(S("gate_ps"), 1)
            dve.wait_ge(S("params_in"), PARAMS * 16)
            v = ps[:, 2, 0:64].rearrange("p (t c) -> p t c", t=NC)
            dt = hd_bc[:, 1, :]
            dve.tensor_copy(tok[:, X_B, 0:NC, :], v[:, :, 0:8]).then_inc(S("ba_copied"), 1)
            dve.tensor_copy(tok[0:NS, X_B, NC, :], ps[0:NS, 2, 64:72]).then_inc(S("ba_copied"), 1)
            dve.tensor_tensor(tok[:, X_A, 0:NC, :], v[:, :, 8:16], dt.unsqueeze(1).to_broadcast([128, NC, H]), ALU.add)
            link(dve, dve.tensor_tensor(tok[0:NS, X_A, NC, :], ps[0:NS, 2, 72:80], dt[0:NS, :], ALU.add))
            dve.scalar_tensor_tensor(tok[:, 8, :, :], tok[:, X_A, :, :], -1.0, tok[:, X_A, :, :], ALU.mult, ALU.max).then_inc(S("ba_copied"), 1)
            dve.tensor_scalar(tok[:, 11, :, :], tok[:, X_A, :, :], 0.0, None, ALU.max).then_inc(S("ba_copied"), 1)
            dve.wait_ge(S("gate_fn"), 1)
            link(dve, dve.tensor_scalar(tok[:, X_T, :, :], tok[:, X_T, :, :], 1.0, None, ALU.add))
            dve.reciprocal(tok[:, X_BETA, :, :], tok[:, X_T, :, :]).then_inc(S("g_ready"), 1)
            dve.wait_ge(S("gate_fn"), 4)
            link(dve, dve.tensor_tensor(tok[:, 10, :, :], tok[:, 10, :, :], tok[:, 11, :, :], ALU.add))
            dve.wait_ge(S("gate_fn"), 3)
            dve.scalar_tensor_tensor(tok[:, X_G, :, :], tok[:, 10, :, :], -1.0,
                                     hd_bc[:, 0, :].unsqueeze(1).to_broadcast([128, NC + 1, H]), ALU.mult, ALU.mult).then_inc(S("g_ready"), 1)
            dve.wait_ge(S("gate_ps"), 2)
            dve.tensor_copy(tok[:, X_GC, 0:NC, :], ps[:, 3, 0:32].rearrange("p (t h) -> p t h", t=NC)).then_inc(S("gc_copied"), 1)
            dve.wait_ge(S("gc_copied"), 1)
            dve.tensor_tensor(tok[:, X_KE, 0:NC, :], ps[:, 3, 64:96].rearrange("p (t h) -> p t h", t=NC), tok[:, X_GC, 0:NC, :],
                              ALU.subtract).then_inc(S("gc_copied"), 1)
            dve.wait_ge(S("gate_fn"), 6)
            v = lambda x: tok[:, x, 0:NC, :].rearrange("p t h -> p h t")
            dve.tensor_copy(hcols[:, :, H_GC:H_GC + NC], v(X_GC))
            dve.tensor_copy(hcols[:, :, H_BETA:H_BETA + NC], v(X_BETA))
            dve.tensor_copy(hcols[:, :, H_KEND:H_KEND + NC], v(X_KE))
            link(dve, dve.tensor_tensor(hcols[:, :, H_BEXP:H_BEXP + NC], v(X_BETA), v(X_EGC), ALU.mult))

        st3 = ExitStack()
        raw = sb("raw", [128, 3, CONV - 1 + T], st3)
        cacc = sb("cacc", [128, 3, T], st3)
        sacc = sb("sacc", [128, 3, NS, CONV], st3)
        sqk = sb("sqk", [128, 4, TH], st3)
        qk = sb("qk", [128, 2, T], st3)
        zs = sb("zs", [128, T], st3)
        rb = sb("rb", [128, 2, T], st3)
        eg = sb("eg", [128, T], st3)
        qd = sb("qd", [128, T], st3)
        dec = sb("dec", [128, NC, C], st3)
        bdec = sb("bdec", [128, NC, C], st3)
        qkd = sb("qkd", [128, NC, C], st3)
        at = sb("at", [128, NC, C], st3)
        atl = sb("atl", [128, LEVELS, NC, C], st3)
        Tm = sb("Tm", [128, NC, C], st3)
        Um = sb("Um", [128, NC, C], st3)
        Pm = sb("Pm", [128, NC, C], st3)
        kend = sb("kend", [128, NC, DK], st3)
        kbg = sb("kbg", [128, NC, DK], st3)
        vb = sb("vb", [128, NC, DK], st3)
        nwT = sb("nwT", [128, NC, C], st3)
        vnew = sb("vnew", [128, NC, DK], st3)
        Sc = sb("Sc", [128, NC, DK], st3)
        hc = sb("hc", [128, H_COLS], st3)
        sst = sb("sst", [128, NS, DK], st3)
        stmp = sb("stmp", [128, NS, DK], st3)
        svd = sb("svd", [128, NS, DK], st3)
        snew = sb("snew", [128, NS, DK], st3)
        nka = sb("nka", [128, 2, NS], st3)
        oT = sb("oT", [128, T], st3)
        osq = sb("osq", [128, 2, TH], st3)
        tail = sb("tail", [11, 3, DK], st3)
        zero28 = sb("zero28", [128, H_COLS], st3)
        st3.close()
        D_PS, D_FN, D_PRE = 8, 7, 5
        D_PS_TAIL, D_PS_KK, D_PS_KVT, D_PS_A0, D_PS_WT, D_PS_U, D_PS_O, D_PS_OSUM = range(1, D_PS + 1)
        D_FN_TAIL_DONE, D_FN_EG, D_FN_ZS, D_FN_NWT, D_FN_OSQ, D_FN_OLN, D_FN_ORMS = range(1, D_FN + 1)
        D_PRE_SILU, D_PRE_SQK, D_PRE_LN, D_PRE_UNIT, D_PRE_DEC = range(1, D_PRE + 1)
        conv_p_d = A["out_conv_p"][0, 0].rearrange("i (s h p) -> i h s p", s=3, h=H)
        conv_s_d = A["out_conv_s"][0, :, 2].rearrange("b (s h p) -> b h s p", s=3, h=H)
        st_d = A["state_delta"][0]

        def slot_cols(s):
            return W[:, s].rearrange("p k n -> p (k n)").rearrange("p (m k n) -> p m k n", m=2, k=8)

        def sync_delta(sp):
            sp.wait_ge(S("rows_done"), 3)
            sp.dma_start(rows_d, rows[:, :, :]).then_inc(S("rows_out"), 16)
            sp.wait_ge(S("rows_out"), 16)
            sync_weights(sp, 0)
            sp.wait_ge(S("d_go"), 1)
            sync_rows(sp, 0)
            with sp.Fori(0, H - 1) as h:
                sync_weights(sp, h + 1)
                sync_head(sp, h, False)
            sync_head(sp, H - 1, True)
            for s in (0, 1):
                loads[s] += H
            sp.dma_start(A["out_conv_s"][0, :, 0:2], A["state_conv"][0, :, 1:3]).then_inc(S("conv_out"), 16)

        def sync_weights(sp, h):
            for s, cols in ((0, (Q_A, K_A)), (1, (V_A, Z_A))):
                sp.wait_ge(S(f"slot{s}_free"), loads[s] + h + 1)
                sp.sem_inc(S("pad"), 1)
                for m in range(2):
                    sp.dma_start(slot_cols(s)[:, m], w_in[:, :, bass.ds(h * 128 + cols[m], 128)]).then_inc(S(f"dslot{s}_full"), 16)

        def sync_rows(sp, h):
            sp.dma_start(rb[:, :, :], rows_d[bass.ds(h, 1)].rearrange("h a t -> (h a t)").partition_broadcast(128)
                         .rearrange("p (a t) -> p a t", a=2)).then_inc(S("rb_in"), 16)

        def sync_head(sp, h, last):
            n = h + 1
            sp.wait_ge(S("d_go"), h + 1)
            sp.dma_start(sst[:, :, :], st_d[:, bass.ds(h, 1)].rearrange("b h k v -> k (b h) v")).then_inc(S("sst_in"), 16)
            sp.wait_ge(S("d_fn"), h * D_FN + D_FN_TAIL_DONE)
            sp.dma_start(conv_p_d[:, bass.ds(h, 1)].rearrange("i h s p -> (i h) s p"), tail[0:3, :, :]).then_inc(S("d_stored"), 16)
            sp.dma_start(conv_s_d[:, bass.ds(h, 1)].rearrange("b h s p -> (b h) s p"), tail[3:11, :, :]).then_inc(S("d_stored"), 16)
            if not last:
                sp.wait_ge(S("s_ks"), n)
                sp.sem_inc(S("pad"), 1)
                sp.wait_ge(S("d_fn"), h * D_FN + D_FN_EG)
                sync_rows(sp, h + 1)
            sp.wait_ge(S("snew"), n)
            sp.dma_start(A["out_delta_s"][0, :, bass.ds(h, 1)].rearrange("b h k v -> k (b h) v"), snew[:, :, :]).then_inc(S("d_stored"), 16)
            sp.wait_ge(S("d_state"), (h + 1) * NC)
            sp.dma_start(A["out_delta_p"][0, 0, bass.ds(h, 1)].rearrange("h k v -> k (h v)"), Sc[:, NC - 1, :]).then_inc(S("d_stored"), 16)
            sp.wait_ge(S("d_stored"), (h + 1) * 64)
            sp.sem_inc(S("pad"), 1)

        def project(pe, bank, w):
            return project_steps(pe, bank, w, 0, 2 * DT)

        def project_steps(pe, bank, w, first, end):
            for i in range(first, end):
                k, a = divmod(i, 2)
                mm = pe.matmul(ps[:, bank + a, 0:TH], w[:, k, :], HT[:, k, a * TH:(a + 1) * TH], start=(k == 0), stop=(k == DT - 1))
            return mm

        def next_piece(pe, h, g):
            n = h + 1
            x, third = divmod(g, 3)
            s, m = divmod(x, 2)
            if third == 0:
                if m == 0:
                    pe.wait_ge(S(f"dslot{s}_full"), (n + 1) * 32)
                if x == 0:
                    pe.wait_ge(S("d_at"), n * 2)
                elif x == 1:
                    pe.wait_ge(S("d_kv"), n * 3)
                else:
                    pe.wait_ge(S("d_raw"), n * 4 + x - 1)
            mm = project_steps(pe, (4, 6)[m], slot_cols(s)[:, m], (0, 6, 11)[third], (6, 11, 16)[third])
            if third == 2:
                mm.then_inc(S(f"slot{s}_free") if m else S("d_proj"), 1)

        def tensor_delta(pe):
            pe.wait_ge(S("rows_done"), 3)
            pe.wait_ge(S("d_go"), 1)
            for s in (0, 1):
                pe.wait_ge(S(f"dslot{s}_full"), 32)
                w = slot_cols(s)
                project(pe, 4 * s, w[:, 0]).then_inc(S("d_proj"), 1)
                project(pe, 4 * s + 2, w[:, 1]).then_inc(S(f"slot{s}_free"), 1)
            tensor_sums(pe, 0)
            with pe.Fori(0, H - 1) as h:
                tensor_head(pe, h, False)
            tensor_head(pe, H - 1, True)

        def tensor_sums(pe, h):
            pe.wait_ge(S("d_pre"), h * D_PRE + D_PRE_SQK)
            for c in range(4):
                mm = pe.matmul(ps[:, c, 0:TH], ones[:, :], sqk[:, c, :], start=True, stop=True)
            mm.then_inc(S("d_ssum"), 1)

        def tensor_head(pe, h, last):
            n = h + 1
            pe.wait_ge(S("d_go"), n)
            pe.wait_ge(S("d_raw"), n * 4)
            for s in range(3):
                mm = pe.transpose(ps[0:11, 6, s * 128:(s + 1) * 128], raw[:, s, 3 + P - 3:3 + T], ident)
            mm.then_inc(S("d_ps"), 1)
            pe.wait_ge(S("d_qk"), n)
            for c in range(NC):
                kc = qk[:, 1, c * C:(c + 1) * C]
                pe.matmul(ps[:, 4, c * C:(c + 1) * C], kc, kc, start=True, stop=True)
                mm = pe.matmul(ps[:, 5, c * C:(c + 1) * C], kc, qk[:, 0, c * C:(c + 1) * C], start=True, stop=True)
            mm.then_inc(S("d_ps"), 1)
            pe.wait_ge(S("d_fn"), h * D_FN + D_FN_TAIL_DONE)
            for c in range(NC):
                pe.transpose(ps[:, 6, c * C:(c + 1) * C], qk[:, 1, c * C:(c + 1) * C], ident)
                mm = pe.transpose(ps[:, 7, c * C:(c + 1) * C], cacc[:, 2, c * C:(c + 1) * C], ident)
            mm.then_inc(S("d_ps"), 1)
            pe.wait_ge(S("d_atl"), h * LEVELS + 1)
            for c in range(NC):
                mm = pe.transpose(ps[:, 0, c * C:(c + 1) * C], atl[:, 0, c, :], ident)
            mm.then_inc(S("d_ps"), 1)
            for l in range(1, LEVELS):
                pe.wait_ge(S("d_atl"), h * LEVELS + l + 1)
                pe.wait_ge(S("d_T"), h * (LEVELS - 1) + l)
                for c in range(NC):
                    mm = pe.matmul(ps[:, 1, c * C:(c + 1) * C], atl[:, l, c, :], Tm[:, c, :], start=True, stop=True)
                mm.then_inc(S("d_P"), 1)
                if not last:
                    next_piece(pe, h, 2 * l - 2)
                pe.wait_ge(S("d_Pcopy"), h * (LEVELS - 1) + l)
                pe.wait_ge(S("d_U"), h * LEVELS + l)
                for c in range(NC):
                    mm = pe.matmul(ps[:, 2, c * C:(c + 1) * C], Pm[:, c, :], Um[:, c, :], start=True, stop=True)
                mm.then_inc(S("d_dU"), 1)
                if l < LEVELS - 1:
                    for c in range(NC):
                        mm = pe.matmul(ps[:, 3, c * C:(c + 1) * C], Um[:, c, :], Pm[:, c, :], start=True, stop=True)
                    mm.then_inc(S("d_dT"), 1)
                if not last:
                    next_piece(pe, h, 2 * l - 1)
            pe.wait_ge(S("d_U"), (h + 1) * LEVELS)
            pe.wait_ge(S("d_kv"), n * 3)
            for c in range(NC):
                mm = pe.matmul(ps[:, 0, c * C:(c + 1) * C], kbg[:, c, :], Um[:, c, :], start=True, stop=True)
            mm.then_inc(S("d_ps"), 1)
            pe.wait_ge(S("s_vd"), n)
            pe.wait_ge(S("s_ks"), n)
            for a in range(2):
                pe.matmul(ps[:, 1 + a, :], ones[:, :], svd[:, 4 * a:4 * a + 4, :].rearrange("p b v -> p (b v)"), start=True, stop=False)
                mm = pe.matmul(ps[:, 1 + a, :], ones[:, :], stmp[:, 4 * a:4 * a + 4, :].rearrange("p b v -> p (b v)"), start=False, stop=True)
            mm.then_inc(S("d_ps"), 1)
            pe.wait_ge(S("d_fn"), h * D_FN + D_FN_NWT)
            if last:
                pe.wait_ge(S("d_at"), n * 2)
            else:
                pe.wait_ge(S("d_raw"), n * 4 + 4)
            for c in range(NC):
                cc = slice(c * C, (c + 1) * C)
                mm = pe.matmul(ps[:, 4, cc], Um[:, c, :], vb[:, c, :], start=True, stop=(c == 0))
                if c:
                    pe.wait_ge(S("d_state"), h * NC + c)
                    mm = pe.matmul(ps[:, 4, cc], nwT[:, c, :], Sc[:, c - 1, :], start=False, stop=True)
                mm.then_inc(S("d_vn"), 1)
                pe.wait_ge(S("d_vnew"), h * NC + c + 1)
                pe.matmul(ps[:, 5, 0:DK], kend[:, c, :], vnew[:, c, :], start=True, stop=True).then_inc(S("d_ds"), 1)
                if c:
                    pe.matmul(ps[:, 6, cc], Sc[:, c - 1, :], qd[:, cc], start=True, stop=False)
                mm = pe.matmul(ps[:, 6, cc], vnew[:, c, :], qkd[:, c, :], start=(c == 0), stop=True)
            pe.wait_ge(S("snew"), n)
            for b in range(NS):
                mm = pe.matmul(ps[:, 7, b:b + 1], snew[:, b, :], qd[:, P + b:P + b + 1], start=True, stop=True)
            mm.then_inc(S("d_ps"), 1)
            if not last:
                tensor_sums(pe, h + 1)
            pe.wait_ge(S("d_fn"), h * D_FN + D_FN_OSQ)
            pe.wait_ge(S("d_state"), (h + 1) * NC)
            for a in range(2):
                mm = pe.matmul(ps[:, 4 + a, 0:TH], ones[:, :], osq[:, a, :], start=True, stop=True)
            mm.then_inc(S("d_ps"), 1)

        def scalar_delta(act):
            act.wait_ge(S("d_go"), 1)
            for x in range(4):
                scalar_raw(act, 0, x, 2 * x)
            scalar_conv(act, 0)
            scalar_ln(act, 0)
            scalar_unit(act, 0)
            scalar_decay(act, 0)
            with act.Fori(0, H - 1) as h:
                scalar_head(act, h, False)
            scalar_head(act, H - 1, True)

        def scalar_raw(act, h, x, bank):
            if x % 2 == 0:
                act.wait_ge(S("d_proj"), h * 2 + x // 2 + 1)
            else:
                act.wait_ge(S(f"slot{x // 2}_free"), MOD_TURNS + 2 + h)
            dst = raw[:, x, 3:].rearrange("p (a n) -> p a n", a=2) if x < 3 else rsn[:, :, :]
            act.copy(dst, pair(bank)).then_inc(S("d_raw"), 1)

        def scalar_head(act, h, last):
            n = h + 1
            act.wait_ge(S("d_go"), n)
            act.wait_ge(S("d_ps"), h * D_PS + D_PS_TAIL)
            act.wait_ge(S("sst_in"), n * 16)
            act.copy(tail[:, :, :], ps[0:11, 6, 0:384].rearrange("p (s f) -> p s f", s=3)).then_inc(S("d_fn"), 1)
            act.wait_ge(S("rb_in"), n * 16)
            act.activation(eg[:, :], rb[:, 0, :], ACT.Exp).then_inc(S("d_fn"), 1)
            for l in range(1, LEVELS):
                act.wait_ge(S("d_P"), h * (LEVELS - 1) + l)
                act.copy(Pm[:, :, :].rearrange("p c i -> p (c i)"), ps[:, 1, :]).then_inc(S("d_Pcopy"), 1)
                if l == LEVELS - 1:
                    act.activation(halves(zs[:, :]), rsn[:, :, :], ACT.Silu).then_inc(S("d_fn"), 1)
                    act.wait_ge(S("d_fn"), h * D_FN + D_FN_ZS)
                if l in (2, 4, 5, 6) and not last:
                    x = {2: 0, 4: 1, 5: 2, 6: 3}[l]
                    scalar_raw(act, h + 1, x, (4, 6)[x % 2])
            act.wait_ge(S("d_ps"), h * D_PS + D_PS_WT)
            act.mul(nwT[:, :, :].rearrange("p c i -> p (c i)"), ps[:, 0, :], -1.0).then_inc(S("d_fn"), 1)
            if not last:
                scalar_conv(act, h + 1)
            for c in range(NC):
                act.wait_ge(S("d_vn"), h * NC + c + 1)
                act.copy(vnew[:, c, :], ps[:, 4, c * C:(c + 1) * C]).then_inc(S("d_vnew"), 1)
            act.wait_ge(S("d_ps"), h * D_PS + D_PS_O)
            act.copy(oT[:, 0:P], ps[:, 6, :]).then_inc(S("d_oT"), 1)
            act.copy(oT[:, P:T], ps[:, 7, 0:NS]).then_inc(S("d_oT"), 1)
            act.wait_ge(S("d_oT"), n * 2)
            act.activation(osq[:, :, :], halves(oT[:, :]), ACT.Square).then_inc(S("d_fn"), 1)
            if not last:
                scalar_ln(act, h + 1)
            act.wait_ge(S("d_ps"), h * D_PS + D_PS_OSUM)
            act.activation(osq[:, :, :], pair(4), ACT.Ln, bias=eps[:, :], scale=1.0 / DK).then_inc(S("d_fn"), 1)
            act.wait_ge(S("d_fn"), h * D_FN + D_FN_OLN)
            act.activation(osq[:, :, :], osq[:, :, :], ACT.Exp, scale=-0.5).then_inc(S("d_fn"), 1)
            if not last:
                scalar_unit(act, h + 1)
            if not last:
                scalar_decay(act, h + 1)

        def scalar_ln(act, h):
            act.wait_ge(S("d_ssum"), h + 1)
            act.activation(sqk[:, :, :], ps[:, 0:4, 0:TH], ACT.Ln, bias=eps[:, :]).then_inc(S("d_pre"), 1)

        def scalar_unit(act, h):
            act.wait_ge(S("d_pre"), h * D_PRE + D_PRE_LN)
            act.activation(sqk[:, :, :], sqk[:, :, :], ACT.Exp, scale=-0.5).then_inc(S("d_pre"), 1)

        def scalar_conv(act, h):
            act.wait_ge(S("d_conv"), (h + 1) * 13)
            act.activation(cacc[:, :, :], cacc[:, :, :], ACT.Silu).then_inc(S("d_pre"), 1)
            act.wait_ge(S("d_pre"), h * D_PRE + D_PRE_SILU)
            act.activation(sqk[:, :, :].rearrange("p a n -> p (a n)"), cacc[:, 0:2, :].rearrange("p a n -> p (a n)"), ACT.Square)\
               .then_inc(S("d_pre"), 1)

        def scalar_decay(act, h):
            act.wait_ge(S("d_diff"), (h + 1) * NC)
            act.activation(dec[:, :, :], dec[:, :, :], ACT.Exp).then_inc(S("d_pre"), 1)

        D_STEPS = 6

        def vector_delta(dve):
            dve.memset(raw[:, :, 0:3], 0.0)
            link(dve, dve.memset(zero28[:, :], 0.0))
            dve.sem_inc(S("d_go"), 1)
            vector_cols(dve, 0)
            for s in range(3):
                vector_conv(dve, 0, s)
            vector_decay(dve, 0)
            vector_unit(dve, 0)
            with dve.Fori(0, H - 1) as h:
                vector_head(dve, h, False)
            vector_head(dve, H - 1, True)

        def vector_cols(dve, h):
            dve.tensor_tensor(hc[:, :], hcols[:, bass.ds(h, 1), :].rearrange("p h c -> p (h c)"), zero28[:, :], ALU.add).then_inc(S("d_sacc"), 1)
            dve.wait_ge(S("d_sacc"), h * 7 + 1)

        def vector_conv(dve, h, s):
            dve.wait_ge(S("d_raw"), h * 4 + s + 1)
            dve.tensor_scalar(cacc[:, s, 0:P], raw[:, s, 0:P], hc[:, s * 4:s * 4 + 1], None, ALU.mult).then_inc(S("d_conv"), 1)
            dve.tensor_tensor(sacc[:, s, :, 0:3], cst[:, bass.ds(h + s * H, 1), :, :].rearrange("p h b i -> p (h b) i"),
                              hc[:, s * 4:s * 4 + 3].unsqueeze(1).to_broadcast([128, NS, 3]), ALU.mult).then_inc(S("d_sacc"), 1)
            dve.tensor_scalar(sacc[:, s, :, 3], raw[:, s, 3 + P:3 + T], hc[:, s * 4 + 3:s * 4 + 4], None, ALU.mult).then_inc(S("d_sacc"), 1)
            for i in range(1, CONV):
                dve.wait_ge(S("d_conv"), h * 13 + s * 4 + i)
                dve.scalar_tensor_tensor(cacc[:, s, 0:P], raw[:, s, i:i + P], hc[:, s * 4 + i:s * 4 + i + 1], cacc[:, s, 0:P],
                                         ALU.mult, ALU.add).then_inc(S("d_conv"), 1)
            if s == 2:
                dve.wait_ge(S("d_sacc"), (h + 1) * 7)
                dve.tensor_reduce(cacc[:, :, P:T], sacc[:, :, :, :], AX.X, ALU.add).then_inc(S("d_conv"), 1)

        def vector_decay(dve, h):
            dve.wait_ge(S("rb_in"), (h + 1) * 16)
            for c in range(NC):
                dve.tensor_scalar(dec[:, c, :], rb[:, 0, c * C:(c + 1) * C], hc[:, H_GC + c:H_GC + c + 1], 0.0, ALU.subtract, ALU.min)\
                   .then_inc(S("d_diff"), 1)

        def vector_unit(dve, h):
            dve.wait_ge(S("d_pre"), h * D_PRE + D_PRE_UNIT)
            dve.tensor_tensor(qk[:, :, :].rearrange("p a n -> p (a n)"), cacc[:, 0:2, :].rearrange("p a n -> p (a n)"),
                              sqk[:, :, :].rearrange("p a n -> p (a n)"), ALU.mult).then_inc(S("d_qk"), 1)

        def vector_head(dve, h, last):
            n = h + 1
            dve.wait_ge(S("d_qk"), n)
            dve.wait_ge(S("d_pre"), h * D_PRE + D_PRE_DEC)
            dve.tensor_tensor(dec[:, :, :], dec[:, :, :], incl.unsqueeze(1).to_broadcast([128, NC, C]), ALU.mult).then_inc(S("d_step"), 1)
            dve.wait_ge(S("d_step"), h * D_STEPS + 1)
            dve.tensor_tensor(bdec[:, :, :], dec[:, :, :], rb[:, 1, 0:P].rearrange("p (c i) -> p c i", c=NC), ALU.mult).then_inc(S("d_step"), 1)
            dve.wait_ge(S("d_ps"), h * D_PS + D_PS_KK)
            dve.wait_ge(S("d_step"), h * D_STEPS + 2)
            dve.tensor_tensor(at[:, :, :], ps[:, 4, :].rearrange("p (c i) -> p c i", c=NC), bdec[:, :, :], ALU.mult).then_inc(S("d_at"), 1)
            dve.scalar_tensor_tensor(qkd[:, :, :], ps[:, 5, :].rearrange("p (c i) -> p c i", c=NC), DK ** -0.5, dec[:, :, :],
                                     ALU.mult, ALU.mult).then_inc(S("d_at"), 1)
            dve.wait_ge(S("d_at"), n * 2)
            for l in range(2):
                dve.tensor_tensor(atl[:, l], at[:, :, :], lmask[:, l].unsqueeze(1).to_broadcast([128, NC, C]), ALU.mult).then_inc(S("d_atl"), 1)
            eye = ident.unsqueeze(1).to_broadcast([128, NC, C])
            dve.wait_ge(S("d_atl"), h * LEVELS + 1)
            dve.tensor_tensor(Um[:, :, :], eye, atl[:, 0], ALU.subtract).then_inc(S("d_U"), 1)
            dve.wait_ge(S("d_ps"), h * D_PS + D_PS_A0)
            dve.tensor_tensor(Tm[:, :, :], eye, ps[:, 0, :].rearrange("p (c i) -> p c i", c=NC), ALU.subtract).then_inc(S("d_T"), 1)
            for l in range(2, LEVELS):
                dve.tensor_tensor(atl[:, l], at[:, :, :], lmask[:, l].unsqueeze(1).to_broadcast([128, NC, C]), ALU.mult).then_inc(S("d_atl"), 1)
            dve.wait_ge(S("d_fn"), h * D_FN + D_FN_EG)
            dve.scalar_tensor_tensor(qd[:, 0:P], qk[:, 0, 0:P], DK ** -0.5, eg[:, 0:P], ALU.mult, ALU.mult)
            dve.tensor_scalar(qd[:, P:T], qk[:, 0, P:T], DK ** -0.5, None, ALU.mult)
            dve.wait_ge(S("d_ps"), h * D_PS + D_PS_KVT)
            for dst, bank, col in ((kend, 6, H_KEND), (kbg, 6, H_BEXP), (vb, 7, H_BETA)):
                dve.tensor_tensor(dst[:, :, :], ps[:, bank, :].rearrange("p (c k) -> p c k", c=NC),
                                  hc[:, col:col + NC].unsqueeze(2).to_broadcast([128, NC, DK]), ALU.mult).then_inc(S("d_kv"), 1)
            if not last:
                dve.wait_ge(S("d_kv"), n * 3)
                dve.wait_ge(S("s_vd"), n)
                vector_cols(dve, h + 1)
            dve.scalar_tensor_tensor(nka[:, 0, :], qk[:, 1, P:T], -1.0, eg[:, P:T], ALU.mult, ALU.mult).then_inc(S("d_step"), 1)
            dve.tensor_tensor(nka[:, 1, :], qk[:, 1, P:T], rb[:, 1, P:T], ALU.mult).then_inc(S("d_step"), 1)
            dve.wait_ge(S("d_step"), h * D_STEPS + 4)
            dve.wait_ge(S("sst_in"), n * 16)
            dve.tensor_tensor(stmp[:, :, :], sst[:, :, :], nka[:, 0, :].unsqueeze(2).to_broadcast([128, NS, DK]), ALU.mult).then_inc(S("s_ks"), 1)
            for l in range(1, LEVELS):
                dve.wait_ge(S("d_dU"), h * (LEVELS - 1) + l)
                if l < LEVELS - 1:
                    dve.wait_ge(S("d_dT"), h * (LEVELS - 2) + l)
                dve.tensor_tensor(Um[:, :, :], Um[:, :, :], ps[:, 2, :].rearrange("p (c i) -> p c i", c=NC), ALU.subtract).then_inc(S("d_U"), 1)
                if l < LEVELS - 1:
                    dve.tensor_tensor(Tm[:, :, :], Tm[:, :, :], ps[:, 3, :].rearrange("p (c i) -> p c i", c=NC), ALU.subtract).then_inc(S("d_T"), 1)
                if l in (3, 4, 5) and not last:
                    vector_conv(dve, h + 1, l - 3)
            if not last:
                vector_decay(dve, h + 1)
            dve.wait_ge(S("d_ps"), h * D_PS + D_PS_U)
            dve.wait_ge(S("s_decayed"), n)
            dve.tensor_tensor(stmp[:, :, :], ps[:, 1:3, :].rearrange("p a (b v) -> p (a b) v", b=4),
                              nka[:, 1, :].unsqueeze(2).to_broadcast([128, NS, DK]), ALU.mult).then_inc(S("d_step"), 1)
            dve.wait_ge(S("d_step"), h * D_STEPS + 5)
            dve.tensor_tensor(snew[:, :, :], sst[:, :, :], stmp[:, :, :], ALU.add).then_inc(S("snew"), 1)
            for c in range(NC):
                dve.wait_ge(S("d_ds"), h * NC + c + 1)
                if c == 0:
                    dve.tensor_copy(Sc[:, 0, :], ps[:, 5, 0:DK]).then_inc(S("d_state"), 1)
                else:
                    dve.wait_ge(S("d_state"), h * NC + c)
                    dve.scalar_tensor_tensor(Sc[:, c, :], Sc[:, c - 1, :], eg[:, c * C + C - 1:c * C + C], ps[:, 5, 0:DK],
                                             ALU.mult, ALU.add).then_inc(S("d_state"), 1)
            dve.wait_ge(S("d_fn"), h * D_FN + D_FN_ORMS)
            dve.tensor_tensor(halves(oT[:, :]), halves(oT[:, :]), osq[:, :, :], ALU.mult).then_inc(S("d_step"), 1)
            if not last:
                vector_unit(dve, h + 1)
            dve.wait_ge(S("d_step"), h * D_STEPS + 6)
            dve.wait_ge(S("d_fn"), h * D_FN + D_FN_ZS)
            dve.scalar_tensor_tensor(OA[:, bass.ds(h, 1), :].rearrange("p h t -> p (h t)"), oT[:, :], colsT[:, R_DN:R_DN + 1], zs[:, :],
                                     ALU.mult, ALU.mult).then_inc(S("d_go"), 1)

        def pool_delta(pool):
            with pool.Fori(0, H) as h:
                n = h + 1
                pool.wait_ge(S("d_go"), n)
                pool.wait_ge(S("d_pre"), h * D_PRE + D_PRE_SILU)
                pool.tensor_tensor(svd[:, :, :], ident.unsqueeze(1).to_broadcast([128, NS, DK]),
                                   cacc[:, 2, P:T].unsqueeze(2).to_broadcast([128, NS, DK]), ALU.mult).then_inc(S("s_vd"), 1)
                pool.wait_ge(S("s_ks"), n)
                pool.wait_ge(S("d_fn"), h * D_FN + D_FN_EG)
                pool.tensor_tensor(sst[:, :, :], sst[:, :, :], eg[:, P:T].unsqueeze(2).to_broadcast([128, NS, DK]), ALU.mult).then_inc(S("s_decayed"), 1)

        OB = sb("OB", [128, RH * 4, T])
        st4 = ExitStack()
        rot = sqn
        rt = sb("rt", [128, 4, T], st4)
        ON = sb("ON", [128, NC + 1, RV], st4)
        flat_on = ON[:, :, :].rearrange("p t v -> p (t v)")
        qr = flat_on[:, 0:2 * T].rearrange("p (a t) -> p a t", a=2)
        kr = flat_on[:, 2 * T:4 * T].rearrange("p (a t) -> p a t", a=2)
        V = sb("V", [128, NC + 1, RV], st4)
        SG = sb("SG", [128, 4, T], st4)
        dm = sb("dm", [128, P], st4)
        PT = sb("PT", [128, 1280], st4)
        PO = (0, 512, 896, 1152)
        kd = PT[:, 0:NC * RK].rearrange("p (t k) -> p t k", t=NC)
        rst = sb("rst", [128, 2, 2, RV], st4)
        rnew = sb("rnew", [128, 2, 2, RV], st4)
        rc = sb("rc", [128, 8], st4)
        bn6 = sb("bn6", [128, NC + 1, 6], st4)
        mv = sb("mv", [128, NC + 1, 2], st4)
        sd = sb("sd", [128, NC + 1], st4)
        qdg = sb("qdg", [128, 2, NS, NS], st4)
        gnc = sb("gnc", [128, 2, 4], st4)
        zero4 = sb("zero4", [128, 4], st4)
        st4.close()
        kdg = rt[0:NS, :, :].rearrange("p a t -> p (a t)")[:, 0:NS * RK].rearrange("p (b k) -> p b k", b=NS)
        ret_p_d = A["out_ret_p"][0, 0].rearrange("h (a p) v -> p h a v", p=128)
        ret_s_d = A["out_ret_s"][0].rearrange("b h (a p) v -> p b h a v", p=128)
        ret_i_d = A["state_ret"][0].rearrange("b h (a p) v -> p b h a v", p=128)

        def delta_over(eng):
            eng.wait_ge(S("d_go"), H + 1)
            eng.wait_ge(S("d_stored"), H * 64)

        def sync_ret(sp):
            sync_ret_weights(sp, 0)
            delta_over(sp)
            sp.wait_ge(S("norm_done"), NORMED)
            sp.dma_start(rot[:, :, :], A["rot"]).then_inc(S("tables_in"), 16)
            with sp.Fori(0, RH - 1) as h:
                sync_ret_tables(sp, h)
                sync_ret_weights(sp, h + 1)
            sync_ret_tables(sp, RH - 1)
            for s in range(SLOTS):
                loads[s] += RH

        def sync_ret_weights(sp, h):
            for s, col, w in ((0, Q_B, RK), (1, K_B, RK), (2, V_B, RV), (3, V_B + 256, RV), (4, G_B, RV), (5, G_B + 256, RV)):
                load_slot(sp, s, w_in[:, :, bass.ds(h * w + col, 256)], h)

        def sync_ret_tables(sp, h):
            sp.wait_ge(S("r_go"), h + 1)
            sp.dma_start(dm[:, :], A["dmat"][bass.ds(h, 1)].rearrange("h p i -> p (h i)")).then_inc(S("r_tab"), 16)
            sp.dma_start(rc[:, :], A["rcol"][bass.ds(h, 1)].rearrange("h p i -> p (h i)")).then_inc(S("r_tab"), 16)

        def tensor_ret(pe):
            pe.wait_ge(S("r_go"), 1)
            with pe.Fori(0, RH) as h:
                n = h + 1
                pe.wait_ge(S("r_aff"), h * 8 + 1)
                for s in (0, 1):
                    slot_ready(pe, s, h)
                    project(pe, 4 * s, W[:, s, :, 0:128])
                    project(pe, 4 * s + 2, W[:, s, :, 128:256]).then_inc(S(f"slot{s}_free"), 1)
                for s in (2, 3):
                    slot_ready(pe, s, h)
                    for t in range(NC + 1):
                        if s == 2 and t == 0:
                            pe.wait_ge(S("r_rt"), h * 8 + 4)
                        if s == 2 and t == NC:
                            pe.wait_ge(S("r_rt"), h * 8 + 8)
                        m = 128 if t < NC else NS
                        for k in range(DT):
                            mm = pe.matmul(ps[0:m, t, (s - 2) * 256:(s - 1) * 256], HT[:, k, t * 128:t * 128 + m], W[:, s, k, :],
                                           start=(k == 0), stop=(k == DT - 1))
                    mm.then_inc(S(f"slot{s}_free"), 1)
                for f in range(4):
                    s = 4 + f // 2
                    if f % 2 == 0:
                        slot_ready(pe, s, h)
                    if f in (1, 2):
                        pe.wait_ge(S("r_V"), h * 5 + 2 * f)
                    if f == 3:
                        pe.wait_ge(S("r_sg"), h * 4 + 1)
                    mm = project(pe, (6, 0, 2, 6)[f], W[:, s, :, (f % 2) * 128:(f % 2) * 128 + 128])
                    if f % 2 == 0:
                        mm.then_inc(S("r_g"), 1)
                    else:
                        mm.then_inc(S(f"slot{s}_free"), 1)
                pe.wait_ge(S("r_qkr"), n * 4)
                pe.wait_ge(S("r_V"), n * 5)
                for t in range(NC):
                    if t == 2:
                        pe.wait_ge(S("r_sg"), h * 4 + 2)
                    for a in range(2):
                        mm = pe.matmul(ps[:, (4, 5, 0, 1)[t], 0:P - t * 128], kr[:, a, t * 128:(t + 1) * 128], qr[:, a, t * 128:P],
                                       start=(a == 0), stop=(a == 1))
                    mm.then_inc(S("r_s"), 1)
                for i in range(NC):
                    pe.wait_ge(S("r_pt"), h * 4 + i + 1)
                    pe.wait_ge(S("r_sg"), h * 4 + (3 if i < 2 else 4))
                    for j in range(i + 1):
                        o = PO[j] + (i - j) * 128
                        mm = pe.matmul(ps[:, (2, 3, 6, 7)[i], :], PT[:, o:o + 128], V[:, j, :], start=(j == 0), stop=(j == i))
                    mm.then_inc(S("r_o"), 1)
                for t in range(NC):
                    for a in range(2):
                        pe.transpose(ps[:, t // 2, (t % 2) * 256 + a * 128:(t % 2) * 256 + (a + 1) * 128], kr[:, a, t * 128:(t + 1) * 128], ident)
                for a in range(2):
                    mm = pe.transpose(ps[0:NS, 4, a * 128:(a + 1) * 128], kr[:, a, P:T], ident)
                mm.then_inc(S("r_ks"), 1)
                pe.wait_ge(S("r_kd"), n * 2)
                for a in range(2):
                    for t in range(NC):
                        mm = pe.matmul(ps[:, 4 + a, :], kd[:, t, a * 128:(a + 1) * 128], V[:, t, :], start=(t == 0), stop=(t == NC - 1))
                mm.then_inc(S("r_ks"), 1)
                pe.wait_ge(S("r_on"), h * 5 + 4)
                for b in range(NS):
                    if b == 1:
                        pe.wait_ge(S("r_sfc"), n)
                    if b >= 2:
                        pe.wait_ge(S("r_new"), h * NS + b - 1)
                    for a in range(2):
                        mm = pe.matmul(ps[:, (b % 2) * 4 + a, :], kdg[:, b, a * 128:(a + 1) * 128], V[0:NS, NC, :], start=True, stop=True)
                    mm.then_inc(S("r_kv"), 1)
                    if b >= 1:
                        tensor_ret_o(pe, h, b - 1)
                tensor_ret_o(pe, h, NS - 1)
                for f in range(4):
                    if f == 3:
                        pe.wait_ge(S("r_on"), n * 5)
                    for i in range(NC):
                        mm = pe.transpose(ps[:, (2, 3, 7, 0)[f], i * 128:(i + 1) * 128], ON[:, i, f * 128:(f + 1) * 128], ident)
                    mm.then_inc(S("r_onT"), 1)
                for f in range(4):
                    mm = pe.transpose(ps[:, 1, f * NS:(f + 1) * NS], ON[0:NS, NC, f * 128:(f + 1) * 128], ident[0:NS, 0:NS])
                mm.then_inc(S("r_onT"), 1)
            for s in range(SLOTS):
                fulls[s] += RH

        def tensor_ret_o(pe, h, b):
            pe.wait_ge(S("r_new"), h * NS + b + 1)
            for a in range(2):
                mm = pe.matmul(ps[0:NS, 6, :], qdg[:, a, b, :], rnew[:, b % 2, a, :], start=(b == 0 and a == 0), stop=(b == NS - 1 and a == 1))
            mm.then_inc(S("r_os"), 1)

        def scalar_ret(act):
            delta_over(act)
            act.sem_inc(S("r_aff"), 1)
            with act.Fori(0, RH) as h:
                n = h + 1
                hs = bass.ds(h, 1)
                act.wait_ge(S("r_go"), n)
                for b in range(2):
                    act.dma_start(rst[:, b], ret_i_d[:, b, hs].rearrange("p h a v -> p (h a) v")).then_inc(S(f"r_st{b}"), 16)
                act.wait_ge(S("slot3_free"), MOD_TURNS + 1 + n)
                for t in range(NC):
                    act.copy(V[:, t, :], ps[:, t, :]).then_inc(S("r_V"), 1)
                act.copy(V[0:NS, NC, :], ps[0:NS, 4, :]).then_inc(S("r_V"), 1)
                for f in range(4):
                    if f % 2 == 0:
                        act.wait_ge(S("r_g"), h * 2 + f // 2 + 1)
                    else:
                        act.wait_ge(S(f"slot{4 + f // 2}_free"), MOD_TURNS + 1 + n)
                    act.activation(halves(SG[:, f, :]), pair((6, 0, 2, 6)[f]), ACT.Silu).then_inc(S("r_sg"), 1)
                act.wait_ge(S("r_mv"), h * 5 + 4)
                act.activation(sd[:, 0:NC], mv[:, 0:NC, 1], ACT.Sqrt, bias=eps[:, :]).then_inc(S("r_sd"), 1)
                act.wait_ge(S("r_ks"), n * 2)
                act.copy(rnew[:, 1], ps[:, 4:6, :]).then_inc(S("r_sfc"), 1)
                act.wait_ge(S("r_sfc"), n)
                act.dma_start(ret_p_d[:, hs].rearrange("p h a v -> p (h a) v"), rnew[:, 1]).then_inc(S("r_out1"), 16)
                for b in range(NS):
                    act.wait_ge(S("r_new"), h * NS + b + 1)
                    act.dma_start(ret_s_d[:, b, hs].rearrange("p h a v -> p (h a) v"), rnew[:, b % 2]).then_inc(S(f"r_out{b % 2}"), 16)
                    if b + 2 < NS:
                        act.dma_start(rst[:, b % 2], ret_i_d[:, b + 2, hs].rearrange("p h a v -> p (h a) v")).then_inc(S(f"r_st{b % 2}"), 16)
                act.wait_ge(S("r_mv"), n * 5)
                act.activation(sd[0:NS, NC:NC + 1], mv[0:NS, NC, 1:2], ACT.Sqrt, bias=eps[0:NS, :]).then_inc(S("r_sd"), 1)
                for f in range(4):
                    act.wait_ge(S("r_onT"), h * 5 + f + 1)
                    act.activation(rt[:, f, 0:P], ps[:, (2, 3, 7, 0)[f], :], ACT.Identity, scale=gnc[:, 0, f:f + 1], bias=gnc[:, 1, f:f + 1])\
                       .then_inc(S("r_aff"), 1)
                act.wait_ge(S("r_onT"), n * 5)
                for f in range(4):
                    act.activation(rt[:, f, P:T], ps[:, 1, f * NS:(f + 1) * NS], ACT.Identity, scale=gnc[:, 0, f:f + 1], bias=gnc[:, 1, f:f + 1])\
                       .then_inc(S("r_aff"), 1)

        R_STEPS = 7

        def vector_ret(dve):
            delta_over(dve)
            link(dve, dve.memset(zero4[:, :], 0.0))
            dve.wait_ge(S("tables_in"), 16)
            dve.sem_inc(S("r_go"), 1)
            with dve.Fori(0, RH) as h:
                n = h + 1
                dve.wait_ge(S("r_go"), n)
                for i, r in enumerate((R_GNW, R_GNB)):
                    dve.tensor_tensor(gnc[:, i, :], colsT[:, bass.ds(h * 4 + r, 4)], zero4[:, :], ALU.add)
                for s, dst in ((0, qr), (1, kr)):
                    dve.wait_ge(S(f"slot{s}_free"), MOD_TURNS + H + 1 + n)
                    if s == 1:
                        dve.wait_ge(S("r_qkr"), h * 4 + 2)
                    for j, (x, c) in enumerate(((0, 0), (2, 1), (0, 1), (2, 0))):
                        dve.tensor_tensor(halves(rt[:, j, :]), pair(4 * s + x), halves(rot[:, c, :]), ALU.mult).then_inc(S("r_rt"), 1)
                dve.wait_ge(S("r_qkr"), n * 4)
                for a in range(2):
                    dve.tensor_tensor(qdg[:, a], qr[:, a, P:T].unsqueeze(1).to_broadcast([128, NS, NS]), mask8, ALU.mult)
                dve.wait_ge(S("r_tab"), n * 32)
                for t in range(NC):
                    w = P - t * 128
                    dve.wait_ge(S("r_s"), h * 4 + t + 1)
                    dve.tensor_tensor(PT[:, PO[t]:PO[t] + w], ps[:, (4, 5, 0, 1)[t], 0:w], dm[:, 0:w], ALU.mult).then_inc(S("r_pt"), 1)
                for i in range(NC):
                    dve.wait_ge(S("r_o"), h * 4 + i + 1)
                    dve.bn_stats(bn6[:, i, :], ps[:, (2, 3, 6, 7)[i], :]).then_inc(S("r_step"), 1)
                    dve.wait_ge(S("r_step"), h * R_STEPS + i + 1)
                    dve.sem_inc(S("pad"), 1)
                    dve.bn_aggr(mv[:, i, :], bn6[:, i, :]).then_inc(S("r_mv"), 1)
                dve.wait_ge(S("r_ks"), h * 2 + 1)
                dve.tensor_tensor(kd[:, :, :], ps[:, 0:2, :].rearrange("p a (t k) -> p (a t) k", t=2),
                                  rc[:, 0:NC].unsqueeze(2).to_broadcast([128, NC, RK]), ALU.mult).then_inc(S("r_kd"), 1)
                dve.scalar_tensor_tensor(kdg, ps[0:NS, 4, 0:RK].unsqueeze(1).to_broadcast([NS, NS, RK]), RK ** -0.5,
                                         ident[0:NS, 0:NS].unsqueeze(2).to_broadcast([NS, NS, RK]), ALU.mult, ALU.mult).then_inc(S("r_kd"), 1)
                dve.wait_ge(S("r_sd"), h * 2 + 1)
                dve.reciprocal(sd[:, 0:NC], sd[:, 0:NC]).then_inc(S("r_step"), 1)
                dve.wait_ge(S("r_step"), h * R_STEPS + 5)
                for i in range(NC):
                    dve.tensor_scalar(ON[:, i, :], ps[:, (2, 3, 6, 7)[i], :], mv[:, i, 0:1], sd[:, i:i + 1], ALU.subtract, ALU.mult).then_inc(S("r_on"), 1)
                for b in range(NS):
                    dve.wait_ge(S("r_kv"), h * NS + b + 1)
                    dve.wait_ge(S(f"r_st{b % 2}"), (h * 4 + b // 2 + 1) * 16)
                    if b % 2 == 1:
                        dve.wait_ge(S("r_out1"), (h * 5 + b // 2 + 1) * 16)
                    elif b >= 2:
                        dve.wait_ge(S("r_out0"), (h * 4 + b // 2) * 16)
                    if b >= 2:
                        dve.wait_ge(S("r_os"), h * NS + b - 1)
                    dve.scalar_tensor_tensor(rnew[:, b % 2], rst[:, b % 2], rc[:, NC:NC + 1], ps[:, (b % 2) * 4:(b % 2) * 4 + 2, :],
                                             ALU.mult, ALU.add).then_inc(S("r_new"), 1)
                dve.wait_ge(S("r_os"), n * NS)
                dve.bn_stats(bn6[0:NS, NC, :], ps[0:NS, 6, :]).then_inc(S("r_step"), 1)
                dve.wait_ge(S("r_step"), h * R_STEPS + 6)
                dve.sem_inc(S("pad"), 1)
                dve.bn_aggr(mv[0:NS, NC, :], bn6[0:NS, NC, :]).then_inc(S("r_mv"), 1)
                dve.wait_ge(S("r_sd"), n * 2)
                dve.reciprocal(sd[0:NS, NC:NC + 1], sd[0:NS, NC:NC + 1]).then_inc(S("r_step"), 1)
                dve.wait_ge(S("r_step"), h * R_STEPS + 7)
                dve.tensor_scalar(ON[0:NS, NC, :], ps[0:NS, 6, :], mv[0:NS, NC, 0:1], sd[0:NS, NC:NC + 1], ALU.subtract, ALU.mult)\
                   .then_inc(S("r_on"), 1)
                dve.wait_ge(S("r_aff"), n * 8 + 1)
                dve.wait_ge(S("r_out0"), n * 64)
                dve.wait_ge(S("r_out1"), n * 80)
                dve.tensor_tensor(OB[:, bass.ds(h * 4, 4), :], rt[:, :, :], SG[:, :, :], ALU.mult).then_inc(S("r_go"), 1)

        def pool_ret(pool):
            with pool.Fori(0, RH) as h:
                for s, dst in ((0, qr), (1, kr)):
                    pool.wait_ge(S("r_rt"), h * 8 + 4 * s + 4)
                    pool.tensor_tensor(dst[:, 0, :], rt[:, 0, :], rt[:, 1, :], ALU.subtract).then_inc(S("r_qkr"), 1)
                    pool.tensor_tensor(dst[:, 1, :], rt[:, 2, :], rt[:, 3, :], ALU.add).then_inc(S("r_qkr"), 1)

        Y = sb("Y", [128, DT, T])
        st5 = ExitStack()
        sg = sb("sg", [128, 2, T], st5)
        mt = sb("mt", [128, 2, T], st5)
        smx = sb("smx", [128, DT, NS], st5)
        st5.close()
        GATE_TURNS = 4
        USED_MIX = [MOD_TURNS + H + RH if s < 2 else MOD_TURNS + RH for s in range(SLOTS)]
        wda = A["w_down_a"][0].rearrange("(k p) n -> p k n", p=128)
        wdb = A["w_down_b"][0].rearrange("(k p) n -> p k n", p=128)
        wo = A["w_out"][0].rearrange("(k p) n -> p k n", p=128)

        def sync_merge(sp):
            with sp.Fori(0, GATE_TURNS) as i:
                for s, src in enumerate((w_in[:, :, bass.ds(i * 256 + GATE_A, 256)], w_in[:, :, bass.ds(i * 256 + GATE_B, 256)],
                                         wda[:, :, bass.ds(i * 256, 256)], wdb[:, 0:8, bass.ds(i * 256, 256)],
                                         wdb[:, 8:16, bass.ds(i * 256, 256)])):
                    load_slot(sp, s, src, i)
            for s in range(5):
                loads[s] += GATE_TURNS
            for s in range(4):
                load_slot(sp, s, wo[:, :, s * 256:(s + 1) * 256])
                loads[s] += 1

        def product(pe, bank, parts):
            for k, (w, x) in enumerate(parts):
                for a in range(2):
                    mm = pe.matmul(ps[:, bank + a, 0:TH], w, x[:, a * TH:(a + 1) * TH], start=(k == 0), stop=(k == len(parts) - 1))
            return mm

        def tensor_merge(pe):
            pe.wait_ge(S("r_go"), RH + 1)
            with pe.Fori(0, GATE_TURNS) as i:
                for m in range(2):
                    f = slice(m * 128, (m + 1) * 128)
                    plans = ((0, [(W[:, 0, k, f], HT[:, k, :]) for k in range(DT)], (0,)),
                             (2, [(W[:, 1, k, f], HT[:, k, :]) for k in range(DT)], (1,)),
                             (4, [(W[:, 2, k, f], OA[:, k, :]) for k in range(DT)], (2,)),
                             (6, [(W[:, 3 + k // 8, k % 8, f], OB[:, k, :]) for k in range(16)], (3, 4)))
                    for q, (bank, parts, slots) in enumerate(plans):
                        if m == 0:
                            for s in slots:
                                slot_ready(pe, s, i)
                        if q < 2:
                            pe.wait_ge(S("m_sig"), i * 4 + m * 2 + q + 1)
                        else:
                            pe.wait_ge(S("m_mul"), i * 4 + m * 2 + q - 1)
                        mm = product(pe, bank, parts)
                        mm.then_inc(S("m_tile"), 1)
                        if m == 1 and q:
                            pe.wait_ge(S("m_tile"), i * 8 + 4 + q)
                            for s in plans[q - 1][2]:
                                pe.sem_inc(S(f"slot{s}_free"), 1)
                    if m == 1:
                        pe.wait_ge(S("m_tile"), i * 8 + 8)
                        for s in plans[3][2]:
                            pe.sem_inc(S(f"slot{s}_free"), 1)
            for s in range(5):
                fulls[s] += GATE_TURNS
            pe.wait_ge(S("m_merged"), 9)
            for d in range(DT):
                if d % 2 == 0:
                    slot_ready(pe, d // 2)
                if d >= 4:
                    pe.wait_ge(S("m_res"), d - 3)
                mm = product(pe, 2 * (d % 4), [(W[:, d // 2, k, (d % 2) * 128:(d % 2) * 128 + 128], Y[:, k, :]) for k in range(DT)])
                mm.then_inc(S("m_out"), 1)
            pe.wait_ge(S("m_out"), DT)
            for s in range(4):
                pe.sem_inc(S(f"slot{s}_free"), 1)
                fulls[s] += 1

        def scalar_merge(act):
            act.wait_ge(S("r_go"), RH + 1)
            act.sem_inc(S("m_sig"), 2)
            with act.Fori(0, GATE_TURNS) as i:
                for m in range(2):
                    act.wait_ge(S("m_mul"), i * 4 + m * 2 + 2)
                    for q in range(2):
                        act.wait_ge(S("m_tile"), i * 8 + m * 4 + q + 1)
                        act.activation(halves(sg[:, q, :]), pair(2 * q), ACT.Sigmoid).then_inc(S("m_sig"), 1)

        def vector_merge(dve):
            dve.sem_inc(S("m_mul"), 2)
            dve.sem_inc(S("m_merged"), 1)
            with dve.Fori(0, GATE_TURNS) as i:
                for m in range(2):
                    dve.wait_ge(S("m_merged"), i * 2 + m + 1)
                    for q in range(2):
                        dve.wait_ge(S("m_tile"), i * 8 + m * 4 + q + 3)
                        dve.wait_ge(S("m_sig"), i * 4 + m * 2 + q + 3)
                        dve.tensor_tensor(halves(mt[:, q, :]), pair(4 + 2 * q), halves(sg[:, q, :]), ALU.mult).then_inc(S("m_mul"), 1)
                    dve.wait_ge(S("m_mul"), i * 4 + m * 2 + 4)
                    dve.tensor_tensor(Y[:, bass.ds(i * 2 + m, 1), :].rearrange("p d t -> p (d t)"), mt[:, 0, :], mt[:, 1, :], ALU.add)\
                       .then_inc(S("m_merged"), 1)
            residual(dve, "m_out", "m_res", 2)

        def residual(dve, ready, done, part):
            for d in range(DT):
                g = modT[:, part * 8 + d, :]
                dve.wait_ge(S(ready), d + 1)
                b = 2 * (d % 4)
                dve.scalar_tensor_tensor(XT[:, d, 0:TH], ps[:, b, 0:TH], g[:, 0:1], XT[:, d, 0:TH], ALU.mult, ALU.add)
                dve.scalar_tensor_tensor(XT[:, d, TH:P], ps[:, b + 1, 0:P - TH], g[:, 0:1], XT[:, d, TH:P], ALU.mult, ALU.add)
                dve.tensor_tensor(smx[:, d, :], ps[:, b + 1, P - TH:TH], g[:, 1:9], ALU.mult).then_inc(S(done), 1)
            dve.wait_ge(S(done), DT)
            dve.tensor_tensor(XT[:, :, P:T], XT[:, :, P:T], smx[:, :, :], ALU.add).then_inc(S(done), 1)

        st6 = ExitStack()
        rwrow = sb("rwrow", [E, DT, 128], st6)
        rwT = sb("rwT", [128, DT, E], st6)
        rbias = sb("rbias", [128, E], st6)
        NT = NC + 1
        sc = sb("sc", [128, NT, E], st6)
        bs = sb("bs", [128, NT, E], st6)
        rep = sb("rep", [128, NT, E], st6)
        sel = sb("sel", [128, NT, E], st6)
        g8 = sb("g8", [128, NT, NG, 8], st6)
        gs = sb("gs", [128, NT, 16], st6)
        gv = sb("gv", [128, NT, 8], st6)
        gr = sb("gr", [128, NT, 16], st6)
        gm = sb("gm", [128, NT, NG], st6)
        v8 = sb("v8", [128, NT, 8], st6)
        wsum = sb("wsum", [128, NT], st6)
        selT = sb("selT", [E, T], st6)
        cwT = sb("cwT", [E, T], st6)
        posT = sb("posT", [E, T], st6)
        rankT = sb("rankT", [E, T], st6)
        cnt = sb("cnt", [E, 4], st6)
        thr = sb("thr", [E, 5], st6)
        own = sb("own", [E, 5, NB], st6)
        LOW, LOWER = -1e30, -2e30

        def sync_route(sp):
            sp.wait_ge(S("m_res"), DT + 1)
            sp.dma_start(rwrow[:, :, :], A["router_w"][0].rearrange("e (k p) -> e k p", p=128)).then_inc(S("tables_in"), 16)
            sp.dma_start(rbias[:, :], A["router_bias"].partition_broadcast(128).rearrange("p a e -> p (a e)")).then_inc(S("tables_in"), 16)

        def tensor_route(pe):
            pe.wait_ge(S("tables_in"), 64)
            for k in range(DT):
                mm = pe.transpose(ps[:, 2, k * E:(k + 1) * E], rwrow[:, k, :], ident[0:E, 0:E])
            mm.then_inc(S("route_ps"), 1)
            pe.wait_ge(S("rwT"), 1)
            pe.wait_ge(S("norm_done"), 2 * NORMED)
            for t in range(NT):
                n = 128 if t < NC else NS
                for k in range(DT):
                    mm = pe.matmul(ps[0:n, 3, t * E:(t + 1) * E], HT[:, k, t * 128:t * 128 + n], rwT[:, k, :], start=(k == 0), stop=(k == DT - 1))
            mm.then_inc(S("route_ps"), 1)

        def scalar_route(act):
            act.wait_ge(S("route_ps"), 1)
            act.wait_ge(S("m_res"), DT + 1)
            act.copy(rwT[:, :, :], ps[:, 2, :].rearrange("p (k e) -> p k e", k=DT)).then_inc(S("rwT"), 1)
            act.wait_ge(S("sc_clear"), 1)
            act.wait_ge(S("route_ps"), 2)
            act.activation(sc[:, 0:NC, :], ps[:, 3, 0:NC * E].rearrange("p (t e) -> p t e", t=NC), ACT.Exp, scale=-1.0).then_inc(S("sc_exp"), 1)
            act.activation(sc[0:NS, NC, :], ps[0:NS, 3, NC * E:NT * E], ACT.Exp, scale=-1.0).then_inc(S("sc_exp"), 1)

        def vector_route(dve):
            dve.wait_ge(S("m_res"), DT + 1)
            dve.memset(sc[:, NC, :], 0.0).then_inc(S("sc_clear"), 1)
            dve.memset(gs[:, :, 8:16], LOW)
            link(dve, dve.memset(gv[:, :, 4:8], LOW))
            dve.wait_ge(S("sc_exp"), 2)
            flat = lambda x: x[:, :, :].rearrange("p t e -> p (t e)")
            link(dve, dve.tensor_scalar(flat(sc), flat(sc), 1.0, None, ALU.add))
            link(dve, dve.reciprocal(flat(sc), flat(sc)))
            dve.wait_ge(S("tables_in"), 64)
            link(dve, dve.tensor_tensor(bs[:, :, :], sc[:, :, :], rbias[:, :].unsqueeze(1).to_broadcast([128, NT, E]), ALU.add))
            for t in range(NT):
                for g in range(NG):
                    ins = dve.max(g8[:, t, g, :], bs[:, t, g * 8:(g + 1) * 8])
            link(dve, ins)
            link(dve, dve.tensor_tensor(gs[:, :, 0:NG], g8[:, :, :, 0], g8[:, :, :, 1], ALU.add))
            for t in range(NT):
                ins = dve.max(v8[:, t, :], gs[:, t, 0:NG])
            link(dve, ins)
            link(dve, dve.tensor_copy(gv[:, :, 0:TOPG], v8[:, :, 0:TOPG]))
            for t in range(NT):
                ins = dve.match_replace(gr[:, t, :], gv[:, t, :], gs[:, t, :], LOWER)
            link(dve, ins)
            link(dve, dve.tensor_tensor(gm[:, :, :], gr[:, :, 0:NG], gs[:, :, 0:NG], ALU.not_equal))
            link(dve, dve.tensor_copy(rep[:, :, :].rearrange("p t (g e) -> p t g e", g=NG), gm[:, :, :].unsqueeze(3).to_broadcast([128, NT, NG, 8])))
            dve.tensor_tensor(flat(bs), flat(bs), flat(rep), ALU.mult)
            link(dve, dve.tensor_scalar(flat(rep), flat(rep), 1.0, -LOW, ALU.subtract, ALU.mult))
            link(dve, dve.tensor_tensor(flat(bs), flat(bs), flat(rep), ALU.add))
            for t in range(NT):
                ins = dve.max(v8[:, t, :], bs[:, t, :])
            link(dve, ins)
            for t in range(NT):
                ins = dve.match_replace(rep[:, t, :], v8[:, t, :], bs[:, t, :], LOWER)
            link(dve, ins)
            link(dve, dve.tensor_tensor(flat(sel), flat(rep), flat(bs), ALU.not_equal))
            link(dve, dve.tensor_tensor(flat(sc), flat(sc), flat(sel), ALU.mult))
            link(dve, dve.tensor_reduce(wsum[:, :], sc[:, :, :], AX.X, ALU.add))
            link(dve, dve.reciprocal(wsum[:, :], wsum[:, :]))
            dve.scalar_tensor_tensor(sc[:, :, :], sc[:, :, :], RSCALE, wsum[:, :].unsqueeze(2).to_broadcast([128, NT, E]), ALU.mult, ALU.mult)\
               .then_inc(S("cw"), 1)

        I32 = mybir.dt.int32
        mtab = sb("mtab", [128, M_END], st6)
        rb_t = sb("rb_t", [128, NT, NB], st6)
        val = sb("val", [128, NT, NB, 2], st6)
        erow = sb("erow", [1, NB], st6, I32)
        turn2 = sb("turn2", [1, 2], st6, I32)
        ob = OB[:, :, :].rearrange("p a t -> p (a t)")
        gsl = ob[:, 4 * D:4 * D + 2 * T].rearrange("p (f t) -> p f t", f=2)
        ush = ob[:, 4 * D + 2 * T:4 * D + 4 * T].rearrange("p (f t) -> p f t", f=2)
        hsh = OA[:, 6:8, :]
        hrow = ob[:, 2 * D:4 * D].rearrange("p (j d) -> p j d", j=2)
        pick = OA[:, 0:3, :].rearrange("p a t -> p (a t)")[:, 0:2 * NT * 128].rearrange("p (j t s) -> p j t s", j=2, t=NT)
        pv = sb("pv", [128, NT, 2], st6)
        zval = sb("zval", [128, NT, 2], st6)
        vf = sb("vf", [128, 2, 2], st6)
        wcur = sb("wcur", [128, 2, 1], st6)
        posg = sb("posg", [128, 2, 1], st6, I32)
        gidx = sb("gidx", [128, 2, 1], st6, mybir.dt.uint32)
        poss = sb("poss", [128, 2, 1], st6, mybir.dt.uint32)
        xg = ob[:, 0:2 * D].rearrange("p (j d) -> p j d", j=2)
        xgT = ob[:, 4 * D:6 * D].rearrange("p (j k s) -> p j k s", j=2, k=DT)
        ysc = hrow
        bsl = ob[:, 6 * D:6 * D + 256]
        bhid = ob[:, 6 * D + 256:6 * D + 512].rearrange("p (f s) -> p f s", f=2)
        st6.close()
        h2_d = nc.dram_tensor("ffn_rows", [T + 2, D], F32, kind="Internal").ap()
        yk_d = nc.dram_tensor("expert_rows", [(T + 1) * TOPK + 1, D], F32, kind="Internal").ap()
        wg = A["w_gate"][0].rearrange("e (k p) n -> p e k n", p=128)
        wu = A["w_up"][0].rearrange("e (k p) n -> p e k n", p=128)
        wd = A["w_down"][0].rearrange("e (k p) n -> p e k n", p=128)

        def down(w):
            return w.rearrange("p k n -> p (k n)").rearrange("p (k n) -> p k n", k=2)

        def turns_of(eng):
            eng.wait_ge(S("list_done"), 2)
            return eng.value_load(turn2[0:1, 1:2], min_val=1, max_val=NB // 2 - 3)

        def sync_list(sp):
            load_slot(sp, 0, A["ws_gate"][0].rearrange("(k p) n -> p k n", p=128))
            load_slot(sp, 1, A["ws_up"][0].rearrange("(k p) n -> p k n", p=128))
            load_slot(sp, 2, A["ws_down"][0].rearrange("(k p) n -> p k n", p=128), shape=down)
            for s in range(3):
                loads[s] += 1
            sp.dma_start(mtab[:, :], A["moe"]).then_inc(S("tables_in"), 16)
            for t in range(NT):
                n = 128 if t < NC else NS + 2
                sp.wait_ge(S("rows_evac"), (t + 1) * 2)
                sp.dma_start(h2_d[t * 128:t * 128 + n, :], hrow[0:n, t % 2, :]).then_inc(S(f"rows_out{t % 2}"), 16)

        def tensor_list(pe):
            for t in range(NT):
                n = 128 if t < NC else NS
                if t >= 2:
                    pe.wait_ge(S("rows_evac"), (t - 1) * 2)
                for d in range(DT):
                    mm = pe.transpose(ps[0:n, 4 + 2 * (t % 2) + d // 4, (d % 4) * 128:(d % 4) * 128 + 128], HT[:, d, t * 128:t * 128 + n], ident)
                mm.then_inc(S("rows_T"), 1)
            for f in range(2):
                for q in range(2):
                    if f == 0:
                        slot_ready(pe, q)
                    if f == 1:
                        pe.wait_ge(S("rows_evac"), NT * 2)
                    if (f, q) == (0, 1):
                        pe.wait_ge(S("sc_exp"), 2)
                    mm = product(pe, 4 * f + 2 * q, [(W[:, q, k, f * 128:(f + 1) * 128], HT[:, k, :]) for k in range(DT)])
                    mm.then_inc(S(f"slot{q}_free") if f == 1 else S("sh_gu"), 1)
            slot_ready(pe, 2)
            for d in range(DT):
                if d == 0:
                    pe.wait_ge(S("sh_hid"), 2)
                if d >= 4:
                    pe.wait_ge(S("sh_y"), d - 3)
                mm = product(pe, 2 * (d % 4), [(down(W[:, 2])[:, k, d * 128:(d + 1) * 128], hsh[:, k, :]) for k in range(2)])
                mm.then_inc(S("sh_down"), 1)
            pe.wait_ge(S("sh_down"), DT)
            pe.sem_inc(S("slot2_free"), 1)
            for s in range(3):
                fulls[s] += 1
            pe.wait_ge(S("sh_y"), DT)
            pe.wait_ge(S("cw"), 1)
            for x, b in ((sel, 4), (sc, 6)):
                for t in range(NC):
                    pe.transpose(ps[0:E, b, t * 128:(t + 1) * 128], x[:, t, :], ident)
                pe.transpose(ps[0:E, b + 1, 0:NS], x[0:NS, NC, :], ident[0:NS, 0:NS]).then_inc(S("route_ps"), 1)
            for i in range(NT):
                n = 128 if i < NC else NS
                out = ps[0:E, 0, i * 128:i * 128 + 128] if i < NC else ps[0:E, 1, 0:NS]
                for t in range(i + 1):
                    m = 128 if t < NC else NS
                    pe.matmul(out, sel[0:m, t, :], (incl if t == i else ones)[0:m, 0:n], start=(t == 0), stop=(t == i))
            for t in range(NT):
                m = 128 if t < NC else NS
                mm = pe.matmul(ps[0:E, 1, 16:17], sel[0:m, t, :], ones[0:m, 0:1], start=(t == 0), stop=(t == NT - 1))
            mm.then_inc(S("route_ps"), 1)
            pe.wait_ge(S("l_Tc"), 4)
            for a in range(2):
                mm = pe.matmul(ps[0:E, 2 + a, 0:TH], incl[0:E, 0:E], selT[:, a * TH:(a + 1) * TH], start=True, stop=True)
            mm.then_inc(S("route_ps"), 1)
            pe.wait_ge(S("l_nb"), 1)
            pe.matmul(ps[0:E, 1, 32:33], incl[0:E, 0:E], cnt[:, 1:2], start=True, stop=True)
            pe.matmul(ps[:, 1, 48:49], ones[0:E, :], cnt[:, 1:2], start=True, stop=True).then_inc(S("route_ps"), 1)
            pe.wait_ge(S("l_own"), 1)
            pe.wait_ge(S("l_pos"), 2)
            pe.matmul(ps[:, 4, 0:NB], ones[0:E, :], own[:, 4, :], start=True, stop=True)
            for t in range(NT):
                n = 128 if t < NC else NS
                tok_ = slice(t * 128, t * 128 + n)
                blk = slice(t * NB, (t + 1) * NB)
                pe.matmul(ps[0:n, 0, blk], rankT[:, tok_], own[:, 1, :], start=True, stop=False)
                pe.matmul(ps[0:n, 0, blk], ones[0:E, 0:n], own[:, 3, :], start=False, stop=True)
                pe.matmul(ps[0:n, 5, blk], posT[:, tok_], own[:, 1, :], start=True, stop=True)
                mm = pe.matmul(ps[0:n, 6, blk], cwT[:, tok_], own[:, 1, :], start=True, stop=True)
            mm.then_inc(S("route_ps"), 1)

        def scalar_list(act):
            for t in range(NT):
                n = 128 if t < NC else NS
                act.wait_ge(S("rows_T"), t + 1)
                if t >= 2:
                    act.wait_ge(S(f"rows_out{t % 2}"), (t // 2) * 16)
                for a in range(2):
                    act.copy(hrow[0:n, t % 2, a * 512:(a + 1) * 512], ps[0:n, 4 + 2 * (t % 2) + a, :]).then_inc(S("rows_evac"), 1)
            for f in range(2):
                if f == 0:
                    act.wait_ge(S("sh_gu"), 2)
                else:
                    act.wait_ge(S("slot1_free"), USED_MIX[1] + 5 + 2)
                act.activation(halves(gsl[:, f, :]), pair(4 * f), ACT.Silu).then_inc(S("sh_act"), 1)
                act.copy(halves(ush[:, f, :]), pair(4 * f + 2)).then_inc(S("sh_act"), 1)
            for d in range(DT):
                act.wait_ge(S("sh_down"), d + 1)
                act.copy(halves(Y[:, d, :]), pair(2 * (d % 4))).then_inc(S("sh_y"), 1)
            act.wait_ge(S("route_ps"), 4)
            for dst, b in ((selT, 4), (cwT, 6)):
                act.copy(dst[:, 0:P], ps[0:E, b, :]).then_inc(S("l_Tc"), 1)
                act.copy(dst[:, P:T], ps[0:E, b + 1, 0:NS]).then_inc(S("l_Tc"), 1)

        def pool_list(pool):
            for f in range(2):
                pool.wait_ge(S("sh_act"), 2 * f + 2)
                pool.tensor_tensor(hsh[:, f, :], gsl[:, f, :], ush[:, f, :], ALU.mult).then_inc(S("sh_hid"), 1)

        def vector_list(dve):
            dve.memset(rb_t[:, NC, :], 0.0)
            dve.memset(val[:, NC, :, :], 0.0)
            dve.memset(zval[:, :, :], 0.0)
            link(dve, dve.memset(xg[:, :, :], 0.0))
            dve.wait_ge(S("tables_in"), 64)
            for j in range(2):
                dve.tensor_copy(poss[:, j, :], mtab[:, M_CAP + j:M_CAP + j + 1]).then_inc(S("b_spare"), 1)
            dve.wait_ge(S("route_ps"), 5)
            dve.wait_ge(S("l_Tc"), 4)
            dve.tensor_tensor(rankT[:, 0:P], ps[0:E, 0, :], selT[:, 0:P], ALU.mult)
            dve.tensor_tensor(rankT[:, P:T], ps[0:E, 1, 0:NS], selT[:, P:T], ALU.mult)
            link(dve, dve.tensor_copy(cnt[:, 0:1], ps[0:E, 1, 16:17]))
            link(dve, dve.tensor_scalar(thr[:, :], mtab[0:E, M_THR:M_THR + 5], cnt[:, 0:1], None, ALU.is_lt))
            dve.tensor_reduce(cnt[:, 1:2], thr[:, :], AX.X, ALU.add).then_inc(S("l_nb"), 1)
            dve.wait_ge(S("route_ps"), 6)
            dve.tensor_tensor(halves(posT[:, :]), ps[0:E, 2:4, 0:TH], halves(mtab[0:E, M_POS:M_POS + T]), ALU.add).then_inc(S("l_pos"), 1)
            dve.wait_ge(S("route_ps"), 7)
            dve.wait_ge(S("l_nb"), 1)
            link(dve, dve.tensor_tensor(cnt[:, 3:4], ps[0:E, 1, 32:33], cnt[:, 1:2], ALU.subtract))
            link(dve, dve.tensor_scalar(own[:, 0, :], mtab[0:E, M_BLOCK:M_BLOCK + NB], cnt[:, 3:4], None, ALU.subtract))
            dve.tensor_scalar(own[:, 1, :], own[:, 0, :], 0.0, None, ALU.is_ge)
            link(dve, dve.tensor_scalar(own[:, 2, :], own[:, 0, :], cnt[:, 1:2], None, ALU.is_ge))
            link(dve, dve.tensor_tensor(own[:, 1, :], own[:, 1, :], own[:, 2, :], ALU.subtract))
            dve.scalar_tensor_tensor(own[:, 3, :], own[:, 0, :], -128.0, own[:, 1, :], ALU.mult, ALU.mult)
            dve.tensor_scalar(own[:, 4, :], own[:, 1, :], mtab[0:E, M_EXP:M_EXP + 1], None, ALU.mult).then_inc(S("l_own"), 1)
            link(dve, dve.tensor_scalar(turn2[0:1, 0:1], ps[0:1, 1, 48:49], 1.0, None, ALU.add))
            dve.tensor_scalar(turn2[0:1, 1:2], turn2[0:1, 0:1], 1, None, ALU.logical_shift_right).then_inc(S("l_pos"), 1)
            dve.wait_ge(S("route_ps"), 8)
            dve.tensor_copy(erow[:, :], ps[0:1, 4, 0:NB]).then_inc(S("list_done"), 1)
            v = lambda b, n=128, t0=0, t1=NC: ps[0:n, b, t0 * NB:t1 * NB].rearrange("p (t b) -> p t b", b=NB)
            for n, t0, t1 in ((128, 0, NC), (NS, NC, NT)):
                dve.tensor_copy(rb_t[0:n, t0:t1, :], v(0, n, t0, t1))
                dve.tensor_copy(val[0:n, t0:t1, :, 0], v(5, n, t0, t1))
                ins = dve.tensor_copy(val[0:n, t0:t1, :, 1], v(6, n, t0, t1))
            link(dve, ins)
            dve.sem_inc(S("list_done"), 1)

        USED_MOE = [u + g for u, g in zip(USED_MIX, (6, 6, 6, 5, 4, 0))]

        def block_pick(dve, j, n):
            dve.tensor_tensor(pick[:, j], mtab[:, M_PLACE:M_PLACE + 128].unsqueeze(1).to_broadcast([128, NT, 128]),
                              rb_t[:, :, bass.ds(n, 1)].to_broadcast([128, NT, 128]), ALU.is_equal)
            dve.tensor_tensor(pv[:, :, :], val[:, :, bass.ds(n, 1), :].rearrange("p t b v -> p t (b v)"), zval[:, :, :], ALU.add)\
               .then_inc(S("b_sel"), 1)

        def block_index(dve, j, n, step):
            dve.wait_ge(S("b_ps"), n + 1)
            dve.tensor_copy(vf[:, j, 1:2], ps[:, 6, 1:2])
            link2(dve, step, dve.tensor_scalar(vf[:, j, 0:1], ps[:, 6, 0:1], float(BIG), mtab[:, M_CAP + j:M_CAP + j + 1], ALU.add, ALU.min))
            link2(dve, step + 1, dve.tensor_copy(posg[:, j, :], vf[:, j, 0:1]))
            dve.tensor_scalar(gidx[:, j, :].bitcast(I32), posg[:, j, :], 3, None, ALU.logical_shift_right).then_inc(S("b_idx"), 1)

        def link2(dve, done, ins):
            ins.then_inc(S("b_step"), 1)
            dve.wait_ge(S("b_step"), done + 1)

        def vector_blocks(dve):
            dve.sem_inc(S("b_y"), 2)
            for t, count in ((0, 3), (1, 2)):
                dve.wait_ge(S(f"rows_out{t}"), count * 16)
            turns = turns_of(dve)
            block_pick(dve, 0, 0)
            block_index(dve, 0, 0, 0)
            block_pick(dve, 1, 1)
            block_index(dve, 1, 1, 2)
            block_pick(dve, 0, 2)
            with dve.Fori(0, turns) as i:
                for j in range(2):
                    n = i * 2 + j
                    dve.wait_ge(S(f"b_scat{j}"), (i + 1) * 16)
                    dve.wait_ge(S("b_idx"), n + 1)
                    dve.tensor_copy(wcur[:, j, :], vf[:, j, 1:2])
                    link2(dve, n * 3 + 4, dve.tensor_copy(poss[:, j, :], vf[:, j, 0:1]))
                    block_index(dve, j, n + 2, n * 3 + 5)
                    dve.wait_ge(S(f"slot{3 * j + 1}_free"), i + USED_MOE[3 * j + 1] + 2)
                    dve.wait_ge(S("b_silu"), n + 1)
                    dve.tensor_tensor(bhid[:, :, :].rearrange("p f s -> p (f s)"), ps[:, 1, 0:256], bsl, ALU.mult).then_inc(S("b_hid"), 1)
                    block_pick(dve, 1 - j, n + 3)
                    dve.wait_ge(S(f"slot{3 * j + 2}_free"), i + USED_MOE[3 * j + 2] + 2)
                    dve.tensor_scalar(ysc[:, j, 512:D], ps[:, 3, :], wcur[:, j, :], None, ALU.mult).then_inc(S("b_y"), 1)

        def scalar_blocks(act):
            for t, count in ((0, 3), (1, 2)):
                act.wait_ge(S(f"rows_out{t}"), count * 16)
            turns = turns_of(act)
            block_xT(act, 0, 0)
            with act.Fori(0, turns) as i:
                for j in range(2):
                    n = i * 2 + j
                    act.wait_ge(S(f"slot{3 * j}_free"), i + USED_MOE[3 * j] + 2)
                    act.activation(bsl, ps[:, 0, 0:256], ACT.Silu).then_inc(S("b_silu"), 1)
                    block_xT(act, 1 - j, n + 1)
                    act.wait_ge(S(f"b_scat{j}"), (i + 1) * 16)
                    act.wait_ge(S(f"slot{3 * j + 2}_free"), i + USED_MOE[3 * j + 2] + 2)
                    act.mul(ysc[:, j, 0:512], ps[:, 2, :], wcur[:, j, :]).then_inc(S("b_y"), 1)

        def block_xT(act, j, n):
            act.wait_ge(S("b_T"), n + 1)
            act.copy(xgT[:, j].rearrange("p k s -> p (k s)"), ps[:, 4:6, :].rearrange("p a s -> p (a s)")).then_inc(S("b_xT"), 1)

        def block_places(pe, j, n):
            pe.wait_ge(S("b_sel"), n + 1)
            for t in range(NT):
                m = 128 if t < NC else NS
                mm = pe.matmul(ps[:, 6, 0:2], pick[0:m, j, t, :], pv[0:m, t, :], start=(t == 0), stop=(t == NT - 1))
            mm.then_inc(S("b_ps"), 1)

        def block_T(pe, j, n, loads_):
            pe.wait_ge(S(f"b_gat{j}"), loads_ * 16)
            for d in range(DT):
                mm = pe.transpose(ps[:, 4 + d // 4, (d % 4) * 128:(d % 4) * 128 + 128], xg[:, j, d * 128:(d + 1) * 128], ident)
            mm.then_inc(S("b_T"), 1)

        def tensor_blocks(pe):
            turns = turns_of(pe)
            block_places(pe, 0, 0)
            block_T(pe, 0, 0, 1)
            pe.wait_ge(S("b_idx"), 1)
            block_places(pe, 1, 1)
            with pe.Fori(0, turns) as i:
                for j in range(2):
                    n = i * 2 + j
                    pe.wait_ge(S("b_idx"), n + 2)
                    block_places(pe, j, n + 2)
                    pe.wait_ge(S("b_xT"), n + 1)
                    for q in range(2):
                        slot_ready(pe, 3 * j + q, i)
                        for f in range(2):
                            for k in range(DT):
                                mm = pe.matmul(ps[:, q, f * 128:(f + 1) * 128], W[:, 3 * j + q, k, f * 128:(f + 1) * 128], xgT[:, j, k, :],
                                               start=(k == 0), stop=(k == DT - 1))
                        mm.then_inc(S(f"slot{3 * j + q}_free"), 1)
                    block_T(pe, 1 - j, n + 1, i + 1 + j)
                    slot_ready(pe, 3 * j + 2, i)
                    pe.wait_ge(S("b_hid"), n + 1)
                    pe.wait_ge(S("b_y"), n * 2 + 2)
                    for a in range(2):
                        for k in range(2):
                            mm = pe.matmul(ps[:, 2 + a, :], bhid[:, k, :], down(W[:, 3 * j + 2])[:, k, a * 512:(a + 1) * 512],
                                           start=(k == 0), stop=(k == 1))
                    mm.then_inc(S(f"slot{3 * j + 2}_free"), 1)

        def pool_blocks(pool):
            pool.wait_ge(S("rows_out0"), 48)
            pool.wait_ge(S("rows_out1"), 32)
            pool.wait_ge(S("b_spare"), 2)
            for j in range(2):
                block_scatter(pool, j)
            turns = turns_of(pool)
            block_gather(pool, 0, 0)
            block_gather(pool, 1, 1)
            with pool.Fori(0, turns) as i:
                for j in range(2):
                    n = i * 2 + j
                    block_gather(pool, j, n + 2)
                    pool.wait_ge(S("b_y"), n * 2 + 4)
                    pool.sem_inc(S("pad"), 1)
                    block_scatter(pool, j)

        def block_scatter(pool, j):
            pool.indirect_dma_start(yk_d, bass.IndirectOffsetOnAxis(poss[:, j, :], 0), ysc[:, j, :], None,
                                    bounds_check=(T + 1) * TOPK, oob_is_err=False).then_inc(S(f"b_scat{j}"), 16)

        def block_gather(pool, j, n):
            pool.wait_ge(S("b_idx"), n + 1)
            pool.sem_inc(S("pad"), 1)
            pool.indirect_dma_start(xg[:, j, :], None, h2_d, bass.IndirectOffsetOnAxis(gidx[:, j, :], 0),
                                    bounds_check=T + 1, oob_is_err=False).then_inc(S(f"b_gat{j}"), 16)

        def sync_blocks(sp):
            turns = turns_of(sp)
            with sp.Fori(0, turns) as i:
                for j in range(2):
                    e = sp.value_load(erow[0:1, bass.ds(i * 2 + j, 1)], min_val=0, max_val=E - 1)
                    for q, w in enumerate((wg, wu, wd)):
                        load_slot(sp, 3 * j + q, w[:, bass.ds(e, 1)].rearrange("p e k n -> p (e k) n"), i, shape=down if q == 2 else None)
            sp.wait_ge(S("b_scat0"), (turns + 1) * 16)
            sp.sem_inc(S("pad"), 1)
            sp.wait_ge(S("b_scat1"), (turns + 1) * 16)
            sp.sem_inc(S("pad"), 1)
            sp.wait_ge(S("b_gat0"), (turns + 1) * 16)
            sp.sem_inc(S("pad"), 1)
            sp.wait_ge(S("b_gat1"), (turns + 1) * 16)
            sp.sem_inc(S("rows_ready"), 1)
            for t in range(NT):
                n = 128 if t < NC else NS
                if t >= 2:
                    sp.wait_ge(S("k_sum"), t - 1)
                sp.dma_start(ykt[t % 2][0:n], yk_d[t * 128 * TOPK:(t * 128 + n) * TOPK, :].rearrange("(p k) d -> p k d", k=TOPK))\
                  .then_inc(S(f"yk_in{t % 2}"), 16)

        ykt = [ob[:, 0:TOPK * D].rearrange("p (k d) -> p k d", k=TOPK),
               W[:, 0:4].rearrange("p s k n -> p (s k n)").rearrange("p (k d) -> p k d", k=TOPK)]
        ysum = OA[:, 0:4, :].rearrange("p a t -> p (a t)")[:, 0:2 * D].rearrange("p (j d) -> p j d", j=2)

        def vector_gather(dve):
            dve.wait_ge(S("rows_ready"), 1)
            for t in range(NT):
                n = 128 if t < NC else NS
                dve.wait_ge(S(f"yk_in{t % 2}"), (t // 2 + 1) * 16)
                if t >= 2:
                    dve.wait_ge(S("rows_T"), NT + t - 1)
                dve.tensor_reduce(ysum[0:n, t % 2, :], ykt[t % 2][0:n].rearrange("p k d -> p d k"), AX.X, ALU.add).then_inc(S("k_sum"), 1)
                if t >= 1:
                    gather_add(dve, t - 1)
            gather_add(dve, NT - 1)

        def gather_add(dve, t):
            n = 128 if t < NC else NS
            dve.wait_ge(S("rows_T"), NT + t + 1)
            y = Y[:, :, t * 128:t * 128 + n]
            dve.tensor_tensor(y, ps[:, 2 * (t % 2):2 * (t % 2) + 2, :].rearrange("p a (d s) -> p (a d) s", d=4)[:, :, 0:n], y, ALU.add).then_inc(S("k_add"), 1)

        def tensor_gather(pe):
            for t in range(NT):
                n = 128 if t < NC else NS
                pe.wait_ge(S("k_sum"), t + 1)
                if t >= 2:
                    pe.wait_ge(S("k_add"), t - 1)
                for d in range(DT):
                    mm = pe.transpose(ps[:, 2 * (t % 2) + d // 4, (d % 4) * 128:(d % 4) * 128 + n], ysum[0:n, t % 2, d * 128:(d + 1) * 128], ident[0:n, 0:n])
                mm.then_inc(S("rows_T"), 1)

        yout = sb("yout", [128, 2, D])

        def vector_final(dve):
            for d in range(DT):
                g = modT[:, 40 + d, :]
                if d == 0:
                    dve.wait_ge(S("k_add"), NT)
                dve.scalar_tensor_tensor(XT[:, d, 0:P], Y[:, d, 0:P], g[:, 0:1], XT[:, d, 0:P], ALU.mult, ALU.add).then_inc(S("f_res"), 1)
            link(dve, dve.tensor_tensor(Y[:, :, P:T], Y[:, :, P:T], modT[:, 40:48, 1:9], ALU.mult))
            dve.tensor_tensor(XT[:, :, P:T], XT[:, :, P:T], Y[:, :, P:T], ALU.add).then_inc(S("f_res"), 1)

        def tensor_final(pe):
            pe.wait_ge(S("norm_done"), 2 * NORMED + 1)
            for t in range(NC + 1):
                n = 128 if t < NC else NS
                if t >= 2:
                    pe.wait_ge(S("rows_evac"), (NT + t - 1) * 2)
                for d in range(DT):
                    mm = pe.transpose(ps[0:n, 4 + 2 * (t % 2) + d // 4, (d % 4) * 128:(d % 4) * 128 + 128], HT[:, d, t * 128:t * 128 + n], ident)
                mm.then_inc(S("rows_T"), 1)

        def scalar_final(act):
            for t in range(NC + 1):
                n = 128 if t < NC else NS
                act.wait_ge(S("rows_T"), 2 * NT + t + 1)
                if t >= 2:
                    act.wait_ge(S(f"rows_out{t % 2}"), (3 - t % 2 + t // 2) * 16)
                for a in range(2):
                    act.copy(yout[0:n, t % 2, a * 512:(a + 1) * 512], ps[0:n, 4 + 2 * (t % 2) + a, :]).then_inc(S("rows_evac"), 1)

        def sync_final(sp):
            for t in range(NC + 1):
                sp.wait_ge(S("rows_evac"), (NT + t + 1) * 2)
                if t < NC:
                    sp.dma_start(A["out_y_p"][0, t * 128:(t + 1) * 128, :], yout[:, t % 2, :]).then_inc(S(f"rows_out{t % 2}"), 16)
                else:
                    sp.dma_start(A["out_y_s"][:, 0, :], yout[0:NS, t % 2, :]).then_inc(S(f"rows_out{t % 2}"), 16)
            sp.wait_ge(S("rows_out0"), 96)
            sp.wait_ge(S("rows_out1"), 64)
            sp.wait_ge(S("conv_out"), 16)
            sp.wait_ge(S("d_stored"), H * 64)
            sp.wait_ge(S("r_out0"), RH * 64)
            sp.wait_ge(S("r_out1"), RH * 80)

        block = ctx.enter_context(nc.Block())

        @block.sync
        def _(sp):
            sync_start(sp)
            sync_delta(sp)
            sync_ret(sp)
            sync_merge(sp)
            sync_route(sp)
            sync_list(sp)
            sync_blocks(sp)
            sync_final(sp)

        @block.tensor
        def _(pe):
            tensor_start(pe)
            tensor_norm(pe, 0, [("mod_copied", MOD_TURNS + 1), ("xT_copied", DT + 1)])
            tensor_gates(pe)
            tensor_delta(pe)
            tensor_ret(pe)
            tensor_merge(pe)
            tensor_norm(pe, 1, [("m_res", DT + 1)])
            tensor_route(pe)
            tensor_list(pe)
            tensor_blocks(pe)
            tensor_gather(pe)
            tensor_norm(pe, 2, [("k_add", NT)])
            tensor_final(pe)

        @block.scalar
        def _(act):
            scalar_start(act)
            scalar_norm(act, 0, [("xT_copied", DT + 1)])
            scalar_gates(act)
            scalar_delta(act)
            scalar_ret(act)
            scalar_merge(act)
            scalar_norm(act, 1, [("m_res", DT + 1)])
            scalar_route(act)
            scalar_list(act)
            scalar_blocks(act)
            scalar_norm(act, 2, [("f_res", DT + 1)])
            scalar_final(act)

        @block.vector
        def _(dve):
            vector_start(dve)
            vector_norm(dve, 0, R_NMIX, 0)
            vector_gates(dve)
            vector_delta(dve)
            vector_ret(dve)
            vector_merge(dve)
            vector_norm(dve, 1, R_NFFN, 3)
            vector_route(dve)
            vector_list(dve)
            vector_blocks(dve)
            vector_gather(dve)
            vector_final(dve)
            vector_norm(dve, 2, R_NFIN, None)

        @block.gpsimd
        def _(pool):
            pool_delta(pool)
            pool_ret(pool)
            pool_list(pool)
            pool_blocks(pool)


_INS = ['x_prompt', 'x_sample', 'state_conv', 'state_delta', 'state_ret', 'c_prompt', 'c_sample',
        'w_mod', 'b_mod', 'norm_mix_w', 'w_in', 'conv_w', 'a_log', 'dt_bias', 'dn_norm_w', 'ret_gn_w', 'ret_gn_b',
        'w_down_a', 'w_down_b', 'w_out', 'norm_ffn_w', 'router_w', 'router_bias', 'w_gate', 'w_up', 'w_down',
        'ws_gate', 'ws_up', 'ws_down', 'final_norm_w']
_OUTS = [('y_p', (1, P, D)), ('y_s', (NS, 1, D)), ('conv_p', (1, 1, 3, CW)), ('delta_p', (1, 1, H, DK, DK)),
         ('ret_p', (1, 1, RH, RK, RV)), ('conv_s', (1, NS, 3, CW)), ('delta_s', (1, NS, H, DK, DK)),
         ('ret_s', (1, NS, RH, RK, RV))]


def kernel(**inputs):
    import concourse.bacc as _bacc
    from concourse.bass_utils import run_bass_kernel_spmd as _run

    nc = _bacc.Bacc("TRN2", target_bir_lowering=False, num_devices=1)
    arrays, aps = {}, {}
    given = {name: np.ascontiguousarray(inputs[name]) for name in _INS}
    for name, a in list(given.items()) + list(constants().items()):
        arrays[f"in_{name}_dram"] = a
        aps[name] = nc.dram_tensor(f"in_{name}_dram", a.shape, mybir.dt.from_np(a.dtype), kind="ExternalInput").ap()
    for name, shape in _OUTS:
        aps[f"out_{name}"] = nc.dram_tensor(f"out_{name}_dram", shape, F32, kind="ExternalOutput").ap()
    build(nc, aps)
    r = _run(nc, [arrays], core_ids=[0])
    return tuple(r.results[0][f"out_{name}_dram"] for name, _ in _OUTS)
```
